# Optimizing a Trainium2 kernel written in Bass

```python
import math
import jax, jax.numpy as jnp
from jax import lax
import numpy as np
import jax
import jax.numpy as jnp

D_MODEL = 1024
BATCH = 1
SEQ = 256
DEPTH = 2

N_HEADS = 16
HEAD_DIM = D_MODEL // N_HEADS
D_FF = 4 * D_MODEL
N_MIXERS = 2
N_A_LAYERS = (DEPTH + 1) // 2
N_B_LAYERS = DEPTH // 2
NUM_BUCKETS = 32
MAX_DISTANCE = 128
MOBA_BLOCK = 256
MOBA_TOPK = 3
MOBA_Q_CHUNK = 64
DSA_Q_LORA = 256
DSA_KV_LORA = 256
IDX_HEADS = 8
IDX_DIM = 64
DSA_TOPK_MAX = 256
DSA_Q_CHUNK = 128
DSA_IN_DIM = DSA_Q_LORA + DSA_KV_LORA + IDX_DIM + IDX_HEADS
EPS = 1e-6
NEG = -1e30


def rms_norm(x, g):
    x32 = x.astype(jnp.float32)
    y = x32 * lax.rsqrt(jnp.mean(x32 * x32, axis=-1, keepdims=True) + EPS)
    return y.astype(x.dtype) * g

def rel_bucket(dist):
    n = jnp.maximum(dist, 0)
    exact = NUM_BUCKETS // 2
    nf = jnp.maximum(n, 1).astype(jnp.float32)
    large = exact + (jnp.log(nf / exact) / math.log(MAX_DISTANCE / exact) * (NUM_BUCKETS - exact)).astype(jnp.int32)
    large = jnp.minimum(large, NUM_BUCKETS - 1)
    return jnp.where(n < exact, n, large)

def moba_attention(h, w_qkv, w_o, bias_table):
    B, S, _ = h.shape
    H, Dh, BLK, QC = N_HEADS, HEAD_DIM, MOBA_BLOCK, MOBA_Q_CHUNK
    q, k, v = jnp.split(h @ w_qkv, 3, axis=-1)
    q = q.reshape(B, S, H, Dh).transpose(0, 2, 1, 3)
    k = k.reshape(B, S, H, Dh).transpose(0, 2, 1, 3)
    v = v.reshape(B, S, H, Dh).transpose(0, 2, 1, 3)
    n_blk = -(-S // BLK)
    pad = ((0, 0), (0, 0), (0, n_blk * BLK - S), (0, 0))
    kb = jnp.pad(k, pad).reshape(B, H, n_blk, BLK, Dh)
    vb = jnp.pad(v, pad).reshape(B, H, n_blk, BLK, Dh)
    k_mean = jnp.mean(kb.astype(jnp.float32), axis=3)
    gate = jnp.einsum('bhsd,bhnd->bhsn', q.astype(jnp.float32), k_mean)
    n_past = jnp.arange(S) // BLK
    past = jnp.arange(n_blk)[None, :] < n_past[:, None]
    gate = jnp.where(past[None, None], gate, NEG)
    k_sel = max(1, min(MOBA_TOPK, n_blk - 1))
    _, sel = lax.top_k(gate, k_sel)
    sel = sel.astype(jnp.int32)

    n_ch = S // QC

    def to_chunks(a):
        a = a.reshape(B, H, n_ch, QC, *a.shape[3:])
        a = jnp.moveaxis(a, 2, 1)
        return a.reshape(B * n_ch, H, QC, *a.shape[4:])

    q_c, sel_c = to_chunks(q), to_chunks(sel)
    b_idx = jnp.repeat(jnp.arange(B, dtype=jnp.int32), n_ch)
    c_idx = jnp.tile(jnp.arange(n_ch, dtype=jnp.int32), B)
    head_ids = jnp.arange(H)
    scale = HEAD_DIM ** -0.5

    def step(args):
        qc, selc, b, c = args
        t = c * QC + jnp.arange(QC, dtype=jnp.int32)
        j_own = (c * QC) // BLK
        kbb = lax.dynamic_index_in_dim(kb, b, 0, keepdims=False)
        vbb = lax.dynamic_index_in_dim(vb, b, 0, keepdims=False)
        k_g = kbb[head_ids[:, None, None], selc]
        v_g = vbb[head_ids[:, None, None], selc]
        k_own = lax.dynamic_index_in_dim(kbb, j_own, 1, keepdims=False)
        v_own = lax.dynamic_index_in_dim(vbb, j_own, 1, keepdims=False)
        qf = qc.astype(jnp.float32)
        l_sel = jnp.einsum('hqd,hqnjd->hqnj', qf, k_g.astype(jnp.float32)) * scale
        pos_sel = selc[..., None] * BLK + jnp.arange(BLK, dtype=jnp.int32)
        b_sel = bias_table[rel_bucket(t[None, :, None, None] - pos_sel), head_ids[:, None, None, None]].astype(jnp.float32)
        slot_ok = jnp.arange(k_sel)[None, :] < (t // BLK)[:, None]
        l_sel = jnp.where(slot_ok[None, :, :, None], l_sel + b_sel, NEG).reshape(H, QC, k_sel * BLK)
        l_own = jnp.einsum('hqd,hkd->hqk', qf, k_own.astype(jnp.float32)) * scale
        d_own = t[:, None] - (j_own * BLK + jnp.arange(BLK, dtype=jnp.int32))[None, :]
        b_own = jnp.moveaxis(bias_table[rel_bucket(d_own)].astype(jnp.float32), -1, 0)
        l_own = jnp.where((d_own >= 0)[None], l_own + b_own, NEG)
        p = jax.nn.softmax(jnp.concatenate([l_sel, l_own], axis=-1), axis=-1)
        p_sel = p[..., :k_sel * BLK].reshape(H, QC, k_sel, BLK)
        p_own = p[..., k_sel * BLK:]
        o = (jnp.einsum('hqnj,hqnjd->hqd', p_sel, v_g.astype(jnp.float32))
             + jnp.einsum('hqk,hkd->hqd', p_own, v_own.astype(jnp.float32)))
        return o.astype(qc.dtype)

    o = lax.map(step, (q_c, sel_c, b_idx, c_idx))
    o = o.reshape(B, n_ch, H, QC, Dh).transpose(0, 1, 3, 2, 4).reshape(B, S, H * Dh)
    return o @ w_o

def dsa_attention(h, w_in, g_q, g_kv, w_uq, w_qi, w_uk, w_uv, w_o, bias_table):
    B, S, _ = h.shape
    H, Dh, QC = N_HEADS, HEAD_DIM, DSA_Q_CHUNK
    proj = h @ w_in
    c_q, c_kv, k_idx, w_idx = jnp.split(proj, [DSA_Q_LORA, DSA_Q_LORA + DSA_KV_LORA, DSA_Q_LORA + DSA_KV_LORA + IDX_DIM], axis=-1)
    c_q = rms_norm(c_q, g_q)
    c_kv = rms_norm(c_kv, g_kv)
    q_nope = (c_q @ w_uq).reshape(B, S, H, Dh)
    q_idx = (c_q @ w_qi).reshape(B, S, IDX_HEADS, IDX_DIM)
    w_idx = w_idx.astype(jnp.float32) * (IDX_HEADS ** -0.5 * IDX_DIM ** -0.5)
    top_k = min(DSA_TOPK_MAX, S // 4)
    n_ch = S // QC

    def to_chunks(a):
        return jnp.moveaxis(a.reshape(B, n_ch, QC, *a.shape[2:]), 1, 0)

    k_idx32 = k_idx.astype(jnp.float32)
    key_pos = jnp.arange(S, dtype=jnp.int32)
    b_ids = jnp.arange(B)[:, None, None]
    scale = HEAD_DIM ** -0.5

    def step(args):
        qn, qi, wi, c = args
        t = c * QC + jnp.arange(QC, dtype=jnp.int32)
        rel = jax.nn.relu(jnp.einsum('bqhd,bsd->bqhs', qi.astype(jnp.float32), k_idx32))
        score = jnp.einsum('bqh,bqhs->bqs', wi, rel)
        score = jnp.where((key_pos[None, :] <= t[:, None])[None], score, NEG)
        _, idx = lax.top_k(score, top_k)
        valid = idx <= t[None, :, None]
        c_sel = c_kv[b_ids, idx].astype(jnp.float32)
        q_lat = jnp.einsum('bqhd,hdc->bqhc', qn.astype(jnp.float32), w_uk.astype(jnp.float32))
        logits = jnp.einsum('bqhc,bqkc->bhqk', q_lat, c_sel) * scale
        bias = jnp.moveaxis(bias_table[rel_bucket(t[None, :, None] - idx)].astype(jnp.float32), -1, 1)
        logits = jnp.where(valid[:, None], logits + bias, NEG)
        p = jax.nn.softmax(logits, axis=-1)
        o_lat = jnp.einsum('bhqk,bqkc->bqhc', p, c_sel)
        o = jnp.einsum('bqhc,hcd->bqhd', o_lat, w_uv.astype(jnp.float32))
        return o.astype(qn.dtype)

    o = lax.map(step, (to_chunks(q_nope), to_chunks(q_idx), to_chunks(w_idx), jnp.arange(n_ch, dtype=jnp.int32)))
    o = jnp.moveaxis(o, 0, 1).reshape(B, S, H * Dh)
    return o @ w_o

def sq_relu_mlp(h, w_up, w_down):
    return jnp.square(jax.nn.relu(h @ w_up)) @ w_down

def first_inputs(seed: int = 0) -> dict:
    key = jax.random.key(seed)
    ks = jax.random.split(key, 20)
    D, H, Dh = D_MODEL, N_HEADS, HEAD_DIM
    nrm = lambda k, shape, s: jax.random.normal(k, shape, jnp.float32) * s
    gain = lambda k, shape: 1.0 + 0.05 * jax.random.normal(k, shape, jnp.float32)
    return {
        "x": nrm(ks[0], (BATCH, SEQ, D), 1.0),
        "rel_bias": nrm(ks[1], (NUM_BUCKETS, H), 0.2),
        "ln_attn": gain(ks[2], (DEPTH, D)),
        "ln_mlp": gain(ks[3], (DEPTH, D)),
        "moba_w_qkv": nrm(ks[4], (N_A_LAYERS, D, 3 * D), D ** -0.5),
        "moba_w_o": nrm(ks[5], (N_A_LAYERS, D, D), D ** -0.5),
        "dsa_w_in": nrm(ks[6], (N_B_LAYERS, D, DSA_IN_DIM), D ** -0.5),
        "dsa_g_q": gain(ks[7], (N_B_LAYERS, DSA_Q_LORA)),
        "dsa_g_kv": gain(ks[8], (N_B_LAYERS, DSA_KV_LORA)),
        "dsa_w_uq": nrm(ks[9], (N_B_LAYERS, DSA_Q_LORA, H * Dh), DSA_Q_LORA ** -0.5),
        "dsa_w_qi": nrm(ks[10], (N_B_LAYERS, DSA_Q_LORA, IDX_HEADS * IDX_DIM), DSA_Q_LORA ** -0.5),
        "dsa_w_uk": nrm(ks[11], (N_B_LAYERS, H, Dh, DSA_KV_LORA), DSA_KV_LORA ** -0.5),
        "dsa_w_uv": nrm(ks[12], (N_B_LAYERS, H, DSA_KV_LORA, Dh), DSA_KV_LORA ** -0.5),
        "dsa_w_o": nrm(ks[13], (N_B_LAYERS, H * Dh, D), (H * Dh) ** -0.5),
        "mlp_w_up": nrm(ks[14], (DEPTH, D, D_FF), D ** -0.5),
        "mlp_w_down": nrm(ks[15], (DEPTH, D_FF, D), 0.5 * D_FF ** -0.5),
        "final_norm": gain(ks[16], (D,)),
    }

def first_block(x, rel_bias, ln_attn, ln_mlp, moba_w_qkv, moba_w_o, dsa_w_in, dsa_g_q, dsa_g_kv,
              dsa_w_uq, dsa_w_qi, dsa_w_uk, dsa_w_uv, dsa_w_o, mlp_w_up, mlp_w_down, final_norm):
    for i in range(DEPTH):
        hn = rms_norm(x, ln_attn[i])
        j = i // N_MIXERS
        if i % N_MIXERS == 0:
            x = x + moba_attention(hn, moba_w_qkv[j], moba_w_o[j], rel_bias)
        else:
            x = x + dsa_attention(hn, dsa_w_in[j], dsa_g_q[j], dsa_g_kv[j], dsa_w_uq[j], dsa_w_qi[j],
                                  dsa_w_uk[j], dsa_w_uv[j], dsa_w_o[j], rel_bias)
        x = x + sq_relu_mlp(rms_norm(x, ln_mlp[i]), mlp_w_up[i], mlp_w_down[i])
    return rms_norm(x, final_norm)


CHUNK = 64
Q_BLOCK = 128
NORM_EPS = 1e-6
NEG_INF = -1e30

N_EVEN = (DEPTH + 1) // 2
N_ODD = DEPTH // 2

RWKV_HEAD_DIM = 64
RWKV_WIDTH = D_MODEL // 2
RWKV_HEADS = RWKV_WIDTH // RWKV_HEAD_DIM
DECAY_LORA = 64
ICLR_LORA = 64
GATE_LORA = 160
RWKV_GN_EPS = 1e-5 * RWKV_HEAD_DIM
RWKV_SPLITS = (RWKV_WIDTH, 2 * RWKV_WIDTH, 3 * RWKV_WIDTH,
               3 * RWKV_WIDTH + DECAY_LORA, 3 * RWKV_WIDTH + DECAY_LORA + ICLR_LORA)
RWKV_COLS = 3 * RWKV_WIDTH + DECAY_LORA + ICLR_LORA + GATE_LORA

S5_WIDTH = D_MODEL - RWKV_WIDTH
S5_GROUP = 16
S5_GROUPS = S5_WIDTH // S5_GROUP
S5_STATE = 64
S5_DT_MIN = 1e-3
S5_DT_MAX = 1e-1

IN_COLS = RWKV_COLS + S5_WIDTH
MIX_WIDTH = RWKV_WIDTH + S5_WIDTH

DIFF_HEAD_DIM = 64
DIFF_V_DIM = 2 * DIFF_HEAD_DIM
DIFF_HEADS = D_MODEL // DIFF_V_DIM
DIFF_WIDTH = DIFF_HEADS * DIFF_V_DIM

MEM_LEN = 256
MEM_HEADS = 4
MEM_HEAD_DIM = D_MODEL // MEM_HEADS

D_FF_2 = 2816
N_EXPERTS = 8
TOP_K = 2
D_FF_EXPERT = 3584


F32 = jnp.float32

def rms_norm_2(x, gain):
    xf = x.astype(F32)
    y = xf * lax.rsqrt(jnp.mean(xf * xf, axis=-1, keepdims=True) + NORM_EPS)
    return (y * gain.astype(F32)).astype(x.dtype)

def token_shift(z):
    return jnp.pad(z, ((0, 0), (1, 0), (0, 0)))[:, :-1]

def alibi_slopes(n_heads):
    return 2.0 ** (-8.0 * jnp.arange(1, n_heads + 1, dtype=F32) / n_heads)

def rwkv7_recurrence(r, decay, k, v, kk, a):
    b, _, h, n = r.shape

    def step(state, inp):
        r_t, w_t, k_t, v_t, kk_t, a_t = inp
        s_kk = jnp.einsum('bhvk,bhk->bhv', state, kk_t)
        state = (state * w_t[:, :, None, :]
                 - s_kk[..., None] * (kk_t * a_t)[:, :, None, :]
                 + v_t[..., None] * k_t[:, :, None, :])
        return state, jnp.einsum('bhvk,bhk->bhv', state, r_t)

    xs = tuple(jnp.moveaxis(t, 1, 0) for t in (r, decay, k, v, kk, a))
    _, out = lax.scan(step, jnp.zeros((b, h, n, n), F32), xs)
    return jnp.moveaxis(out, 0, 1)

def rwkv7_time_mix(zr, mu, w0, w_up, a0, a_up, g_up, k_k, k_a, r_k, ln_w, ln_b):
    b, t, _ = zr.shape
    zr = zr.astype(F32)
    zr = zr + (token_shift(zr) - zr) * mu.astype(F32)
    r, k, v, wd, ad, gd = jnp.split(zr, RWKV_SPLITS, axis=-1)
    heads = lambda u: u.reshape(b, t, RWKV_HEADS, RWKV_HEAD_DIM)
    w_log = -jax.nn.softplus(-(w0.astype(F32) + jnp.tanh(wd) @ w_up.astype(F32))) - 0.5
    decay = jnp.exp(-jnp.exp(w_log))
    a = jax.nn.sigmoid(a0.astype(F32) + ad @ a_up.astype(F32))
    g = jax.nn.sigmoid(gd) @ g_up.astype(F32)
    kk = heads(k * k_k.astype(F32))
    kk = kk * lax.rsqrt(jnp.maximum(jnp.sum(kk * kk, axis=-1, keepdims=True), 1e-24))
    k = k * (1.0 + (a - 1.0) * k_a.astype(F32))
    r_h, k_h, v_h = heads(r), heads(k), heads(v)
    o = rwkv7_recurrence(r_h, heads(decay), k_h, v_h, kk, heads(a))
    mean = jnp.mean(o, axis=-1, keepdims=True)
    var = jnp.mean(jnp.square(o - mean), axis=-1, keepdims=True)
    o = ((o - mean) * lax.rsqrt(var + RWKV_GN_EPS)).reshape(b, t, RWKV_WIDTH)
    o = o * ln_w.astype(F32) + ln_b.astype(F32)
    bonus = jnp.sum(r_h * k_h * r_k.astype(F32), axis=-1, keepdims=True) * v_h
    return (o + bonus.reshape(b, t, RWKV_WIDTH)) * g

def s5_ssm(u, lam_re, lam_im, log_dt, b_re, b_im, c_re, c_im, d_skip, w_glu, b_glu):
    b, t, _ = u.shape
    ug = u.astype(F32).reshape(b, t, S5_GROUPS, S5_GROUP)
    lam = lax.complex(lam_re.astype(F32), lam_im.astype(F32))
    dt = jnp.exp(log_dt.astype(F32))[:, None]
    lam_bar = jnp.exp(lam * dt)
    b_bar = ((lam_bar - 1.0) / lam)[..., None] * lax.complex(b_re.astype(F32), b_im.astype(F32))
    bu = jnp.einsum('gpi,btgi->btgp', b_bar, ug.astype(jnp.complex64))

    def combine(left, right):
        a_l, x_l = left
        a_r, x_r = right
        return a_r * a_l, a_r * x_l + x_r

    _, states = lax.associative_scan(combine, (jnp.broadcast_to(lam_bar, bu.shape), bu), axis=1)
    c_mat = lax.complex(c_re.astype(F32), c_im.astype(F32))
    y = jnp.real(jnp.einsum('gip,btgp->btgi', c_mat, states))
    y = y + d_skip.astype(F32).reshape(S5_GROUPS, S5_GROUP) * ug
    y = jax.nn.gelu(y.reshape(b, t, S5_WIDTH))
    return y * jax.nn.sigmoid(y @ w_glu.astype(F32) + b_glu.astype(F32))

def diff_attention(h, w_qkv, q_gain, k_gain, lam_q1, lam_k1, lam_q2, lam_k2, sub_gain, w_o, lambda_init):
    b, t, _ = h.shape
    q, k, v = jnp.split(h @ w_qkv, 3, axis=-1)
    q = rms_norm_2(q.reshape(b, t, DIFF_HEADS, 2, DIFF_HEAD_DIM), q_gain).astype(F32)
    k = rms_norm_2(k.reshape(b, t, DIFF_HEADS, 2, DIFF_HEAD_DIM), k_gain).astype(F32)
    v = v.reshape(b, t, DIFF_HEADS, DIFF_V_DIM).astype(F32)
    lam = (jnp.exp(jnp.sum(lam_q1.astype(F32) * lam_k1.astype(F32)))
           - jnp.exp(jnp.sum(lam_q2.astype(F32) * lam_k2.astype(F32))) + lambda_init)
    slopes = alibi_slopes(DIFF_HEADS)
    key_pos = jnp.arange(t)
    n_blocks = t // Q_BLOCK
    q_blocks = jnp.moveaxis(q.reshape(b, n_blocks, Q_BLOCK, DIFF_HEADS, 2, DIFF_HEAD_DIM), 1, 0)
    starts = jnp.arange(n_blocks) * Q_BLOCK
    scale = DIFF_HEAD_DIM ** -0.5

    def attend_block(args):
        qb, start = args
        q_pos = start + jnp.arange(Q_BLOCK)
        s = jnp.einsum('bqhcd,bshcd->bhcqs', qb, k) * scale
        dist = jnp.abs(q_pos[:, None] - key_pos[None, :]).astype(F32)
        bias = -slopes[:, None, None, None] * dist
        visible = (key_pos[None, :] // CHUNK) <= (q_pos[:, None] // CHUNK)
        p = jax.nn.softmax(jnp.where(visible, s + bias, NEG_INF), axis=-1)
        attn = p[:, :, 0] - lam * p[:, :, 1]
        return jnp.einsum('bhqs,bshe->bqhe', attn, v)

    o = lax.map(attend_block, (q_blocks, starts))
    o = jnp.moveaxis(o, 0, 1).reshape(b, t, DIFF_HEADS, DIFF_V_DIM)
    o = rms_norm_2(o, sub_gain) * (1.0 - lambda_init)
    return o.reshape(b, t, DIFF_WIDTH).astype(h.dtype) @ w_o

def memory_cross_attention(h, mem_n, w_q, w_kv, q_gain, k_gain, w_o):
    b, t, _ = h.shape
    m = mem_n.shape[1]
    q = rms_norm_2((h @ w_q).reshape(b, t, MEM_HEADS, MEM_HEAD_DIM), q_gain).astype(F32)
    k, v = jnp.split(mem_n @ w_kv, 2, axis=-1)
    k = rms_norm_2(k.reshape(b, m, MEM_HEADS, MEM_HEAD_DIM), k_gain).astype(F32)
    v = v.reshape(b, m, MEM_HEADS, MEM_HEAD_DIM).astype(F32)
    p = jax.nn.softmax(jnp.einsum('bthd,bmhd->bhtm', q, k) * MEM_HEAD_DIM ** -0.5, axis=-1)
    o = jnp.einsum('bhtm,bmhd->bthd', p, v).reshape(b, t, D_MODEL)
    return o.astype(h.dtype) @ w_o

def swiglu(h, w_gate, w_up, w_down):
    return (jax.nn.silu(h @ w_gate) * (h @ w_up)) @ w_down

def moe_swiglu(h, w_router, b_router, w_gate, w_up, w_down):
    logits = (h @ w_router).astype(F32) + b_router.astype(F32)
    top_logits, top_idx = lax.top_k(logits, TOP_K)
    top_w = jax.nn.softmax(top_logits, axis=-1)
    gates = jnp.sum(jax.nn.one_hot(top_idx, N_EXPERTS, dtype=F32) * top_w[..., None], axis=-2)
    out = jnp.zeros(h.shape, F32)
    for e in range(N_EXPERTS):
        y_e = swiglu(h, w_gate[e], w_up[e], w_down[e]).astype(F32)
        out = out + gates[..., e:e + 1] * y_e
    return out.astype(h.dtype)

def second_inputs(seed: int = 0) -> dict:
    key = jax.random.key(seed)
    keys = iter(jax.random.split(key, 80))

    def nrm(shape, scale):
        return jax.random.normal(next(keys), shape, F32) * scale

    def gain(shape):
        return 1.0 + nrm(shape, 0.02)

    D, L, NE, NO = D_MODEL, DEPTH, N_EVEN, N_ODD
    G, P, I = S5_GROUPS, S5_STATE, S5_GROUP
    decay_ramp = -6.5 + 5.0 * jnp.linspace(0.0, 1.0, RWKV_WIDTH, dtype=F32) ** 0.85
    return {
        'x': nrm((BATCH, SEQ, D), 1.0),
        'mem': nrm((BATCH, MEM_LEN, D), 1.0),
        'norm_mix': gain((L, D)),
        'norm_xattn': gain((L, D)),
        'norm_mem': gain((L, D)),
        'norm_ffn': gain((L, D)),
        'xa_w_q': nrm((L, D, D), D ** -0.5),
        'xa_w_kv': nrm((L, D, 2 * D), D ** -0.5),
        'xa_q_gain': gain((L, MEM_HEAD_DIM)),
        'xa_k_gain': gain((L, MEM_HEAD_DIM)),
        'xa_w_o': nrm((L, D, D), D ** -0.5),
        'hy_w_in': nrm((NE, D, IN_COLS), D ** -0.5),
        'rw_mu': jax.random.uniform(next(keys), (NE, RWKV_COLS), F32),
        'rw_w0': decay_ramp + nrm((NE, RWKV_WIDTH), 0.01),
        'rw_w_up': nrm((NE, DECAY_LORA, RWKV_WIDTH), 0.1),
        'rw_a0': nrm((NE, RWKV_WIDTH), 0.1),
        'rw_a_up': nrm((NE, ICLR_LORA, RWKV_WIDTH), ICLR_LORA ** -0.5),
        'rw_g_up': nrm((NE, GATE_LORA, RWKV_WIDTH), GATE_LORA ** -0.5),
        'rw_k_k': 0.85 + nrm((NE, RWKV_WIDTH), 0.02),
        'rw_k_a': gain((NE, RWKV_WIDTH)),
        'rw_r_k': nrm((NE, RWKV_HEADS, RWKV_HEAD_DIM), 0.1),
        'rw_ln_w': gain((NE, RWKV_WIDTH)),
        'rw_ln_b': nrm((NE, RWKV_WIDTH), 0.02),
        's5_lam_re': -0.5 + nrm((NE, G, P), 0.01),
        's5_lam_im': jnp.pi * jnp.arange(P, dtype=F32) + nrm((NE, G, P), 0.01),
        's5_log_dt': jax.random.uniform(next(keys), (NE, G), F32, math.log(S5_DT_MIN), math.log(S5_DT_MAX)),
        's5_b_re': nrm((NE, G, P, I), (2 * I) ** -0.5),
        's5_b_im': nrm((NE, G, P, I), (2 * I) ** -0.5),
        's5_c_re': nrm((NE, G, I, P), P ** -0.5),
        's5_c_im': nrm((NE, G, I, P), P ** -0.5),
        's5_d': nrm((NE, S5_WIDTH), 1.0),
        's5_w_glu': nrm((NE, S5_WIDTH, S5_WIDTH), S5_WIDTH ** -0.5),
        's5_b_glu': nrm((NE, S5_WIDTH), 0.02),
        'hy_w_out': nrm((NE, MIX_WIDTH, D), MIX_WIDTH ** -0.5),
        'ff_w_gate': nrm((NE, D, D_FF_2), D ** -0.5),
        'ff_w_up': nrm((NE, D, D_FF_2), D ** -0.5),
        'ff_w_down': nrm((NE, D_FF_2, D), D_FF_2 ** -0.5),
        'da_w_qkv': nrm((NO, D, 3 * DIFF_WIDTH), D ** -0.5),
        'da_q_gain': gain((NO, DIFF_HEAD_DIM)),
        'da_k_gain': gain((NO, DIFF_HEAD_DIM)),
        'da_lam_q1': nrm((NO, DIFF_HEAD_DIM), 0.1),
        'da_lam_k1': nrm((NO, DIFF_HEAD_DIM), 0.1),
        'da_lam_q2': nrm((NO, DIFF_HEAD_DIM), 0.1),
        'da_lam_k2': nrm((NO, DIFF_HEAD_DIM), 0.1),
        'da_sub_gain': gain((NO, DIFF_V_DIM)),
        'da_w_o': nrm((NO, DIFF_WIDTH, D), DIFF_WIDTH ** -0.5),
        'moe_w_router': nrm((NO, D, N_EXPERTS), D ** -0.5),
        'moe_b_router': nrm((NO, N_EXPERTS), 0.01),
        'moe_w_gate': nrm((NO, N_EXPERTS, D, D_FF_EXPERT), D ** -0.5),
        'moe_w_up': nrm((NO, N_EXPERTS, D, D_FF_EXPERT), D ** -0.5),
        'moe_w_down': nrm((NO, N_EXPERTS, D_FF_EXPERT, D), D_FF_EXPERT ** -0.5),
    }

def second_block(x, mem, norm_mix, norm_xattn, norm_mem, norm_ffn,
              xa_w_q, xa_w_kv, xa_q_gain, xa_k_gain, xa_w_o,
              hy_w_in, rw_mu, rw_w0, rw_w_up, rw_a0, rw_a_up, rw_g_up, rw_k_k, rw_k_a, rw_r_k,
              rw_ln_w, rw_ln_b,
              s5_lam_re, s5_lam_im, s5_log_dt, s5_b_re, s5_b_im, s5_c_re, s5_c_im, s5_d,
              s5_w_glu, s5_b_glu, hy_w_out,
              ff_w_gate, ff_w_up, ff_w_down,
              da_w_qkv, da_q_gain, da_k_gain, da_lam_q1, da_lam_k1, da_lam_q2, da_lam_k2,
              da_sub_gain, da_w_o,
              moe_w_router, moe_b_router, moe_w_gate, moe_w_up, moe_w_down):
    h = x
    for l in range(DEPTH):
        i = l // 2
        hn = rms_norm_2(h, norm_mix[l])
        if l % 2 == 0:
            z = hn @ hy_w_in[i]
            y_a = rwkv7_time_mix(z[..., :RWKV_COLS], rw_mu[i], rw_w0[i], rw_w_up[i], rw_a0[i],
                                 rw_a_up[i], rw_g_up[i], rw_k_k[i], rw_k_a[i], rw_r_k[i],
                                 rw_ln_w[i], rw_ln_b[i])
            y_b = s5_ssm(z[..., RWKV_COLS:], s5_lam_re[i], s5_lam_im[i], s5_log_dt[i], s5_b_re[i],
                         s5_b_im[i], s5_c_re[i], s5_c_im[i], s5_d[i], s5_w_glu[i], s5_b_glu[i])
            y_mix = jnp.concatenate([y_a, y_b], axis=-1).astype(h.dtype) @ hy_w_out[i]
        else:
            lambda_init = 0.8 - 0.6 * math.exp(-0.3 * l)
            y_mix = diff_attention(hn, da_w_qkv[i], da_q_gain[i], da_k_gain[i], da_lam_q1[i],
                                   da_lam_k1[i], da_lam_q2[i], da_lam_k2[i], da_sub_gain[i],
                                   da_w_o[i], lambda_init)
        h = h + y_mix.astype(h.dtype)
        y_mem = memory_cross_attention(rms_norm_2(h, norm_xattn[l]), rms_norm_2(mem, norm_mem[l]),
                                       xa_w_q[l], xa_w_kv[l], xa_q_gain[l], xa_k_gain[l], xa_w_o[l])
        h = h + y_mem.astype(h.dtype)
        hn = rms_norm_2(h, norm_ffn[l])
        if l % 2 == 0:
            y_ff = swiglu(hn, ff_w_gate[i], ff_w_up[i], ff_w_down[i])
        else:
            y_ff = moe_swiglu(hn, moe_w_router[i], moe_b_router[i], moe_w_gate[i],
                              moe_w_up[i], moe_w_down[i])
        h = h + y_ff.astype(h.dtype)
    return h


def setup_inputs(seed=0):
    out = dict(first_inputs(seed))
    for name, value in second_inputs(seed + 1).items():
        if name != "x":
            out[name + "_2"] = value
    return out


def reference(
    x, rel_bias, ln_attn, ln_mlp, moba_w_qkv, moba_w_o, dsa_w_in, dsa_g_q, dsa_g_kv, dsa_w_uq,
    dsa_w_qi, dsa_w_uk, dsa_w_uv, dsa_w_o, mlp_w_up, mlp_w_down, final_norm, mem_2, norm_mix_2,
    norm_xattn_2, norm_mem_2, norm_ffn_2, xa_w_q_2, xa_w_kv_2, xa_q_gain_2, xa_k_gain_2,
    xa_w_o_2, hy_w_in_2, rw_mu_2, rw_w0_2, rw_w_up_2, rw_a0_2, rw_a_up_2, rw_g_up_2, rw_k_k_2,
    rw_k_a_2, rw_r_k_2, rw_ln_w_2, rw_ln_b_2, s5_lam_re_2, s5_lam_im_2, s5_log_dt_2, s5_b_re_2,
    s5_b_im_2, s5_c_re_2, s5_c_im_2, s5_d_2, s5_w_glu_2, s5_b_glu_2, hy_w_out_2, ff_w_gate_2,
    ff_w_up_2, ff_w_down_2, da_w_qkv_2, da_q_gain_2, da_k_gain_2, da_lam_q1_2, da_lam_k1_2,
    da_lam_q2_2, da_lam_k2_2, da_sub_gain_2, da_w_o_2, moe_w_router_2, moe_b_router_2,
    moe_w_gate_2, moe_w_up_2, moe_w_down_2,
):
    x = first_block(
        x, rel_bias, ln_attn, ln_mlp, moba_w_qkv, moba_w_o, dsa_w_in, dsa_g_q, dsa_g_kv,
        dsa_w_uq, dsa_w_qi, dsa_w_uk, dsa_w_uv, dsa_w_o, mlp_w_up, mlp_w_down, final_norm,
    )
    return second_block(
        x, mem_2, norm_mix_2, norm_xattn_2, norm_mem_2, norm_ffn_2, xa_w_q_2, xa_w_kv_2,
        xa_q_gain_2, xa_k_gain_2, xa_w_o_2, hy_w_in_2, rw_mu_2, rw_w0_2, rw_w_up_2, rw_a0_2,
        rw_a_up_2, rw_g_up_2, rw_k_k_2, rw_k_a_2, rw_r_k_2, rw_ln_w_2, rw_ln_b_2, s5_lam_re_2,
        s5_lam_im_2, s5_log_dt_2, s5_b_re_2, s5_b_im_2, s5_c_re_2, s5_c_im_2, s5_d_2,
        s5_w_glu_2, s5_b_glu_2, hy_w_out_2, ff_w_gate_2, ff_w_up_2, ff_w_down_2, da_w_qkv_2,
        da_q_gain_2, da_k_gain_2, da_lam_q1_2, da_lam_k1_2, da_lam_q2_2, da_lam_k2_2,
        da_sub_gain_2, da_w_o_2, moe_w_router_2, moe_b_router_2, moe_w_gate_2, moe_w_up_2,
        moe_w_down_2,
    )


_drawn_inputs = setup_inputs


def setup_inputs(seed=0):
    import zlib

    import numpy as np

    out = dict(_drawn_inputs(seed))
    spreads = {}
    factors = {'norm_xattn_2': 8.0,
     'norm_mem_2': 7.368,
     'xa_q_gain_2': 8.0,
     'xa_k_gain_2': 8.0,
     'rw_k_k_2': 2.722,
     'rw_ln_w_2': 5.502,
     'rw_ln_b_2': 3.686,
     's5_lam_re_2': 200.0,
     's5_b_glu_2': 8.0,
     'da_q_gain_2': 4.968,
     'da_k_gain_2': 5.774,
     'da_lam_q1_2': 8.0,
     'da_lam_q2_2': 2.897,
     'da_lam_k2_2': 3.914,
     'da_sub_gain_2': 3.243,
     'moe_b_router_2': 86.545}
    for name, (base, spread) in spreads.items():
        noise = np.random.default_rng([zlib.crc32(name.encode()), seed]).standard_normal(out[name].shape)
        drawn = base * np.exp(spread * noise) if base else spread * noise
        out[name] = jnp.asarray(drawn.astype(out[name].dtype))
    for name, factor in factors.items():
        out[name] = (out[name] * factor).astype(out[name].dtype)
    return out
```

```python
import math

import numpy as np

import concourse.bass as bass
from concourse import mybir

F32 = mybir.dt.float32
U32 = mybir.dt.uint32
ALU = mybir.AluOpType
ACT = mybir.ActivationFunctionType
AXX = mybir.AxisListType.X

P = 128
T = 256
TT = T // P
D = 1024
KD = D // P
H = 16
DH = 64
DFF = 4096
EPS = 1e-6
NEG = -1e30
TAKEN = -3e38
NBUCKET = 32
MAXDIST = 128
TOPK = 64
IDXH = 8
LORA = 256
CH = 64
NCH = T // CH
RW = 512
RWKV_COLS = 3 * RW + 64 + 64 + 160
SG = 16
SP_ = 64
ST = RW // SG * SP_ // P
FF2 = 2816
NE = 8
FE = 3584
GN_EPS = 1e-5 * 64
LAMBDA_INIT = 0.8 - 0.6 * math.exp(-0.3)

RING = 7
KW = 4
NW = 512
CAUS = P + T


def _bucket(d):
    n = np.maximum(d, 0)
    exact = NBUCKET // 2
    nf = np.maximum(n, 1).astype(np.float32)
    large = exact + (np.log(nf / np.float32(exact)) / np.float32(math.log(MAXDIST / exact))
                     * np.float32(NBUCKET - exact)).astype(np.int32)
    return np.where(n < exact, n, np.minimum(large, NBUCKET - 1))


def constants():
    parts = {}
    eye = np.eye(P)
    i = np.arange(P)
    parts["ident"] = eye
    half = i // 64
    parts["mean64"] = (half[:, None] == half[None, :]) / 64.0
    parts["sum64"] = (half[:, None] == half[None, :]) * 1.0
    parts["mean128"] = np.full((P, P), 1 / 128)
    parts["mean256"] = np.full((P, P), 1 / 256)
    same = (i[:, None] // CH) == (i[None, :] // CH)
    parts["strict"] = (same & (i[:, None] < i[None, :])) * 1.0
    parts["upto"] = (same & (i[:, None] <= i[None, :])) * 1.0
    for s in (1, 2, 4, 8, 16, 32):
        parts[f"level{s}"] = ((i[:, None] // (2 * s) == i[None, :] // (2 * s))
                              & (i[:, None] % (2 * s) < s) & (i[None, :] % (2 * s) >= s)) * 1.0
    t = np.arange(4 * T)
    parts["carry"] = np.broadcast_to((t % CH != 0) * 1.0, (P, 4 * T))
    dist = np.concatenate([i[:, None] - np.arange(P)[None, :], P + i[:, None] - np.arange(T)[None, :]], 1)
    parts["seen"] = (dist >= 0) * 1.0
    parts["unseen"] = np.where(dist >= 0, 0.0, NEG)
    q = np.concatenate([np.repeat(i[:, None], P, 1), np.repeat(P + i[:, None], T, 1)], 1)
    k = q - dist
    parts["alibi"] = np.where(k // 64 <= q // 64, -np.abs(dist), -1e33)
    j = np.arange(CAUS)
    d = T - 1 - j
    onehot = np.zeros((P, CAUS))
    onehot[_bucket(d), j] = 1.0
    parts["onehot"] = onehot
    parts["future"] = np.broadcast_to(np.where(d >= 0, 0.0, NEG), (P, CAUS))
    parts["iota8"] = np.broadcast_to(np.arange(8.0), (P, 8))
    parts["parity"] = np.stack([(i // SG) % 2 == 0, (i // SG) % 2 == 1], 1) * 1.0
    eps = [EPS, 64 * EPS, 256 * EPS, EPS / (1 - LAMBDA_INIT) ** 2, GN_EPS, math.pi / 2, 0.0, 1.0]
    parts["eps"] = np.broadcast_to(np.array(eps), (P, 8))
    at, n = {}, 0
    for name, a in parts.items():
        at[name] = (n, a.shape[1])
        n += a.shape[1]
    return np.ascontiguousarray(np.concatenate(list(parts.values()), 1).astype(np.float32)), at


E_EPS, E_EPS64, E_EPS256, E_SUB, E_GN, E_HALFPI = range(6)


class Signal:

    def __init__(self, nc, name):
        self.sem = nc.alloc_semaphore(name)
        self.base = self.total = 0

    def up(self, by=1):
        self.total += by
        return self.sem, by

    def at(self, n):
        return self.sem, self.base + n

    def close(self):
        self.base = self.total


class Core:

    def __init__(self, nc, const_at):
        self.nc = nc
        self.const_at = const_at
        self.signals = {}
        sb = lambda name, shape: nc.alloc_sbuf_tensor(name, shape, F32)
        self.ring = sb("ring", [P, RING, KW * NW])
        self.x = sb("residual", [P, TT, D])
        self.xnT = sb("xnT", [P, KD, T])
        self.const = sb("const", [P, sum(n for _, n in const_at.values())])
        self.rows = sb("rows", [P, 2, P])
        self.cols = sb("cols", [P, 2, P])
        self.stat = sb("stat", [P, 64])
        self.ARENA = 24576
        self.arena = sb("arena", [P, self.ARENA])
        self.ps = nc.alloc_psum_tensor("ps", [P, 8, 512], F32)
        self.landed = [self.sig(f"weights_landed{i}") for i in range(RING)]
        self.filled = self.sig("products")
        self.bank_full = []
        self.slot_used = []
        self.tiles = []
        self.issued = self.taken = 0
        self.chains = {e: self.sig(f"{e}_step") for e in ("pe", "act", "dve", "pool")}

    def sig(self, name):
        if name not in self.signals:
            self.signals[name] = Signal(self.nc, name)
        return self.signals[name]

    def c(self, name):
        at, n = self.const_at[name]
        return self.const[:, at:at + n]

    def a(self, off, n):
        assert off + n <= self.ARENA, (off, n)
        return self.arena[:, off:off + n]

    def close(self):
        for s in self.signals.values():
            s.close()
        self.bank_full = []

    def fill(self, matmul, bank=False, slots=0):
        matmul.then_inc(*self.filled.up())
        if bank:
            self.bank_full.append(self.filled.total)
        self.slot_used += [self.filled.total] * slots

    def wait_bank(self, eng, unit):
        eng.wait_ge(self.filled.sem, self.bank_full[unit])

    def link(self, eng, who, ins):
        s = self.chains[who]
        ins.then_inc(*s.up())
        eng.wait_ge(s.sem, s.total)

    def slot(self, i, kt, n):
        return self.ring[:, i % RING, 0:kt * n].rearrange("p (k n) -> p k n", n=n)

    def wait_tile(self, pe, i):
        pe.wait_ge(self.landed[i % RING].sem, 16 * (i // RING + 1))

    def issue(self, sp, upto):
        while self.issued < min(upto, len(self.tiles)):
            i = self.issued
            src = self.tiles[i]
            kt, n = src.shape[1], src.shape[2]
            if i >= RING:
                sp.wait_ge(self.filled.sem, self.slot_used[i - RING])
            sp.dma_start(self.slot(i, kt, n), src).then_inc(*self.landed[i % RING].up(16))
            self.issued += 1


def k_tiles(w):
    return w.rearrange("(k p) n -> p k n", p=P)


def col_chunks(w, c0=0, c1=None):
    v = k_tiles(w)
    c1 = w.shape[1] if c1 is None else c1
    out = []
    for n0 in range(c0, c1, NW):
        for k0 in range(0, v.shape[1], KW):
            out.append(v[:, k0:min(k0 + KW, v.shape[1]), n0:min(n0 + NW, c1)])
    return out


def row_chunks(w):
    v = k_tiles(w)
    return [v[:, k0:min(k0 + KW, v.shape[1]), n0:n0 + NW]
            for k0 in range(0, v.shape[1], KW) for n0 in range(0, w.shape[1], NW)]


def stage(core, sp=None, pe=None, act=None, dve=None, pool=None, uses=0):
    nc = core.nc
    upto = core.taken + uses + RING
    with nc.Block(no_gpsimd_drain=True) as block:
        if pe:
            block.tensor(pe)
        if act:
            block.scalar(act)
        if dve:
            block.vector(dve)
        if pool:
            block.gpsimd(pool)

        @block.sync
        def _(e):
            if sp:
                sp(e)
            core.issue(e, upto)
    core.taken += uses
    core.close()


def features_matmul(core, pe, unit, srcT, kt, widths, free, bank0, nbanks, tile, cols=None):
    per = -(-kt // KW)
    for n in widths:
        for j in range(per):
            core.wait_tile(pe, tile + j)
        for n0 in range(0, n, 2 * P):
            if unit >= nbanks:
                pe.wait_ge(*free.at(unit - nbanks + 1))
            for h, m0 in enumerate(range(n0, min(n0 + 2 * P, n), P)):
                m = min(P, n - m0)
                for k in range(kt):
                    ktile = min(KW, kt - (k // KW) * KW)
                    last = core.nc.tensor.matmul(
                        core.ps[0:m, bank0 + unit % nbanks, h * T:(h + 1) * T],
                        core.slot(tile + k // KW, ktile, n)[:, k % KW, m0:m0 + m], srcT[:, k, :],
                        start=(k == 0), stop=(k == kt - 1))
            core.fill(last, bank=True, slots=per if n0 + 2 * P >= n else 0)
            unit += 1
        tile += per
    return unit, tile


def tokens_matmul(core, pe, unit, srcT, kt, widths, free, bank0, nbanks, tile):
    per = -(-kt // KW)
    for n in widths:
        for tt in range(TT):
            if unit + tt >= nbanks:
                pe.wait_ge(*free.at(unit + tt - nbanks + 1))
        for j in range(per):
            core.wait_tile(pe, tile)
            ktile = min(KW, kt - j * KW)
            for tt in range(TT):
                for k in range(ktile):
                    last = core.nc.tensor.matmul(
                        core.ps[:, bank0 + (unit + tt) % nbanks, 0:n],
                        srcT[:, j * KW + k, tt * P:(tt + 1) * P], core.slot(tile, ktile, n)[:, k, :],
                        start=(j + k == 0), stop=(j * KW + k == kt - 1))
                if j == per - 1 or tt == TT - 1:
                    core.fill(last, bank=(j == per - 1), slots=int(tt == TT - 1))
            tile += 1
        unit += TT
    return unit, tile


def down_matmul(core, pe, srcT, kt, bank0, tile):
    for k0 in range(0, kt, KW):
        ktile = min(KW, kt - k0)
        for half in range(D // NW):
            core.wait_tile(pe, tile)
            for tt in range(TT):
                for k in range(ktile):
                    last = core.nc.tensor.matmul(
                        core.ps[:, bank0 + tt * 2 + half, :], srcT[:, k0 + k, tt * P:(tt + 1) * P],
                        core.slot(tile, ktile, NW)[:, k, :],
                        start=(k0 + k == 0), stop=(k0 + k == kt - 1))
            core.fill(last, bank=(k0 + KW >= kt and half == 1), slots=1)
            tile += 1
    return tile


def add_to_x(core, dve, unit, bank0):
    core.wait_bank(dve, unit)
    for tt in range(TT):
        core.nc.vector.tensor_tensor(core.x[:, tt, :], core.x[:, tt, :],
                                     core.ps[:, bank0 + 2 * tt:bank0 + 2 * tt + 2, :].rearrange("p b n -> p (b n)"),
                                     ALU.add)


def norm_stage(core, src, dst, gain_col, scratch, extra_sp=None, also=None):
    nc = core.nc
    sums, root, inv, scaled, turned, freed = (core.sig(f"norm_{n}") for n in
                                              ("sums", "root", "inv", "scaled", "turned", "freed"))
    sq, xs = core.a(scratch, D), core.a(scratch + D, TT * D).rearrange("p (t d) -> p t d", t=TT)
    st = core.stat

    def act(e):
        for tt in range(TT):
            nc.scalar.activation(sq, src[:, tt, :], ACT.Square, accum_out=st[:, tt:tt + 1]).then_inc(*sums.up())
            e.wait_ge(*sums.at(tt + 1))
            nc.scalar.activation(st[:, 2 + tt:3 + tt], st[:, tt:tt + 1], ACT.Sqrt, scale=1.0 / D,
                                 bias=core.c("eps")[:, E_EPS:E_EPS + 1]).then_inc(*root.up())
        for b in range(2):
            evac(e, nc.scalar, 2 * b + 1)

    def evac(e, eng, b):
        e.wait_ge(*turned.at(b + 1))
        for j in range(2):
            k = 2 * b + j
            g = core.cols[:, gain_col[0], gain_col[1] + k:gain_col[1] + k + 1]
            if eng is nc.scalar:
                eng.activation(dst[:, k, :], core.ps[:, b, j * T:(j + 1) * T], ACT.Identity, scale=g)
            else:
                eng.tensor_scalar(dst[:, k, :], core.ps[:, b, j * T:(j + 1) * T], g, None, ALU.mult)

    def dve(e):
        for tt in range(TT):
            e.wait_ge(*root.at(tt + 1))
            nc.vector.reciprocal(st[:, 4 + tt:5 + tt], st[:, 2 + tt:3 + tt]).then_inc(*inv.up())
            e.wait_ge(*inv.at(tt + 1))
            nc.vector.tensor_scalar(xs[:, tt, :], src[:, tt, :], st[:, 4 + tt:5 + tt], None, ALU.mult)\
                .then_inc(*scaled.up())
        for b in range(2):
            evac(e, nc.vector, 2 * b)

    def pe(e):
        e.wait_ge(*scaled.at(TT))
        for b in range(4):
            for j in range(2):
                for tt in range(TT):
                    k = 2 * b + j
                    last = nc.tensor.transpose(core.ps[:, b, j * T + tt * P:j * T + (tt + 1) * P],
                                               xs[:, tt, k * P:(k + 1) * P], core.c("ident"))
            last.then_inc(*turned.up())

    stage(core, sp=extra_sp, pe=pe, act=act, dve=dve)


def grouped_norm(core, buf, ntiles, mean, span, scale2, eps_col, gain, sq, root, bank0=0, subtract=False):
    nc = core.nc
    squares, means, roots, done = (core.sig(f"group_{n}") for n in ("squares", "means", "roots", "inv"))
    units = ntiles // 2

    def act(e):
        for u in range(units):
            nc.scalar.activation(sq[:, u % 2, :], buf[:, 2 * u:2 * u + 2, :].rearrange("p a t -> p (a t)"),
                                 ACT.Square).then_inc(*squares.up())
            if u:
                take_root(e, u - 1)
        take_root(e, units - 1)

    def take_root(e, u):
        e.wait_ge(*means.at(u + 1))
        if u >= 2:
            e.wait_ge(*done.at(u - 1))
        nc.scalar.activation(root[:, u % 2, :], core.ps[:, bank0 + u % 4, :], ACT.Sqrt, scale=scale2,
                             bias=core.c("eps")[:, eps_col:eps_col + 1]).then_inc(*roots.up())

    def pe(e):
        for u in range(units):
            e.wait_ge(*squares.at(u + 1))
            if u >= 4:
                e.wait_ge(*roots.at(u - 3))
            for j in range(2):
                for s in range(span):
                    src = sq[:, u % 2, (s if span == 2 else j) * T:((s if span == 2 else j) + 1) * T]
                    last = nc.tensor.matmul(core.ps[:, bank0 + u % 4, j * T:(j + 1) * T], mean, src,
                                            start=(s == 0), stop=(s == span - 1))
            last.then_inc(*means.up())

    def dve(e):
        for u in range(units):
            e.wait_ge(*roots.at(u + 1))
            core.link(e, "dve", nc.vector.reciprocal(root[:, u % 2, :], root[:, u % 2, :]))
            for j in range(2):
                last = nc.vector.scalar_tensor_tensor(buf[:, 2 * u + j, :], buf[:, 2 * u + j, :], gain(2 * u + j),
                                                      root[:, u % 2, j * T:(j + 1) * T], ALU.mult, ALU.mult)
            last.then_inc(*done.up())

    return pe, act, dve


def attention(core, heads, comps, q_rows, k_rows, v_cols, dv, causal, bias, vN, oT, scratch, lam=None):
    nc = core.nc
    units = heads * comps
    W = CAUS if causal else 2 * T
    q1 = P if causal else T
    spans = [(0, q1), (q1, T)]
    nd = max(1, dv // P)
    pair = dv == DH
    scores, negmax, expd, probs, flipped, copied, outs, kept = (
        core.sig(f"attn_{n}") for n in
        ("scores", "negmax", "expd", "probs", "flipped", "copied", "outs", "kept"))
    s_sb = core.a(scratch, 2 * 512).rearrange("p (b n) -> p b n", b=2)
    p_sb = core.a(scratch + 1024, 4 * 512).rearrange("p (b n) -> p b n", b=4)
    pT = core.a(scratch + 3072, 2 * 512).rearrange("p (b n) -> p b n", b=2)
    nmx = core.a(scratch + 4096, 2 * units)
    sums = core.a(scratch + 4096 + 2 * units, 2 * units)
    rs = core.a(scratch + 4096 + 4 * units, 2 * units)

    def pe(e):
        for s in range(heads + 2):
            if s < heads:
                for c in range(comps):
                    u = s * comps + c
                    if u >= 2:
                        e.wait_ge(*probs.at(u - 1))
                    for tt in range(TT):
                        lo, n = spans[tt]
                        ql, kl = q_rows(u, tt), k_rows(u, n)
                        for i, (q, k) in enumerate(zip(ql, kl)):
                            last = nc.tensor.matmul(core.ps[:, u % 2, lo:lo + n], q, k,
                                                    start=(i == 0), stop=(i == len(ql) - 1))
                    last.then_inc(*scores.up())
            if 1 <= s <= heads:
                h = s - 1
                u = (h + 1) * comps - 1
                e.wait_ge(*probs.at(u + 1))
                if h >= 2:
                    e.wait_ge(*copied.at(h - 1))
                for tt in range(TT):
                    lo, n = spans[tt]
                    for kt in range(n // P):
                        at = (kt * T + tt * P) if (kt == 0 or not causal) else T
                        last = nc.tensor.transpose(core.ps[:, 2 + h % 2, at:at + P],
                                                   p_sb[:, u % 4, lo + kt * P:lo + (kt + 1) * P], core.c("ident"))
                last.then_inc(*flipped.up())
            if s >= 2:
                h = s - 2
                e.wait_ge(*copied.at(h + 1))
                o = h // 2 if pair else h
                if o >= 4 and (not pair or h % 2 == 0):
                    e.wait_ge(*kept.at(o - 3))
                for d in range(nd):
                    m = min(dv, P)
                    m0 = DH * (h % 2) if pair else 0
                    for kt in range(2):
                        if kt == 0 or not causal:
                            cols, src = (d * T, T), pT[:, h % 2, kt * T:(kt + 1) * T]
                        else:
                            cols, src = (d * T + P, P), pT[:, h % 2, T:T + P]
                        last = nc.tensor.matmul(core.ps[m0:m0 + m, 4 + o % 4, cols[0]:cols[0] + cols[1]],
                                                vN[:, kt, v_cols(h) + d * P:v_cols(h) + d * P + m], src,
                                                start=(kt == 0), stop=(kt == 1))
                last.then_inc(*outs.up())

    def act(e):
        for s in range(heads + 2):
            if s < heads:
                for c in range(comps):
                    u = s * comps + c
                    e.wait_ge(*negmax.at(u + 1))
                    if u >= 4:
                        e.wait_ge(*flipped.at((u - 4) // comps + 1))
                    for tt in range(TT):
                        lo, n = spans[tt]
                        src = s_sb[:, u % 2, lo:lo + n] if bias else core.ps[:, u % 2, lo:lo + n]
                        last = nc.scalar.activation(p_sb[:, u % 4, lo:lo + n], src, ACT.Exp,
                                                    bias=nmx[:, 2 * u + tt:2 * u + tt + 1],
                                                    accum_out=sums[:, 2 * u + tt:2 * u + tt + 1])
                    last.then_inc(*expd.up())
            if 1 <= s <= heads:
                h = s - 1
                e.wait_ge(*flipped.at(h + 1))
                if h >= 2:
                    e.wait_ge(*outs.at(h - 1))
                nc.scalar.activation(pT[:, h % 2, 0:W], core.ps[:, 2 + h % 2, 0:W], ACT.Copy).then_inc(*copied.up())
            if s >= 2:
                h = s - 2
                if not pair or h % 2 == 1:
                    o = h // 2 if pair else h
                    e.wait_ge(*outs.at(h + 1))
                    nc.scalar.activation(oT[:, o * nd:(o + 1) * nd, :].rearrange("p a t -> p (a t)"),
                                         core.ps[:, 4 + o % 4, 0:nd * T], ACT.Copy).then_inc(*kept.up())

    def dve(e):
        for u in range(units + 1):
            if u < units:
                e.wait_ge(*scores.at(u + 1))
                if bias:
                    b = bias(e, u)
                    if u >= 2:
                        e.wait_ge(*expd.at(u - 1))
                    for tt in range(TT):
                        lo, n = spans[tt]
                        last = nc.vector.tensor_tensor_reduce(
                            out=s_sb[:, u % 2, lo:lo + n], in0=core.ps[:, u % 2, lo:lo + n], in1=b[tt], scale=1.0,
                            scalar=-3e38, op0=ALU.add, op1=ALU.max, accum_out=rs[:, 2 * u + tt:2 * u + tt + 1])
                    core.link(e, "dve", last)
                    nc.vector.tensor_scalar(nmx[:, 2 * u:2 * u + 2], rs[:, 2 * u:2 * u + 2], -1.0, None, ALU.mult)\
                        .then_inc(*negmax.up())
                else:
                    nc.vector.tensor_reduce(nmx[:, 2 * u:2 * u + 2],
                                            core.ps[:, u % 2, :].rearrange("p (t n) -> p t n", t=TT),
                                            AXX, ALU.max, negate=True).then_inc(*negmax.up())
            if u >= 1:
                w = u - 1
                e.wait_ge(*expd.at(w + 1))
                core.link(e, "dve", nc.vector.reciprocal(rs[:, 2 * w:2 * w + 2], sums[:, 2 * w:2 * w + 2]))
                second = comps == 2 and w % 2 == 1
                if second:
                    e.wait_ge(*probs.at(w))
                    core.link(e, "dve", nc.vector.tensor_scalar(rs[:, 2 * w:2 * w + 2], rs[:, 2 * w:2 * w + 2],
                                                                lam, None, ALU.mult))
                for tt in range(TT):
                    lo, n = spans[tt]
                    p = p_sb[:, w % 4, lo:lo + n]
                    r = rs[:, 2 * w + tt:2 * w + tt + 1]
                    if second:
                        last = nc.vector.scalar_tensor_tensor(p, p, r, p_sb[:, (w - 1) % 4, lo:lo + n],
                                                              ALU.mult, ALU.add)
                    else:
                        last = nc.vector.tensor_scalar(p, p, r, None, ALU.mult)
                last.then_inc(*probs.up())

    return pe, act, dve


def bc(ap, axis, n):
    ap = ap.unsqueeze(axis)
    shape = list(ap.shape)
    shape[axis] = n
    return ap.broadcast_to(shape)


def cross_attention(core, w, layer, at_col, project_to_x, mem_off):
    nc, a, ps, c = core.nc, core.a, core.ps, core.c
    freed = core.sig("bank_copied")
    MH, MD = 4, 256
    mem = a(mem_off, TT * D).rearrange("p (t d) -> p t d", t=TT)
    memT = a(mem_off + 2048, KD * T).rearrange("p (k t) -> p k t", k=KD)
    mem_landed = core.sig("memory_landed")

    def sp(e):
        e.dma_start(mem, w["mem_2"][0].rearrange("(t p) d -> p t d", p=P)).then_inc(*mem_landed.up(16))
    norm_stage(core, core.x, core.xnT, at_col("norm_xattn_2", 8 * layer), 0, extra_sp=sp)

    def sp(e):
        e.wait_ge(*mem_landed.at(0))
    stage(core, sp=sp)
    norm_stage(core, mem, memT, at_col("norm_mem_2", 8 * layer), 0)

    qk = a(0, 16 * T).rearrange("p (n t) -> p n t", t=T)
    vN = a(4096, TT * D).rearrange("p (t d) -> p t d", t=TT)
    oT = a(6144, 8 * T).rearrange("p (n t) -> p n t", t=T)
    SCR = 8192

    def pe(e):
        u, tile = features_matmul(core, e, 0, core.xnT, KD, [NW] * 2, freed, 0, 4, core.taken)
        u, tile = features_matmul(core, e, u, memT, KD, [NW] * 2, freed, 0, 4, tile)
        tokens_matmul(core, e, 0, memT, KD, [NW] * 2, freed, 4, 4, tile)

    def act(e):
        for u in range(8):
            core.wait_bank(e, u)
            nc.scalar.activation(qk[:, 2 * u:2 * u + 2, :].rearrange("p a t -> p (a t)"), ps[:, u % 4, :], ACT.Copy)\
                .then_inc(*freed.up())
        for u in range(4):
            core.wait_bank(e, 8 + u)
            nc.scalar.activation(vN[:, u % 2, (u // 2) * NW:(u // 2 + 1) * NW], ps[:, 4 + u, :], ACT.Copy)
    stage(core, pe=pe, act=act, uses=12)

    sq = a(SCR, 1024).rearrange("p (b n) -> p b n", b=2)
    root = a(SCR + 1024, 1024).rearrange("p (b n) -> p b n", b=2)

    def gain(name):
        which, r = at_col(name, 2 * layer)
        return lambda j: core.cols[:, which, r + j % 2:r + j % 2 + 1]
    for part, scale2, eps, name in ((0, 256.0, E_EPS256, "xa_q_gain_2"), (8, 1.0, E_EPS, "xa_k_gain_2")):
        gpe, gact, gdve = grouped_norm(core, qk[:, part:part + 8, :], 8, c("mean256"), 2, scale2, eps, gain(name), sq, root)
        stage(core, pe=gpe, act=gact, dve=gdve)
    q, k = qk[:, 0:8, :], qk[:, 8:16, :]
    pe, act, dve = attention(core, MH, 1, lambda u, tt: [q[:, 2 * u + i, tt * P:(tt + 1) * P] for i in range(2)],
                             lambda u, n: [k[:, 2 * u + i, 0:n] for i in range(2)], lambda h: h * MD, MD, False,
                             None, vN, oT, SCR)
    stage(core, pe=pe, act=act, dve=dve)
    project_to_x(oT)


def swiglu(core):
    nc, a, ps = core.nc, core.a, core.ps
    hT = a(0, FF2 // P * T).rearrange("p (n t) -> p n t", t=T)
    tmp = a(8192, 2 * 512).rearrange("p (b n) -> p b n", b=2)
    silud, multiplied = core.sig("silu_done"), core.sig("gated")
    widths = [min(NW, FF2 - n0) for n0 in range(0, FF2, NW)]
    n = FF2 // (2 * P)

    def pe(e):
        tile, done = core.taken, 0
        for width in widths:
            units = width // (2 * P)
            for part in range(2):
                for j in range(2):
                    core.wait_tile(e, tile + j)
                for b in range(units):
                    u = done + b
                    if u >= 2:
                        e.wait_ge(*multiplied.at(u - 1))
                    for h in range(2):
                        m0 = (2 * b + h) * P
                        for k in range(KD):
                            last = nc.tensor.matmul(ps[:, 2 * part + u % 2, h * T:(h + 1) * T],
                                                    core.slot(tile + k // KW, KW, width)[:, k % KW, m0:m0 + P],
                                                    core.xnT[:, k, :], start=(k == 0), stop=(k == KD - 1))
                    core.fill(last, bank=True, slots=2 if b == units - 1 else 0)
                tile += 2
            done += units
        e.wait_ge(*multiplied.at(n))
        down_matmul(core, e, hT, FF2 // P, 4, tile)

    order = []
    for i, width in enumerate(widths):
        units = width // (2 * P)
        base = sum(widths[:i]) // P
        order += [(base + b, base + units + b) for b in range(units)]

    def act(e):
        for u in range(n):
            core.wait_bank(e, order[u][0])
            if u >= 2:
                e.wait_ge(*multiplied.at(u - 1))
            nc.scalar.activation(tmp[:, u % 2, :], ps[:, u % 2, :], ACT.Silu).then_inc(*silud.up())

    def dve(e):
        for u in range(n):
            core.wait_bank(e, order[u][1])
            e.wait_ge(*silud.at(u + 1))
            nc.vector.tensor_tensor(hT[:, 2 * u:2 * u + 2, :].rearrange("p a t -> p (a t)"), ps[:, 2 + u % 2, :],
                                    tmp[:, u % 2, :], ALU.mult).then_inc(*multiplied.up())
        add_to_x(core, e, 2 * n, 4)
    stage(core, pe=pe, act=act, dve=dve, uses=4 * len(widths) + 2 * -(-FF2 // P // KW))


def mixture(core, w, l0, small):
    nc, a, ps, c, x, xnT = core.nc, core.a, core.ps, core.c, core.x, core.xnT
    link = core.link
    wr = a(0, KD * NE).rearrange("p (k e) -> p k e", k=KD)
    br = a(64, NE)
    lg = a(80, 16).rearrange("p (t e) -> p t e", t=2)
    top = a(96, 16).rearrange("p (t e) -> p t e", t=2)
    idx = a(112, 16).bitcast(U32).rearrange("p (t e) -> p t e", t=2)
    idf = a(128, 16).rearrange("p (t e) -> p t e", t=2)
    diff, ex, w1, w2 = (a(144 + 2 * i, 2) for i in range(4))
    onehot = a(160, 32).rearrange("p (t i e) -> p t i e", t=2, i=2)
    gates = small[:, 0:16].rearrange("p (t e) -> p t e", t=2)
    gated, summed = core.sig("moe_gated"), core.sig("moe_summed")
    landed, logits, shifted = core.sig("router_landed"), core.sig("router_logits"), core.sig("router_gap")
    expd = core.sig("router_exp")

    def sp(e):
        e.dma_start(wr, k_tiles(l0["moe_w_router_2"])).then_inc(*landed.up(16))
        e.dma_start(br, w["moe_b_router_2"][0].partition_broadcast(P)).then_inc(*landed.up(16))
        e.sem_inc(gated.sem, 1)
        e.sem_inc(summed.sem, 1)

    def pe(e):
        e.wait_ge(*landed.at(32))
        for tt in range(TT):
            for k in range(KD):
                last = nc.tensor.matmul(ps[:, 0, tt * NE:(tt + 1) * NE], xnT[:, k, tt * P:(tt + 1) * P], wr[:, k, :],
                                        start=(k == 0), stop=(k == KD - 1))
        last.then_inc(*logits.up())

    def dve(e):
        e.wait_ge(*landed.at(32))
        e.wait_ge(*logits.at(1))
        link(e, "dve", nc.vector.tensor_tensor(lg, ps[:, 0, 0:16].rearrange("p (t e) -> p t e", t=2), bc(br, 1, 2), ALU.add))
        for tt in range(TT):
            link(e, "dve", nc.vector.max(top[:, tt, :], lg[:, tt, :]))
            link(e, "dve", nc.vector.max_index(idx[:, tt, :], top[:, tt, :], lg[:, tt, :]))
        nc.vector.tensor_tensor(diff, top[:, :, 1], top[:, :, 0], ALU.subtract).then_inc(*shifted.up())
        link(e, "dve", nc.vector.tensor_copy(idf, idx))
        for tt in range(TT):
            for i in range(2):
                link(e, "dve", nc.vector.tensor_scalar(onehot[:, tt, i, :], c("iota8"), idf[:, tt, i:i + 1], None, ALU.is_equal))
        e.wait_ge(*expd.at(1))
        link(e, "dve", nc.vector.tensor_scalar(w1, ex, 1.0, None, ALU.add))
        link(e, "dve", nc.vector.reciprocal(w1, w1))
        link(e, "dve", nc.vector.tensor_tensor(w2, ex, w1, ALU.mult))
        for tt in range(TT):
            link(e, "dve", nc.vector.tensor_scalar(gates[:, tt, :], onehot[:, tt, 0, :], w1[:, tt:tt + 1], None, ALU.mult))
            link(e, "dve", nc.vector.scalar_tensor_tensor(gates[:, tt, :], onehot[:, tt, 1, :], w2[:, tt:tt + 1],
                                                          gates[:, tt, :], ALU.mult, ALU.add))

    def act(e):
        e.wait_ge(*shifted.at(1))
        nc.scalar.activation(ex, diff, ACT.Exp).then_inc(*expd.up())
    stage(core, sp=sp, pe=pe, act=act, dve=dve)

    assert core.issued == core.taken == len(core.tiles)
    first = core.taken
    chunks, halves = FE // NW, 2
    per = chunks * (2 * halves) + FE // P // KW * 2
    turns = per // RING
    assert per % RING == 0
    hT = a(0, FE // P * T).rearrange("p (n t) -> p n t", t=T)
    tmp = a(8192, 4 * 512).rearrange("p (b n) -> p b n", b=4)
    gate_up, silud, gated, down, summed = (core.sig(f"moe_{n}") for n in
        ("gate_up", "silu", "gated", "down", "summed"))
    wg, wu, wd = l0["moe_w_gate_2"], l0["moe_w_up_2"], l0["moe_w_down_2"]
    units = 2 * chunks

    def source(e_reg, j):
        if j < 4 * chunks:
            chunk, part, half = j // 4, (j // 2) % 2, j % 2
            m = (wg, wu)[part][bass.ds(e_reg, 1), half * 512:(half + 1) * 512, chunk * NW:(chunk + 1) * NW]
        else:
            r = j - 4 * chunks
            m = wd[bass.ds(e_reg, 1), (r // 2) * 512:(r // 2 + 1) * 512, (r % 2) * NW:(r % 2 + 1) * NW]
        return m.rearrange("e (k p) n -> p (e k) n", p=P)

    def slot(j):
        return (first + j) % RING

    turns_taken = core.sig("moe_turns")

    def used_up(e, j):
        if j < 4 * chunks:
            return gate_up.sem, e * (4 * chunks) + (4 * (j // 4) + 2 + (j // 2) % 2 + 1)
        return down.sem, e * (per - 4 * chunks) + (j - 4 * chunks + 1)

    def landed_value(e, j):
        return 16 * ((first + j) // RING + 1) + e * (16 * turns)

    with nc.Block(no_gpsimd_drain=True) as block:
        @block.sync
        def _(sp):
            def load(ex, j):
                sp.dma_start(core.ring[:, slot(j), :].rearrange("p (k n) -> p k n", n=NW), source(ex, j))\
                    .then_inc(core.landed[slot(j)].sem, 16)

            def free_slot(ex, j):
                sp.wait_ge(*used_up(ex, j))
                sp.sem_inc(turns_taken.sem, 1)
            for j in range(RING):
                load(0, j)
            with sp.Fori(0, NE - 1) as ex:
                for j in range(RING, per):
                    free_slot(ex, j - RING)
                    load(ex, j)
                for j in range(RING):
                    free_slot(ex, per + j - RING)
                    load(ex + 1, j)
            for j in range(RING, per):
                free_slot(NE - 1, j - RING)
                load(NE - 1, j)

        @block.tensor
        def _(pe):
            with pe.Fori(0, NE) as ex:
                for chunk in range(chunks):
                    for b in range(2):
                        u = 2 * chunk + b
                        pe.wait_ge(gated.sem, ex * units + max(u, 1))
                        for part in range(2):
                            if b == 0:
                                for half in range(halves):
                                    j = 4 * chunk + 2 * part + half
                                    pe.wait_ge(core.landed[slot(j)].sem, landed_value(ex, j))
                            for h in range(2):
                                for k in range(KD):
                                    s = slot(4 * chunk + 2 * part + k // KW)
                                    at = (k % KW) * NW + (2 * b + h) * P
                                    last = nc.tensor.matmul(ps[:, 2 * part + u % 2, h * T:(h + 1) * T],
                                                            core.ring[:, s, at:at + P], xnT[:, k, :],
                                                            start=(k == 0), stop=(k == KD - 1))
                            last.then_inc(gate_up.sem, 1)
                pe.wait_ge(gated.sem, ex * units + (units + 1))
                pe.wait_ge(summed.sem, ex + 1)
                for r in range(FE // P // KW):
                    for half in range(2):
                        j = 4 * chunks + 2 * r + half
                        pe.wait_ge(core.landed[slot(j)].sem, landed_value(ex, j))
                        for tt in range(TT):
                            for k in range(KW):
                                last = nc.tensor.matmul(ps[:, 4 + 2 * tt + half, :],
                                                        hT[:, r * KW + k, tt * P:(tt + 1) * P],
                                                        core.ring[:, slot(j), k * NW:(k + 1) * NW],
                                                        start=(r + k == 0), stop=(r * KW + k == FE // P - 1))
                        last.then_inc(down.sem, 1)

        @block.scalar
        def _(act):
            with act.Fori(0, NE) as ex:
                for u in range(units):
                    act.wait_ge(gate_up.sem, ex * (2 * units) + (2 * u + 1))
                    act.wait_ge(gated.sem, ex * units + max(u, 1))
                    nc.scalar.activation(tmp[:, u % 2, :], ps[:, u % 2, :], ACT.Silu).then_inc(silud.sem, 1)

        @block.vector
        def _(dve):
            with dve.Fori(0, NE) as ex:
                for u in range(units):
                    dve.wait_ge(gate_up.sem, ex * (2 * units) + (2 * u + 2))
                    dve.wait_ge(silud.sem, ex * units + (u + 1))
                    nc.vector.tensor_tensor(hT[:, 2 * u:2 * u + 2, :].rearrange("p a t -> p (a t)"),
                                            ps[:, 2 + u % 2, :], tmp[:, u % 2, :], ALU.mult).then_inc(gated.sem, 1)
                dve.wait_ge(down.sem, ex * (2 * units // 2) + (per - 4 * chunks))
                for tt in range(TT):
                    last = nc.vector.scalar_tensor_tensor(
                        x[:, tt, :], ps[:, 4 + 2 * tt:6 + 2 * tt, :].rearrange("p b n -> p (b n)"),
                        gates[:, tt, bass.ds(ex, 1)], x[:, tt, :], ALU.mult, ALU.add)
                last.then_inc(summed.sem, 1)
                dve.wait_ge(summed.sem, ex + 2)


def rwkv_s5(core, w, l0, col, at_col, small):
    nc, a, ps, c, x, xnT, link = core.nc, core.a, core.ps, core.c, core.x, core.xnT, core.link
    freed = core.sig("bank_copied")
    NT = 15
    J = RW // P
    v3 = lambda off, n: a(off, n * T).rearrange("p (n t) -> p n t", t=T)
    flat = lambda b: b.rearrange("p a t -> p (a t)")
    YT = v3(0, 8)
    UT = v3(2048, J)
    LORA_W = a(3072, RW)
    GUP = a(3584, 2 * RW).rearrange("p (k n) -> p k n", k=2)
    Z = a(4608, NT * (T + 1)).rearrange("p (n t) -> p n t", t=T + 1)
    DIF = v3(8704, NT)
    lora_landed = core.sig("lora_landed")

    def sp(e):
        e.dma_start(LORA_W[0:64, :], l0["rw_w_up_2"]).then_inc(*lora_landed.up(16))
        e.dma_start(LORA_W[64:128, :], l0["rw_a_up_2"]).then_inc(*lora_landed.up(16))
        e.dma_start(GUP[:, 0, :], l0["rw_g_up_2"][0:P, :]).then_inc(*lora_landed.up(16))
        e.dma_start(GUP[0:32, 1, :], l0["rw_g_up_2"][P:160, :]).then_inc(*lora_landed.up(16))
    norm_stage(core, x, xnT, at_col("norm_mix_2"), 8704, extra_sp=sp)

    unit_tiles = [(0, 2), (2, 2), (4, 2), (6, 2), (8, 2), (10, 2), (12, 2), (14, 1)]

    def pe(e):
        features_matmul(core, e, 0, xnT, KD, [512, 512, 512, 288, 512], freed, 0, 8, core.taken)

    def dve(e):
        zero = core.sig("z_cleared")
        nc.vector.memset(Z[:, :, 0:1], 0.0)
        nc.vector.memset(Z[:, 14, 1:T + 1], 0.0).then_inc(*zero.up())
        e.wait_ge(*zero.at(1))
        for u, (t0, n) in enumerate(unit_tiles):
            core.wait_bank(e, u)
            m = 32 if u == 7 else P
            nc.vector.tensor_copy(Z[0:m, t0:t0 + n, 1:T + 1], ps[0:m, u, 0:n * T].rearrange("p (n t) -> p n t", t=T))\
                .then_inc(*freed.up())
        for u in (8, 9):
            core.wait_bank(e, u)
            last = nc.vector.tensor_copy(flat(UT[:, 2 * (u - 8):2 * (u - 8) + 2, :]), ps[:, u - 8, :])
            last.then_inc(*freed.up())
        e.wait_ge(*freed.at(8))
        link(e, "dve", nc.vector.tensor_tensor(DIF, Z[:, :, 0:T], Z[:, :, 1:T + 1], ALU.subtract))
        for t in range(NT):
            nc.vector.scalar_tensor_tensor(DIF[:, t, :], DIF[:, t, :], col("mu", t), Z[:, t, 1:T + 1], ALU.mult, ALU.add)
    stage(core, pe=pe, dve=dve, uses=10)

    R, K, V = DIF[:, 0:4, :], DIF[:, 4:8, :], DIF[:, 8:12, :]
    WA, GD = DIF[:, 12, :], DIF[:, 13:15, :]
    G = v3(4608, J)
    A = v3(5632, J)
    LD = v3(6656, J)
    LC = v3(7680, J)
    KK = v3(12544, J)
    PINC, PINV, PEXC = v3(13568, J), v3(14592, J), v3(15616, J)
    BT, KT = v3(16640, J), v3(17664, J)
    AR = a(18688, 2 * J * T).rearrange("p (j t q n) -> p j t q n", j=J, t=TT, q=2)
    BON = v3(20736, J)
    VN = a(21760, TT * RW).rearrange("p (t n) -> p t n", t=TT)

    act_in, lora, act_out = core.sig("lora_inputs"), core.sig("lora_products"), core.sig("lora_applied")
    scan_done, kk_in, kk_sum, kk_root = (core.sig(f"kk_{n}") for n in ("scan", "squares", "sums", "roots"))

    def pe(e):
        e.wait_ge(*lora_landed.at(0))
        e.wait_ge(*act_in.at(1))
        for j in range(J):
            last = nc.tensor.matmul(ps[:, j // 2, (j % 2) * T:(j % 2 + 1) * T], LORA_W[0:64, j * P:(j + 1) * P],
                                    WA[0:64, :], start=True, stop=True)
        last.then_inc(*lora.up())
        for j in range(J):
            last = nc.tensor.matmul(ps[:, 2 + j // 2, (j % 2) * T:(j % 2 + 1) * T], LORA_W[64:128, j * P:(j + 1) * P],
                                    WA[64:128, :], start=True, stop=True)
        last.then_inc(*lora.up())
        e.wait_ge(*act_in.at(2))
        for j in range(J):
            nc.tensor.matmul(ps[:, 4 + j // 2, (j % 2) * T:(j % 2 + 1) * T], GUP[:, 0, j * P:(j + 1) * P],
                             GD[:, 0, :], start=True, stop=False)
            last = nc.tensor.matmul(ps[:, 4 + j // 2, (j % 2) * T:(j % 2 + 1) * T], GUP[0:32, 1, j * P:(j + 1) * P],
                                    GD[0:32, 1, :], start=False, stop=True)
        last.then_inc(*lora.up())
        e.wait_ge(*kk_in.at(1))
        for j in range(J):
            last = nc.tensor.matmul(ps[:, 6 + j // 2, (j % 2) * T:(j % 2 + 1) * T], c("sum64"), PEXC[:, j, :],
                                    start=True, stop=True)
        last.then_inc(*kk_sum.up())

    def act(e):
        nc.scalar.activation(WA[0:64, :], WA[0:64, :], ACT.Tanh).then_inc(*act_in.up())
        nc.scalar.activation(flat(GD), flat(GD), ACT.Sigmoid).then_inc(*act_in.up())
        e.wait_ge(*lora.at(1))
        for j in range(J):
            last = nc.scalar.activation(LD[:, j, :], ps[:, j // 2, (j % 2) * T:(j % 2 + 1) * T], ACT.Sigmoid,
                                        bias=col("rw_w0_2", j))
        last.then_inc(*act_out.up())
        e.wait_ge(*lora.at(2))
        for j in range(J):
            last = nc.scalar.activation(A[:, j, :], ps[:, 2 + j // 2, (j % 2) * T:(j % 2 + 1) * T], ACT.Sigmoid,
                                        bias=col("rw_a0_2", j))
        last.then_inc(*act_out.up())
        e.wait_ge(*lora.at(3))
        nc.scalar.activation(flat(G), ps[:, 4:6, :].rearrange("p b n -> p (b n)"), ACT.Copy)
        e.wait_ge(*kk_root.at(1))
        nc.scalar.activation(flat(PEXC), flat(PEXC), ACT.Sqrt).then_inc(*kk_root.up())

    def dve(e):
        for j in range(J):
            last = nc.vector.tensor_scalar(KK[:, j, :], K[:, j, :], col("rw_k_k_2", j), None, ALU.mult)
        link(e, "dve", last)
        nc.vector.tensor_tensor(flat(PEXC), flat(KK), flat(KK), ALU.mult).then_inc(*kk_in.up())
        e.wait_ge(*act_out.at(1))
        link(e, "dve", nc.vector.tensor_scalar(flat(LD), flat(LD), -math.exp(-0.5), None, ALU.mult))
        link(e, "dve", nc.vector.tensor_tensor_scan(flat(LC), c("carry"), flat(LD), 0.0, ALU.mult, ALU.add))
        e.wait_ge(*kk_sum.at(1))
        nc.vector.tensor_scalar(flat(PEXC), ps[:, 6:8, :].rearrange("p b n -> p (b n)"), 1e-24, None, ALU.max)\
            .then_inc(*kk_root.up())
        e.wait_ge(*kk_root.at(2))
        link(e, "dve", nc.vector.reciprocal(flat(PEXC), flat(PEXC)))
        link(e, "dve", nc.vector.tensor_tensor(flat(KK), flat(KK), flat(PEXC), ALU.mult))
        e.wait_ge(*act_out.at(2))
        for j in range(J):
            link(e, "dve", nc.vector.tensor_scalar(small[:, 20 + j:21 + j], col("rw_k_a_2", j), -1.0, 1.0, ALU.mult, ALU.add))
        for j in range(J):
            last = nc.vector.tensor_scalar(PINC[:, j, :], A[:, j, :], col("rw_k_a_2", j), small[:, 20 + j:21 + j],
                                           ALU.mult, ALU.add)
        link(e, "dve", last)
        link(e, "dve", nc.vector.tensor_tensor(flat(K), flat(K), flat(PINC), ALU.mult))
        for j in range(J):
            last = nc.vector.scalar_tensor_tensor(BON[:, j, :], R[:, j, :], col("rw_r_k_2", j), K[:, j, :], ALU.mult, ALU.mult)
        nc.vector.tensor_tensor(flat(PEXC), flat(LC), flat(LD), ALU.subtract)
        nc.vector.tensor_tensor(flat(A), flat(A), flat(KK), ALU.mult)
    stage(core, pe=pe, act=act, dve=dve)

    exps, applied, turned, bsum = (core.sig(f"decay_{n}") for n in ("exps", "applied", "turned", "bonus"))
    PC = small[:, 24:24 + J * NCH].rearrange("p (j c) -> p j c", c=NCH)
    BN = a(4608 + 1024, TT * RW).rearrange("p (t n) -> p t n", t=TT)
    KN = a(6656, TT * RW).rearrange("p (t n) -> p t n", t=TT)

    def act(e):
        nc.scalar.activation(flat(PINV), flat(LC), ACT.Exp, scale=-1.0).then_inc(*exps.up())
        nc.scalar.activation(flat(PINC), flat(LC), ACT.Exp).then_inc(*exps.up())
        nc.scalar.activation(flat(PEXC), flat(PEXC), ACT.Exp).then_inc(*exps.up())
        for i, dst in enumerate((VN, BN, KN)):
            e.wait_ge(*turned.at(i + 1))
            for tt in range(TT):
                nc.scalar.activation(dst[:, tt, :], ps[:, 2 * i + tt, :], ACT.Copy)

    def dve(e):
        e.wait_ge(*exps.at(1))
        nc.vector.tensor_tensor(flat(BT), flat(A), flat(PINV), ALU.mult).then_inc(*applied.up())
        nc.vector.tensor_tensor(flat(KT), flat(K), flat(PINV), ALU.mult).then_inc(*applied.up())
        e.wait_ge(*exps.at(3))
        shape = lambda b: b.rearrange("p j (t n) -> p j t n", t=TT)
        for j in range(J):
            nc.vector.tensor_tensor(AR[:, j, :, 0, :], shape(KK)[:, j], shape(PEXC)[:, j], ALU.mult)
            nc.vector.tensor_tensor(AR[:, j, :, 1, :], shape(R)[:, j], shape(PINC)[:, j], ALU.mult)
        nc.vector.tensor_copy(PC, PINC.rearrange("p j (c n) -> p j c n", n=CH)[:, :, :, CH - 1])
        e.wait_ge(*bsum.at(1))
        nc.vector.tensor_tensor(flat(BON), ps[:, 6:8, :].rearrange("p b n -> p (b n)"), flat(V), ALU.mult)

    def pe(e):
        for i, src in enumerate((V, BT, KT)):
            if i:
                e.wait_ge(*applied.at(i))
            for tt in range(TT):
                for j in range(J):
                    last = nc.tensor.transpose(ps[:, 2 * i + tt, j * P:(j + 1) * P], src[:, j, tt * P:(tt + 1) * P], c("ident"))
            last.then_inc(*turned.up())
        for j in range(J):
            last = nc.tensor.matmul(ps[:, 6 + j // 2, (j % 2) * T:(j % 2 + 1) * T], c("sum64"), BON[:, j, :],
                                    start=True, stop=True)
        last.then_inc(*bsum.up())
    stage(core, pe=pe, act=act, dve=dve)

    NU = 16
    PB, PK = (a(off, NU * 256).rearrange("p (u n) -> p u n", u=NU) for off in (7680, 11776))
    pairs, masked = core.sig("pairs"), core.sig("pairs_masked")
    at, _ = core.const_at["strict"]
    masks = core.const[:, at:at + 2 * P]

    def pe(e):
        for u in range(NU):
            j, tt, hp = u // 4, (u // 2) % 2, u % 2
            if u >= 4:
                e.wait_ge(*masked.at(u - 3))
            rows = slice(64 * hp, 64 * hp + 64)
            for i, src in enumerate((BT, KT)):
                last = nc.tensor.matmul(ps[:, u % 4, i * 256:(i + 1) * 256], src[rows, j, tt * P:(tt + 1) * P],
                                        AR[rows, j, tt, :, :].rearrange("p q n -> p (q n)"), start=True, stop=True)
            last.then_inc(*pairs.up())

    def dve(e):
        for u in range(NU):
            e.wait_ge(*pairs.at(u + 1))
            nc.vector.tensor_tensor(PB[:, u, :], ps[:, u % 4, 0:256], masks, ALU.mult)
            nc.vector.tensor_tensor(PK[:, u, :], ps[:, u % 4, 256:512], masks, ALU.mult).then_inc(*masked.up())
    stage(core, pe=pe, dve=dve)

    XT = a(15872, NU * P).rearrange("p (b n) -> p b n", b=4)
    inverse(core, PB, a(0, NU * P).rearrange("p (b n) -> p b n", b=4), XT,
            a(22784, 1024).rearrange("p (b n) -> p b n", b=2), a(3072, 1024).rearrange("p (b n) -> p b n", b=2))
    O = YT[:, 0:4, :]
    recurrence(core, PB, PK, XT, AR, BN, KN, VN, PC, O, a(3072, RW), a(22784, RW),
               a(4096, 512).rearrange("p (j n) -> p j n", j=J))
    head_norm(core, O, BON, G, col, v3(7680, J))
    s5(core, l0, col, UT, YT[:, 4:8, :])

    def pe(e):
        tokens_matmul(core, e, 0, YT, 8, [NW] * 2, freed, 0, 4, core.taken)

    def dve(e):
        for u in range(4):
            core.wait_bank(e, u)
            xs = x[:, u % 2, (u // 2) * NW:(u // 2 + 1) * NW]
            nc.vector.tensor_tensor(xs, xs, ps[:, u, :], ALU.add)
    stage(core, pe=pe, dve=dve, uses=4)


def inverse(core, PB, X, XT, LM, W1):
    nc, ps, c = core.nc, core.ps, core.c
    started, turned, xready, masked, w1, w1_copied, prods, updated = (core.sig(f"inverse_{n}") for n in
        ("started", "turned", "x_ready", "masked", "w1", "w1_copied", "products", "updated"))
    LT = lambda b: PB[:, 4 * b:4 * b + 4, 0:P]
    q = lambda v: v.rearrange("p (u n) -> p u n", u=4)
    levels = (2, 4, 8, 16, 32)
    steps = [(s, b) for s in levels for b in range(4)]

    def dve(e):
        for b in range(4):
            core.link(e, "dve", nc.vector.tensor_tensor(q(XT[:, b, :]), LT(b), bc(c("level1"), 1, 4), ALU.mult))
            nc.vector.tensor_tensor(q(XT[:, b, :]), bc(c("ident"), 1, 4), q(XT[:, b, :]), ALU.subtract)\
                .then_inc(*started.up())
        for n, (s, b) in enumerate(steps):
            e.wait_ge(*prods.at(n + 1))
            if s != levels[-1]:
                nc.vector.tensor_tensor(X[:, b, :], X[:, b, :], ps[:, 2 + n % 2, :], ALU.subtract)
            nc.vector.tensor_tensor(XT[:, b, :], XT[:, b, :], ps[:, 4 + n % 2, :], ALU.subtract).then_inc(*updated.up())

    def act(e):
        for b in range(4):
            e.wait_ge(*turned.at(b + 1))
            nc.scalar.activation(X[:, b, :], ps[:, 6 + b % 2, :], ACT.Copy).then_inc(*xready.up())
        for n in range(len(steps)):
            e.wait_ge(*w1.at(n + 1))
            if n >= 2:
                e.wait_ge(*prods.at(n - 1))
            nc.scalar.activation(W1[:, n % 2, :], ps[:, n % 2, :], ACT.Copy).then_inc(*w1_copied.up())

    def pool(e):
        for n, (s, b) in enumerate(steps):
            if n >= 2:
                e.wait_ge(*w1.at(n - 1))
            nc.gpsimd.tensor_tensor(q(LM[:, n % 2, :]), LT(b), bc(c(f"level{s}"), 1, 4), ALU.mult).then_inc(*masked.up())

    def pe(e):
        for b in range(4):
            e.wait_ge(*started.at(b + 1))
            if b >= 2:
                e.wait_ge(*xready.at(b - 1))
            for u in range(4):
                last = nc.tensor.transpose(ps[:, 6 + b % 2, u * P:(u + 1) * P], XT[:, b, u * P:(u + 1) * P], c("ident"))
            last.then_inc(*turned.up())
        for n in range(len(steps) + 1):
            if n < len(steps):
                s, b = steps[n]
                e.wait_ge(*masked.at(n + 1))
                if n < 4:
                    e.wait_ge(*xready.at(n + 1))
                else:
                    e.wait_ge(*updated.at(n - 3))
                if n >= 2:
                    e.wait_ge(*w1_copied.at(n - 1))
                for u in range(4):
                    cols = slice(u * P, (u + 1) * P)
                    last = nc.tensor.matmul(ps[:, n % 2, cols], LM[:, n % 2, cols], X[:, b, cols], start=True, stop=True)
                last.then_inc(*w1.up())
            if n >= 1:
                m = n - 1
                s, b = steps[m]
                e.wait_ge(*w1_copied.at(m + 1))
                if m >= 2:
                    e.wait_ge(*updated.at(m - 1))
                for u in range(4):
                    cols = slice(u * P, (u + 1) * P)
                    if s != levels[-1]:
                        nc.tensor.matmul(ps[:, 2 + m % 2, cols], XT[:, b, cols], W1[:, m % 2, cols], start=True, stop=True)
                for u in range(4):
                    cols = slice(u * P, (u + 1) * P)
                    last = nc.tensor.matmul(ps[:, 4 + m % 2, cols], W1[:, m % 2, cols], XT[:, b, cols], start=True, stop=True)
                last.then_inc(*prods.up())
    stage(core, pe=pe, act=act, dve=dve, pool=pool)


def recurrence(core, PB, PK, XT, AR, BN, KN, VN, PC, O, GS, US, S):
    nc, ps = core.nc, core.ps
    J = RW // P
    cleared, g_done, g_neg, u_done, u_copied, o_done, o_copied, s_done, s_new = (core.sig(f"state_{n}") for n in
        ("cleared", "g", "g_negated", "u", "u_copied", "o", "o_copied", "products", "new"))

    def split(c):
        return c // 2, CH * (c % 2)

    def pe(e):
        e.wait_ge(*cleared.at(3))
        for c in range(NCH):
            tt, pb = split(c)
            tok = slice(pb, pb + CH)
            if c:
                e.wait_ge(*s_new.at(c))
            for j in range(J):
                nc.tensor.matmul(ps[tok, 0, j * P:(j + 1) * P], AR[:, j, tt, 0, tok], S[:, j, :], start=True, stop=False)
                for hp in range(2):
                    u = 4 * j + 2 * tt + hp
                    h0 = j * P + 64 * hp
                    last = nc.tensor.matmul(ps[tok, 0, h0:h0 + 64], PK[:, u, pb:pb + CH], VN[:, tt, h0:h0 + 64],
                                            start=False, stop=(hp == 1))
            last.then_inc(*g_done.up())
            e.wait_ge(*g_neg.at(c + 1))
            for j in range(J):
                for hp in range(2):
                    u = 4 * j + 2 * tt + hp
                    h0 = j * P + 64 * hp
                    xt = XT[:, u // 4, (u % 4) * P + pb:(u % 4) * P + pb + CH]
                    last = nc.tensor.matmul(ps[tok, 1, h0:h0 + 64], xt, GS[:, h0:h0 + 64], start=True, stop=True)
            last.then_inc(*u_done.up())
            e.wait_ge(*u_copied.at(c + 1))
            if c >= 2:
                e.wait_ge(*o_copied.at(c - 1))
            ob, db = 2 + c % 2, 4 + c % 2
            for j in range(J):
                nc.tensor.matmul(ps[:, ob, j * CH:(j + 1) * CH], S[:, j, :], AR[:, j, tt, 1, tok], start=True, stop=False)
                for hp in range(2):
                    u = 4 * j + 2 * tt + hp
                    h0 = j * P + 64 * hp
                    out = ps[64 * hp:64 * hp + 64, ob, j * CH:(j + 1) * CH]
                    nc.tensor.matmul(out, US[:, h0:h0 + 64], PB[:, u, P + pb:P + pb + CH], start=False, stop=False)
                    last = nc.tensor.matmul(out, VN[:, tt, h0:h0 + 64], PK[:, u, P + pb:P + pb + CH],
                                            start=False, stop=True)
            last.then_inc(*o_done.up())
            if c < NCH - 1:
                for j in range(J):
                    cols = slice(j * P, (j + 1) * P)
                    nc.tensor.matmul(ps[:, db, cols], BN[tok, tt, cols], US[tok, cols], start=True, stop=False)
                    last = nc.tensor.matmul(ps[:, db, cols], KN[tok, tt, cols], VN[tok, tt, cols], start=False, stop=True)
                last.then_inc(*s_done.up())

    def act(e):
        e.wait_ge(*cleared.at(3))
        for c in range(NCH):
            tt, pb = split(c)
            tok = slice(pb, pb + CH)
            e.wait_ge(*g_done.at(c + 1))
            nc.scalar.activation(GS[tok, :], ps[tok, 0, :], ACT.Copy, scale=-1.0).then_inc(*g_neg.up())
            e.wait_ge(*u_done.at(c + 1))
            nc.scalar.activation(US[tok, :], ps[tok, 1, :], ACT.Copy).then_inc(*u_copied.up())
            e.wait_ge(*o_done.at(c + 1))
            nc.scalar.activation(O[:, :, tt * P + pb:tt * P + pb + CH],
                                 ps[:, 2 + c % 2, 0:J * CH].rearrange("p (j n) -> p j n", j=J), ACT.Copy)\
                .then_inc(*o_copied.up())

    def dve(e):
        nc.vector.memset(S, 0.0).then_inc(*cleared.up())
        nc.vector.memset(GS, 0.0).then_inc(*cleared.up())
        nc.vector.memset(US, 0.0).then_inc(*cleared.up())
        for c in range(NCH - 1):
            e.wait_ge(*s_done.at(c + 1))
            for hp in range(2):
                r = slice(64 * hp, 64 * hp + 64)
                own = S[r, :, 64 * hp:64 * hp + 64]
                new = ps[r, 4 + c % 2, :].rearrange("p (j n) -> p j n", j=J)[:, :, 64 * hp:64 * hp + 64]
                core.link(e, "dve", nc.vector.tensor_tensor(own, own, new, ALU.add))
                last = nc.vector.tensor_tensor(own, own, bc(PC[r, :, c], 2, 64), ALU.mult)
                if hp == 0:
                    core.link(e, "dve", last)
            last.then_inc(*s_new.up())
    stage(core, pe=pe, act=act, dve=dve)


def head_norm(core, O, BON, G, col, sq):
    nc, ps, c = core.nc, core.ps, core.c
    J = RW // P
    flat = lambda b: b.rearrange("p a t -> p (a t)")
    mean, squares, var, root = (core.sig(f"head_{n}") for n in ("mean", "squares", "variance", "root"))
    two = lambda b: ps[:, b:b + 2, :].rearrange("p b n -> p (b n)")

    def pe(e):
        for src, bank, s in ((O, 0, mean), (sq, 2, var)):
            if bank:
                e.wait_ge(*squares.at(1))
            for j in range(J):
                last = nc.tensor.matmul(ps[:, bank + j // 2, (j % 2) * T:(j % 2 + 1) * T], c("mean64"), src[:, j, :],
                                        start=True, stop=True)
            last.then_inc(*s.up())

    def act(e):
        e.wait_ge(*var.at(1))
        nc.scalar.activation(flat(sq), two(2), ACT.Sqrt, bias=c("eps")[:, E_GN:E_GN + 1]).then_inc(*root.up())

    def dve(e):
        e.wait_ge(*mean.at(1))
        core.link(e, "dve", nc.vector.tensor_tensor(flat(O), flat(O), two(0), ALU.subtract))
        nc.vector.tensor_tensor(flat(sq), flat(O), flat(O), ALU.mult).then_inc(*squares.up())
        e.wait_ge(*root.at(1))
        core.link(e, "dve", nc.vector.reciprocal(flat(sq), flat(sq)))
        core.link(e, "dve", nc.vector.tensor_tensor(flat(O), flat(O), flat(sq), ALU.mult))
        for j in range(J):
            last = nc.vector.tensor_scalar(O[:, j, :], O[:, j, :], col("rw_ln_w_2", j), col("rw_ln_b_2", j), ALU.mult, ALU.add)
        core.link(e, "dve", last)
        core.link(e, "dve", nc.vector.tensor_tensor(flat(O), flat(O), flat(BON), ALU.add))
        nc.vector.tensor_tensor(flat(O), flat(O), flat(G), ALU.mult)
    stage(core, pe=pe, act=act, dve=dve)


def s5(core, l0, col, UT, Y):
    nc, a, ps, c = core.nc, core.a, core.ps, core.c
    link = core.link
    f16 = lambda off: a(off, ST)
    COS, SIN = (a(off, ST * T).rearrange("p (s t) -> p s t", t=T) for off in (3072, 7168))
    b_re, b_im = (a(off, ST * SG).rearrange("p (s i) -> p s i", i=SG) for off in (11264, 11520))
    bd = [a(off, ST * 32).rearrange("p (s n) -> p s n", n=32) for off in (11776, 12288)]
    bdT = [a(off, 4 * P).rearrange("p (c n) -> p c n", c=4) for off in (12800, 13312)]
    cn = [a(off, 4 * 64).rearrange("p (c n) -> p c n", c=4) for off in (13824, 14080)]
    cpad = [a(off, 4 * P).rearrange("p (c g n) -> p c g n", c=4, g=2) for off in (14336, 14848)]
    cT = [a(off, 4 * P).rearrange("p (c n) -> p c n", c=4) for off in (15360, 15872, 16384)]
    W = 16896
    (dt, re, im, rho, n_, r_, h_, ah, sh, ch, co, si, t1, t2, nr, ni, den, cr, ci, qc, qs, qc2, qs2) = (
        f16(23552 + ST * i) for i in range(23))
    landed = core.sig("s5_landed")
    ex, ang, trig, made, turned = (core.sig(f"s5_{n}") for n in ("exps", "angles", "trig", "made", "turned"))

    def sp(e):
        for dst, name in ((b_re, "s5_b_re_2"), (b_im, "s5_b_im_2")):
            e.dma_start(dst, l0[name].rearrange("(s g) p i -> (g p) s i", g=2)).then_inc(*landed.up(16))
        for dst, name in ((cn[0], "s5_c_re_2"), (cn[1], "s5_c_im_2")):
            e.dma_start(dst, l0[name].rearrange("(c g) i p -> (g i) c p", g=8)).then_inc(*landed.up(16))

    def span(name):
        first = col(name, 0)
        return bass.AP(first.tensor, first.offset, [list(first.ap[0]), [1, ST]])
    lam_re, lam_im, log_dt = span("s5_lam_re_2"), span("s5_lam_im_2"), span("s5_log_dt_2")
    MAGIC = 1.5 * 2 ** 23
    PI_HI = float(np.float32(6.28125))
    PI_LO = 2 * math.pi - PI_HI

    def act(e):
        nc.scalar.activation(dt, log_dt, ACT.Exp).then_inc(*ex.up())
        e.wait_ge(*ang.at(1))
        nc.scalar.activation(rho, re, ACT.Exp).then_inc(*ex.up())
        e.wait_ge(*ang.at(2))
        nc.scalar.activation(sh, h_, ACT.Sin).then_inc(*trig.up())
        e.wait_ge(*ang.at(3))
        nc.scalar.activation(ch, ah, ACT.Sin, scale=-1.0, bias=c("eps")[:, E_HALFPI:E_HALFPI + 1]).then_inc(*trig.up())
        for i in range(2):
            e.wait_ge(*turned.at(i + 1))
            nc.scalar.activation(bdT[i].rearrange("p c n -> p (c n)"), ps[:, i, :], ACT.Copy)
        e.wait_ge(*turned.at(3))
        nc.scalar.activation(cT[0].rearrange("p c n -> p (c n)"), ps[:, 2, :], ACT.Copy)
        nc.scalar.activation(cT[2].rearrange("p c n -> p (c n)"), ps[:, 2, :], ACT.Copy, scale=-1.0)
        e.wait_ge(*turned.at(4))
        nc.scalar.activation(cT[1].rearrange("p c n -> p (c n)"), ps[:, 3, :], ACT.Copy, scale=-1.0)

    def pe(e):
        for i in range(2):
            e.wait_ge(*made.at(i + 1))
            for ct in range(4):
                last = nc.tensor.transpose(ps[:, i, ct * P:(ct + 1) * P],
                                           bd[i][:, 4 * ct:4 * ct + 4, :].rearrange("p s n -> p (s n)"), c("ident"))
            last.then_inc(*turned.up())
        for i in range(2):
            e.wait_ge(*made.at(i + 3))
            for ct in range(4):
                last = nc.tensor.transpose(ps[:, 2 + i, ct * P:(ct + 1) * P],
                                           cpad[i][:, ct, :, :].rearrange("p g n -> p (g n)"), c("ident"))
            last.then_inc(*turned.up())

    V = nc.vector
    tt_ = lambda e, o, x0, x1, op: link(e, "dve", V.tensor_tensor(o, x0, x1, op))
    ts_ = lambda e, o, x0, s1, s2, o0, o1=ALU.bypass: link(e, "dve", V.tensor_scalar(o, x0, s1, s2, o0, o1))

    def dve(e):
        e.wait_ge(*ex.at(1))
        V.tensor_tensor(re, lam_re, dt, ALU.mult).then_inc(*ang.up())
        tt_(e, im, lam_im, dt, ALU.mult)
        ts_(e, n_, im, 1 / (2 * math.pi), MAGIC, ALU.mult, ALU.add)
        ts_(e, n_, n_, MAGIC, None, ALU.subtract)
        link(e, "dve", V.scalar_tensor_tensor(r_, n_, -PI_HI, im, ALU.mult, ALU.add))
        link(e, "dve", V.scalar_tensor_tensor(r_, n_, -PI_LO, r_, ALU.mult, ALU.add))
        V.tensor_scalar(h_, r_, 0.5, None, ALU.mult).then_inc(*ang.up())
        e.wait_ge(*ang.at(2))
        link(e, "dve", V.tensor_scalar(ah, h_, -1.0, None, ALU.mult))
        V.tensor_tensor(ah, ah, h_, ALU.max).then_inc(*ang.up())
        e.wait_ge(*trig.at(2))
        tt_(e, si, sh, ch, ALU.mult)
        ts_(e, si, si, 2.0, None, ALU.mult)
        tt_(e, co, sh, sh, ALU.mult)
        ts_(e, co, co, -2.0, 1.0, ALU.mult, ALU.add)
        e.wait_ge(*ex.at(2))
        tt_(e, nr, rho, co, ALU.mult)
        ts_(e, nr, nr, -1.0, None, ALU.add)
        tt_(e, ni, rho, si, ALU.mult)
        tt_(e, t1, lam_re, lam_re, ALU.mult)
        tt_(e, t2, lam_im, lam_im, ALU.mult)
        tt_(e, den, t1, t2, ALU.add)
        link(e, "dve", V.reciprocal(den, den))
        tt_(e, t1, nr, lam_re, ALU.mult)
        tt_(e, t2, ni, lam_im, ALU.mult)
        tt_(e, cr, t1, t2, ALU.add)
        tt_(e, cr, cr, den, ALU.mult)
        tt_(e, t1, ni, lam_re, ALU.mult)
        tt_(e, t2, nr, lam_im, ALU.mult)
        tt_(e, ci, t1, t2, ALU.subtract)
        tt_(e, ci, ci, den, ALU.mult)
        e.wait_ge(*landed.at(64))
        w1, w2 = (a(W + i * 256, 256).rearrange("p (s i) -> p s i", i=SG) for i in range(2))
        wide = lambda v: bc(v, 2, SG)
        for i, (x1, x2, op) in enumerate(((b_re, b_im, ALU.subtract), (b_im, b_re, ALU.add))):
            link(e, "dve", V.memset(bd[i], 0.0))
            tt_(e, w1, x1, wide(cr), ALU.mult)
            tt_(e, w2, x2, wide(ci), ALU.mult)
            for g in range(2):
                r = slice(64 * g, 64 * g + 64)
                last = V.tensor_tensor(bd[i][r, :, SG * g:SG * g + SG], w1[r], w2[r], op)
                if g == 0:
                    link(e, "dve", last)
            last.then_inc(*made.up())
            e.wait_ge(*made.at(i + 1))
        for i in range(2):
            for g in range(2):
                last = V.tensor_scalar(cpad[i][:, :, g, :], cn[i], c("parity")[:, g:g + 1], None, ALU.mult)
                if g == 0:
                    link(e, "dve", last)
            last.then_inc(*made.up())
        tmp = [a(W + i * 2048, ST * 128) for i in range(2)]
        link(e, "dve", V.memset(COS[:, :, 0:1], 1.0))
        link(e, "dve", V.memset(SIN[:, :, 0:1], 0.0))
        q, q2 = (co, si), (qc, qs)
        n = 1
        while n < T:
            x1, x2 = (t[:, 0:ST * n].rearrange("p (s n) -> p s n", n=n) for t in tmp)
            qc_, qs_ = bc(q[0], 2, n), bc(q[1], 2, n)
            tt_(e, x1, COS[:, :, 0:n], qc_, ALU.mult)
            tt_(e, x2, SIN[:, :, 0:n], qs_, ALU.mult)
            tt_(e, COS[:, :, n:2 * n], x1, x2, ALU.subtract)
            tt_(e, x1, COS[:, :, 0:n], qs_, ALU.mult)
            tt_(e, x2, SIN[:, :, 0:n], qc_, ALU.mult)
            tt_(e, SIN[:, :, n:2 * n], x1, x2, ALU.add)
            tt_(e, t1, q[0], q[0], ALU.mult)
            tt_(e, t2, q[1], q[1], ALU.mult)
            tt_(e, q2[0], t1, t2, ALU.subtract)
            tt_(e, t1, q[0], q[1], ALU.mult)
            ts_(e, q2[1], t1, 2.0, None, ALU.mult)
            q, q2 = q2, ((qc2, qs2) if q2[0] is qc else (qc, qs))
            n *= 2
    stage(core, sp=sp, pe=pe, act=act, dve=dve)

    M1, M2, VV, ZZ = (a(W + i * 1024, 1024).rearrange("p (b n) -> p b n", b=2) for i in range(4))
    N1, N2 = (a(W + 4096 + i * 1024, 1024).rearrange("p (b n) -> p b n", b=2) for i in range(2))
    proj, rot, added, back, ysum, ypre = (core.sig(f"s5_{n}") for n in
                                          ("projected", "rotated", "summed", "back", "outputs", "with_skip"))

    def pe(e):
        for s in range(ST + 1):
            if s < ST:
                ct, j = s // 4, s % 4
                if s >= 4:
                    e.wait_ge(*rot.at(s - 3))
                rows = slice(32 * j, 32 * j + 32)
                for i in range(2):
                    last = nc.tensor.matmul(ps[:, j, i * T:(i + 1) * T], bdT[i][rows, ct, :], UT[rows, ct, :],
                                            start=True, stop=True)
                last.then_inc(*proj.up())
            if s >= 1:
                m = s - 1
                ct, j = m // 4, m % 4
                e.wait_ge(*back.at(m + 1))
                out = ps[32 * j:32 * j + 32, 4 + ct, 0:T]
                cols = slice(32 * j, 32 * j + 32)
                terms = ((cT[0], N1, 0), (cT[2], N2, 1), (cT[1], N1, 1), (cT[1], N2, 0))
                for k, (w_, src, part) in enumerate(terms):
                    last = nc.tensor.matmul(out, w_[:, ct, cols], src[:, m % 2, part * T:(part + 1) * T],
                                            start=(k == 0), stop=(k == 3))
                last.then_inc(*ysum.up())

    def pool(e):
        for s in range(ST):
            e.wait_ge(*rot.at(s + 1))
            if s >= 2:
                e.wait_ge(*back.at(s - 1))
            b = s % 2
            nc.gpsimd.tensor_tensor(VV[:, b, 0:T], M1[:, b, 0:T], M2[:, b, T:2 * T], ALU.add)
            nc.gpsimd.tensor_tensor(VV[:, b, T:2 * T], M1[:, b, T:2 * T], M2[:, b, 0:T], ALU.subtract).then_inc(*added.up())

    def dve(e):
        two = lambda v, s: bc(v[:, s, :], 1, 2)
        half = lambda v, b: v[:, b, :].rearrange("p (i t) -> p i t", i=2)
        for s in range(ST + 1):
            if s < ST:
                e.wait_ge(*proj.at(s + 1))
                if s >= 2:
                    e.wait_ge(*added.at(s - 1))
                pb = ps[:, s % 4, :].rearrange("p (i t) -> p i t", i=2)
                V.tensor_tensor(half(M1, s % 2), two(COS, s), pb, ALU.mult)
                V.tensor_tensor(half(M2, s % 2), two(SIN, s), pb, ALU.mult).then_inc(*rot.up())
            if s >= 1:
                m = s - 1
                b = m % 2
                e.wait_ge(*added.at(m + 1))
                decay = rho[:, m:m + 1].broadcast_to([P, T])
                V.tensor_tensor_scan(ZZ[:, b, 0:T], decay, VV[:, b, 0:T], 0.0, ALU.mult, ALU.add)
                link(e, "dve", V.tensor_tensor_scan(ZZ[:, b, T:2 * T], decay, VV[:, b, T:2 * T], 0.0, ALU.mult, ALU.add))
                if m >= 2:
                    e.wait_ge(*ysum.at(m - 1))
                V.tensor_tensor(half(N1, b), two(COS, m), half(ZZ, b), ALU.mult)
                V.tensor_tensor(half(N2, b), two(SIN, m), half(ZZ, b), ALU.mult).then_inc(*back.up())
        for ct in range(4):
            e.wait_ge(*ysum.at(4 * ct + 4))
            V.scalar_tensor_tensor(Y[:, ct, :], UT[:, ct, :], col("s5_d_2", ct), ps[:, 4 + ct, 0:T], ALU.mult, ALU.add)\
                .then_inc(*ypre.up())

    def act(e):
        for ct in range(4):
            e.wait_ge(*ypre.at(ct + 1))
            nc.scalar.activation(Y[:, ct, :], Y[:, ct, :], ACT.Gelu_apprx_tanh)
    stage(core, pe=pe, act=act, dve=dve, pool=pool)

    freed = core.sig("bank_copied")
    gate = a(W, 4 * T).rearrange("p (n t) -> p n t", t=T)

    def pe(e):
        features_matmul(core, e, 0, Y, 4, [RW], freed, 0, 4, core.taken)

    def act(e):
        for u in range(2):
            core.wait_bank(e, u)
            for h in range(2):
                j = 2 * u + h
                nc.scalar.activation(gate[:, j, :], ps[:, u, h * T:(h + 1) * T], ACT.Sigmoid, bias=col("s5_b_glu_2", j))\
                    .then_inc(*freed.up())

    def dve(e):
        core.wait_bank(e, 1)
        e.wait_ge(*freed.at(4))
        V.tensor_tensor(Y.rearrange("p a t -> p (a t)"), Y.rearrange("p a t -> p (a t)"),
                        gate.rearrange("p a t -> p (a t)"), ALU.mult)
    stage(core, pe=pe, act=act, dve=dve, uses=1)


def program(nc, w, consts, const_at, out):
    core = Core(nc, const_at)
    c, a, ps, x, xnT = core.c, core.a, core.ps, core.x, core.xnT
    sig, link = core.sig, core.link
    l0 = {k: (v[0] if v.shape[0] == 1 else v) for k, v in w.items() if len(v.shape) > 1}

    tiles = core.tiles
    tiles += col_chunks(l0["moba_w_qkv"]) + col_chunks(l0["moba_w_o"])
    tiles += col_chunks(w["mlp_w_up"][0]) + row_chunks(w["mlp_w_down"][0])
    tiles += col_chunks(l0["dsa_w_in"], 0, 512) + col_chunks(l0["dsa_w_in"], 512, 584)
    tiles += col_chunks(l0["dsa_w_uq"]) + col_chunks(l0["dsa_w_qi"]) + col_chunks(l0["dsa_w_o"])
    tiles += col_chunks(w["mlp_w_up"][1]) + row_chunks(w["mlp_w_down"][1])
    z_chunks = [(0, 512), (512, 1024), (1024, 1536), (1536, RWKV_COLS), (RWKV_COLS, RWKV_COLS + RW)]
    for c0, c1 in z_chunks:
        tiles += col_chunks(l0["hy_w_in_2"], c0, c1)
    tiles += col_chunks(l0["s5_w_glu_2"]) + col_chunks(l0["hy_w_out_2"])

    def xattn_tiles(l):
        return (col_chunks(w["xa_w_q_2"][l]) + col_chunks(w["xa_w_kv_2"][l]) + col_chunks(w["xa_w_o_2"][l]))

    tiles += xattn_tiles(0)
    gate_w, up_w = l0["ff_w_gate_2"], l0["ff_w_up_2"]
    for n0 in range(0, FF2, NW):
        n1 = min(n0 + NW, FF2)
        tiles += col_chunks(gate_w, n0, n1) + col_chunks(up_w, n0, n1)
    tiles += row_chunks(l0["ff_w_down_2"])
    tiles += col_chunks(l0["da_w_qkv_2"]) + col_chunks(l0["da_w_o_2"])
    tiles += xattn_tiles(1)

    col_at, loads = {}, []
    place = [0, 0]

    def vector(name, ap, which):
        n = ap.shape[0]
        full = n // P
        r = place[which]
        col_at[name] = (which, r)
        if full:
            loads.append((core.rows[r:r + full, which, :], ap[0:full * P].rearrange("(r p) -> r p", p=P)))
        if n % P:
            loads.append((core.rows[r + full:r + full + 1, which, 0:n % P], ap[full * P:n].rearrange("(r p) -> r p", r=1)))
        place[which] += full + (n % P > 0)

    for name in ("ln_attn", "ln_mlp", "norm_mix_2", "norm_xattn_2", "norm_mem_2", "norm_ffn_2"):
        vector(name, w[name].rearrange("l d -> (l d)"), 0)
    vector("dsa_g_q", l0["dsa_g_q"], 0)
    vector("dsa_g_kv", l0["dsa_g_kv"], 0)
    vector("xa_q_gain_2", w["xa_q_gain_2"].rearrange("l d -> (l d)"), 0)
    vector("xa_k_gain_2", w["xa_k_gain_2"].rearrange("l d -> (l d)"), 0)
    vector("da_sub_gain_2", l0["da_sub_gain_2"], 0)
    for name in ("rw_w0_2", "rw_a0_2", "rw_k_k_2", "rw_k_a_2"):
        vector(name, l0[name], 0)
    mu = l0["rw_mu_2"]
    vector("mu", mu[0:3 * RW + 128], 1)
    vector("mu_g", mu[3 * RW + 128:RWKV_COLS], 1)
    vector("rw_r_k_2", l0["rw_r_k_2"].rearrange("h d -> (h d)"), 1)
    for name in ("rw_ln_w_2", "rw_ln_b_2", "s5_d_2", "s5_b_glu_2"):
        vector(name, l0[name], 1)
    vector("s5_lam_re_2", l0["s5_lam_re_2"].rearrange("g p -> (g p)"), 1)
    vector("s5_lam_im_2", l0["s5_lam_im_2"].rearrange("g p -> (g p)"), 1)
    for name in ("da_q_gain_2", "da_k_gain_2"):
        r = place[1]
        col_at[name] = (1, r)
        for half in range(2):
            loads.append((core.rows[r:r + 1, 1, half * 64:(half + 1) * 64], w[name]))
        place[1] += 1
    col_at["s5_log_dt_2"] = (1, 96)
    assert place[0] <= P and place[1] <= 96

    def col(name, k=0):
        which, r = col_at[name]
        return core.cols[:, which, r + k:r + k + 1]

    def at_col(name, k=0):
        which, r = col_at[name]
        return (which, r + k)

    lam_sb = nc.alloc_sbuf_tensor("lam", [P, 4, 64], F32)
    dt_rows = nc.alloc_sbuf_tensor("dt_rows", [P, 2], F32)
    relb = nc.alloc_sbuf_tensor("relb", [NBUCKET, H], F32)
    small = nc.alloc_sbuf_tensor("small", [P, 96], F32)
    toep = nc.alloc_sbuf_tensor("toep", [P, H, T], F32)
    ext_dram = nc.dram_tensor("bias_rows", [H, P, CAUS], F32, kind="Internal").ap()
    BIAS_SB = 22000
    ext_sb = a(BIAS_SB, CAUS)

    def dve(e):
        nc.vector.memset(core.rows[:, :, :], 0.0)
    stage(core, dve=dve)

    ready = sig("inputs_landed")

    def sp(e):
        e.dma_start(core.const[:, :], consts).then_inc(*ready.up(16))
        e.dma_start(x[:, :, :], w["x"][0].rearrange("(t p) d -> p t d", p=P)).then_inc(*ready.up(16))
        e.dma_start(relb[:, :], w["rel_bias"]).then_inc(*ready.up(16))
        for i, name in enumerate(("da_lam_q1_2", "da_lam_k1_2", "da_lam_q2_2", "da_lam_k2_2")):
            e.dma_start(lam_sb[:, i, :], w[name][0].partition_broadcast(P)).then_inc(*ready.up(16))
        e.dma_start(dt_rows[0:16, :], l0["s5_log_dt_2"].rearrange("(r g) -> r g", g=2)).then_inc(*ready.up(16))
        for dst, src in loads:
            e.dma_start(dst, src).then_inc(*ready.up(16))
        core.issue(e, RING)
        e.wait_ge(ready.sem, ready.total)
    stage(core, sp=sp)

    turned, extd, dt_ok = sig("params_turned"), sig("bias_rows_ready"), sig("dt_spread")
    bias_written, bias_read = sig("bias_rows_written"), sig("bias_landed")
    dt_wide = a(BIAS_SB + 1024, P).rearrange("p (g s) -> p g s", g=2)

    def pe(e):
        nc.tensor.matmul(ps[0:H, 0, 0:CAUS], relb[:, :], c("onehot")[0:NBUCKET, :], start=True, stop=True)\
            .then_inc(*turned.up())
        nc.tensor.transpose(ps[:, 1, 0:P], core.rows[:, 0, :], c("ident")).then_inc(*turned.up())
        nc.tensor.transpose(ps[:, 2, 0:P], core.rows[:, 1, :], c("ident")).then_inc(*turned.up())
        e.wait_ge(*dt_ok.at(1))
        nc.tensor.transpose(ps[:, 3, 0:16], dt_wide[0:16, :, :].rearrange("p g s -> p (g s)"),
                            c("ident")[0:16, 0:16]).then_inc(*turned.up())

    def dve(e):
        nc.vector.tensor_copy(dt_wide[0:16, :, :], bc(dt_rows[0:16, :], 2, 64)).then_inc(*dt_ok.up())
        e.wait_ge(*turned.at(1))
        nc.vector.tensor_tensor(ext_sb[0:H, :], ps[0:H, 0, 0:CAUS], c("future")[0:H, :], ALU.add)\
            .then_inc(*extd.up())
        e.wait_ge(*turned.at(2))
        nc.vector.tensor_copy(core.cols[:, 0, :], ps[:, 1, 0:P])
        e.wait_ge(*turned.at(3))
        nc.vector.tensor_copy(core.cols[:, 1, 0:96], ps[:, 2, 0:96])
        e.wait_ge(*turned.at(4))
        nc.vector.tensor_copy(core.cols[:, 1, 96:112], ps[:, 3, 0:16])

    def sp(e):
        e.wait_ge(*extd.at(1))
        e.dma_start(ext_dram.rearrange("h r n -> h r n"), bc(ext_sb[0:H, :], 1, P)).then_inc(*bias_written.up(16))
    stage(core, sp=sp, pe=pe, dve=dve)

    def read_bias(e):
        e.wait_ge(*bias_written.at(0))
        skew = bass.AP(ext_dram.tensor, ext_dram.offset + P - 1, [[CAUS - 1, P], [P * CAUS, H], [1, T]])
        e.dma_start(toep[:, :, :], skew).then_inc(*bias_read.up(16))

    freed = sig("bank_copied")

    QT, KT_, VN, OT, SCR = 0, 2048, 4096, 6144, 8192

    def view(off, n):
        return a(off, n * T).rearrange("p (n t) -> p n t", t=T)

    def copy_bank(e, eng, dst, bank, scale=None):
        src = ps[:, bank, :]
        if eng == "act":
            return nc.scalar.activation(dst, src, ACT.Copy, scale=1.0 if scale is None else scale)
        return nc.vector.tensor_scalar(dst, src, 1.0 if scale is None else scale, None, ALU.mult)

    def pairs(buf, u):
        return buf[:, 2 * u:2 * u + 2, :].rearrange("p a t -> p (a t)")

    def rows64(buf):
        return lambda u: buf[64 * (u % 2):64 * (u % 2) + 64, u // 2, :]

    def first_attention(before_dve_bias, sel=None):
        qT, kT, oT = view(QT, 8), view(KT_, 8), view(OT, 8)
        vN = a(VN, 2 * D).rearrange("p (t d) -> p t d", t=TT)
        q, k = rows64(qT), rows64(kT)
        masked = sig("bias_masked")
        tmp = a(12500, 2 * CAUS).rearrange("p (b n) -> p b n", b=2)

        def bias(e, u):
            if u == 0 and before_dve_bias:
                e.wait_ge(*bias_read.at(0))
            if sel is None:
                return toep[:, u, P:T], toep[:, u, :]
            e.wait_ge(*masked.at(u + 1))
            return tmp[:, u % 2, 0:P], tmp[:, u % 2, P:CAUS]

        pe, act, dve = attention(core, H, 1, lambda u, tt: [q(u)[:, tt * P:(tt + 1) * P]],
                                 lambda u, n: [k(u)[:, 0:n]], lambda h: h * DH, DH, True, bias, vN, oT, SCR)

        def pool(e):
            for u in range(H):
                if u >= 2:
                    e.wait_ge(*sig("attn_negmax").at(u - 1))
                nc.gpsimd.tensor_tensor(tmp[:, u % 2, 0:P], toep[:, u, P:T], sel[:, 0:P], ALU.add)
                nc.gpsimd.tensor_tensor(tmp[:, u % 2, P:CAUS], toep[:, u, :], sel[:, P:CAUS], ALU.add)\
                    .then_inc(*masked.up())
        stage(core, pe=pe, act=act, dve=dve, pool=pool if sel is not None else None)

    def project_to_x(srcT, kt=8):
        def pe(e):
            tokens_matmul(core, e, 0, srcT, kt, [NW] * 2, freed, 0, 4, core.taken)

        def dve(e):
            for u in range(4):
                core.wait_bank(e, u)
                xs = x[:, u % 2, (u // 2) * NW:(u // 2 + 1) * NW]
                nc.vector.tensor_tensor(xs, xs, ps[:, u, :], ALU.add)
        stage(core, pe=pe, dve=dve, uses=2 * -(-kt // KW))

    def squared_relu_mlp():
        hT = view(0, DFF // P)
        tmp = a(8192, 4 * 512).rearrange("p (b n) -> p b n", b=4)
        relud = sig("relu_done")
        n = DFF // (2 * P)

        def pe(e):
            _, tile = features_matmul(core, e, 0, xnT, KD, [NW] * (DFF // NW), freed, 0, 4, core.taken)
            e.wait_ge(*freed.at(n))
            down_matmul(core, e, hT, DFF // P, 4, tile)

        def act(e):
            for u in range(n):
                core.wait_bank(e, u)
                if u >= 4:
                    e.wait_ge(*freed.at(u - 3))
                nc.scalar.activation(tmp[:, u % 4, :], ps[:, u % 4, :], ACT.Relu).then_inc(*relud.up())

        def dve(e):
            for u in range(n):
                e.wait_ge(*relud.at(u + 1))
                nc.vector.scalar_tensor_tensor(pairs(hT, u), ps[:, u % 4, :], 0.0, tmp[:, u % 4, :],
                                               ALU.max, ALU.mult).then_inc(*freed.up())
            add_to_x(core, e, n, 4)
        stage(core, pe=pe, act=act, dve=dve, uses=2 * (DFF // NW) + 2 * (DFF // P // KW))

    norm_stage(core, x, xnT, at_col("ln_attn"), 0, extra_sp=read_bias)

    def qkv_stage(nq, q_scale):
        qk = view(QT, 16)
        vN = a(VN, 2 * D).rearrange("p (t d) -> p t d", t=TT)
        nu = 8

        def pe(e):
            u, tile = features_matmul(core, e, 0, xnT, KD, [NW] * 4, freed, 0, 4, core.taken)
            tokens_matmul(core, e, 0, xnT, KD, [NW] * 2, freed, 4, 4, tile)

        def act(e):
            for u in range(nu):
                core.wait_bank(e, u)
                copy_bank(e, "act", pairs(qk, u), u % 4, q_scale if u < 4 else None).then_inc(*freed.up())
            for u in range(4):
                core.wait_bank(e, nu + u)
                copy_bank(e, "act", vN[:, u % 2, (u // 2) * NW:(u // 2 + 1) * NW], 4 + u)
        stage(core, pe=pe, act=act, uses=12)

    qkv_stage(8, DH ** -0.5)
    first_attention(True)
    project_to_x(view(OT, 8))
    norm_stage(core, x, xnT, at_col("ln_mlp"), 0)
    squared_relu_mlp()

    UK, UV, CQ, QI, KI, WI, SEL = 13400, 15448, 17496, 18520, 19544, 19800, 19840
    uk_n = a(UK, 8 * 256).rearrange("p (r c) -> p r c", r=8)
    uv = a(UV, 2 * D).rearrange("p (k h d) -> p k h d", k=2, h=H)
    lat_landed = sig("latent_weights_landed")

    def sp(e):
        e.dma_start(uk_n, l0["dsa_w_uk"].rearrange("(r a) d c -> (a d) r c", a=2)).then_inc(*lat_landed.up(16))
        for k in range(2):
            e.dma_start(uv[:, k, :, :], l0["dsa_w_uv"][:, k * P:(k + 1) * P, :].rearrange("h c d -> c h d"))\
                .then_inc(*lat_landed.up(16))
    norm_stage(core, x, xnT, at_col("ln_attn", 8), 0, extra_sp=sp)

    cqkv = view(CQ, 4)
    kiT = view(KI, 1)[:, 0, :]
    wi = a(WI, 2 * IDXH).rearrange("p (t h) -> p t h", t=TT)

    def pe(e):
        u, tile = features_matmul(core, e, 0, xnT, KD, [512], freed, 0, 4, core.taken)
        for j in range(2):
            core.wait_tile(e, tile + j)
        for half in range(2):
            for k in range(KD):
                last = nc.tensor.matmul(ps[64 * half:64 * half + 64, 2, 0:T], core.slot(tile + k // KW, KW, 72)[:, k % KW, 0:64],
                                        xnT[:, k, :], start=(k == 0), stop=(k == KD - 1))
        core.fill(last, bank=True)
        for tt in range(TT):
            for k in range(KD):
                last = nc.tensor.matmul(ps[:, 3, tt * 8:tt * 8 + 8], xnT[:, k, tt * P:(tt + 1) * P],
                                        core.slot(tile + k // KW, KW, 72)[:, k % KW, 64:72],
                                        start=(k == 0), stop=(k == KD - 1))
        core.fill(last, bank=True, slots=2)

    def act(e):
        for u in range(2):
            core.wait_bank(e, u)
            copy_bank(e, "act", pairs(cqkv, u), u)
        core.wait_bank(e, 2)
        nc.scalar.activation(kiT, ps[:, 2, 0:T], ACT.Copy)
        core.wait_bank(e, 3)
        nc.scalar.activation(wi.rearrange("p t h -> p (t h)"), ps[:, 3, 0:16], ACT.Copy,
                             scale=IDXH ** -0.5 * 64 ** -0.5)
    stage(core, pe=pe, act=act, uses=4)

    sq = a(0, 1024).rearrange("p (b n) -> p b n", b=2)
    root = a(1024, 1024).rearrange("p (b n) -> p b n", b=2)
    gpe, gact, gdve = grouped_norm(core, cqkv, 4, c("mean256"), 2, 1.0, E_EPS,
                                   lambda j: col("dsa_g_q", j) if j < 2 else col("dsa_g_kv", j - 2), sq, root)
    ukT = a(2048 + 8192, 2 * D).rearrange("p (k n) -> p k n", k=2)
    uk_turned = sig("uk_turned")

    def pe(e):
        gpe(e)
        e.wait_ge(*lat_landed.at(0))
        for k in range(2):
            for b in range(2):
                for j in range(4):
                    r = 4 * b + j
                    last = nc.tensor.transpose(ps[:, 4 + 2 * k + b, j * P:(j + 1) * P], uk_n[:, r, k * P:(k + 1) * P],
                                               c("ident"))
                last.then_inc(*uk_turned.up())

    def act(e):
        gact(e)
        for k in range(2):
            for b in range(2):
                e.wait_ge(*uk_turned.at(2 * k + b + 1))
                nc.scalar.activation(ukT[:, k, b * 512:(b + 1) * 512], ps[:, 4 + 2 * k + b, :], ACT.Copy)
    stage(core, pe=pe, act=act, dve=gdve)

    qT, kT = view(QT, 8), view(KT_, 8)
    vN = a(VN, 2 * D).rearrange("p (t d) -> p t d", t=TT)
    qiT = view(QI, 4)

    def pe(e):
        cq, ckv = cqkv[:, 0:2, :], cqkv[:, 2:4, :]
        u, tile = features_matmul(core, e, 0, cq, 2, [NW] * 3, freed, 0, 8, core.taken)
        for b in range(4):
            if u >= 8:
                e.wait_ge(*freed.at(u - 7))
            for j in range(2):
                for k in range(2):
                    last = nc.tensor.matmul(ps[:, u % 8, j * T:(j + 1) * T], ukT[:, k, (2 * b + j) * P:(2 * b + j + 1) * P],
                                            ckv[:, k, :], start=(k == 0), stop=(k == 1))
            core.fill(last, bank=True)
            u += 1
        for half in range(2):
            for tt in range(TT):
                e.wait_ge(*freed.at(u - 7))
                for k in range(2):
                    last = nc.tensor.matmul(ps[:, u % 8, :], ckv[:, k, tt * P:(tt + 1) * P],
                                            uv[:, k, half * 8:half * 8 + 8, :].rearrange("p h d -> p (h d)"),
                                            start=(k == 0), stop=(k == 1))
                core.fill(last, bank=True)
                u += 1

    def act(e):
        for u in range(14):
            core.wait_bank(e, u)
            if u < 4:
                dst, s = pairs(qT, u), DH ** -0.5
            elif u < 6:
                dst, s = pairs(qiT, u - 4), None
            elif u < 10:
                dst, s = pairs(kT, u - 6), None
            else:
                dst, s = vN[:, u % 2, ((u - 10) // 2) * NW:((u - 10) // 2 + 1) * NW], None
            copy_bank(e, "act", dst, u % 8, s).then_inc(*freed.up())
    stage(core, pe=pe, act=act, uses=3)

    score = a(8192, CAUS)
    work = a(8192 + CAUS, CAUS)
    relu = a(9216, 4 * T).rearrange("p (b n) -> p b n", b=4)
    best = a(10300, 16).rearrange("p (t n) -> p t n", t=2)
    sel = a(SEL, CAUS)
    spans = [(0, P), (P, T)]

    def pe(e):
        qi = rows64(qiT)
        for u in range(2 * IDXH):
            tt, h = u // IDXH, u % IDXH
            b0 = 64 * (h % 2)
            if u >= 4:
                e.wait_ge(*sig("relu_done").at(u - 3))
            nc.tensor.matmul(ps[:, u % 4, 0:spans[tt][1]], qi(h)[:, tt * P:(tt + 1) * P], kiT[b0:b0 + 64, 0:spans[tt][1]],
                             start=True, stop=True).then_inc(*sig("index_scores").up())

    def act(e):
        for u in range(2 * IDXH):
            e.wait_ge(*sig("index_scores").at(u + 1))
            if u >= 4:
                e.wait_ge(*sig("index_added").at(u - 3))
            n = spans[u // IDXH][1]
            nc.scalar.activation(relu[:, u % 4, 0:n], ps[:, u % 4, 0:n], ACT.Relu).then_inc(*sig("relu_done").up())

    def dve(e):
        added = sig("index_added")
        for u in range(2 * IDXH):
            tt, h = u // IDXH, u % IDXH
            lo, n = spans[tt]
            e.wait_ge(*sig("relu_done").at(u + 1))
            if h == 0:
                nc.vector.tensor_scalar(score[:, lo:lo + n], relu[:, u % 4, 0:n], wi[:, tt, h:h + 1], None, ALU.mult)\
                    .then_inc(*added.up())
            else:
                e.wait_ge(*added.at(u))
                nc.vector.scalar_tensor_tensor(score[:, lo:lo + n], relu[:, u % 4, 0:n], wi[:, tt, h:h + 1],
                                               score[:, lo:lo + n], ALU.mult, ALU.add).then_inc(*added.up())
        e.wait_ge(*added.at(2 * IDXH))
        link(e, "dve", nc.vector.tensor_tensor(score, score, c("seen"), ALU.mult))
        link(e, "dve", nc.vector.tensor_tensor(score, score, c("unseen"), ALU.add))
        src, dst = score, work
        for r in range(TOPK // 8):
            for tt in range(TT):
                lo, n = spans[tt]
                last = nc.vector.max(best[:, tt, :], src[:, lo:lo + n])
            link(e, "dve", last)
            for tt in range(TT):
                lo, n = spans[tt]
                last = nc.vector.match_replace(dst[:, lo:lo + n], best[:, tt, :], src[:, lo:lo + n], TAKEN)
            link(e, "dve", last)
            src, dst = dst, src
        nc.vector.tensor_scalar(sel, src, TAKEN, NEG, ALU.not_equal, ALU.mult)
    stage(core, pe=pe, act=act, dve=dve)

    first_attention(False, sel=sel)
    project_to_x(view(OT, 8))
    norm_stage(core, x, xnT, at_col("ln_mlp", 8), 0)
    squared_relu_mlp()

    gain_landed = sig("final_gain_landed")
    gain = a(0, D)

    def sp(e):
        e.dma_start(gain, w["final_norm"].partition_broadcast(P)).then_inc(*gain_landed.up(16))

    def act(e):
        for tt in range(TT):
            nc.scalar.activation(a(1024 * (1 + tt), D), x[:, tt, :], ACT.Square, accum_out=core.stat[:, tt:tt + 1])\
                .then_inc(*sig("norm_sums").up())
        e.wait_ge(*sig("norm_sums").at(2))
        nc.scalar.activation(core.stat[:, 2:4], core.stat[:, 0:2], ACT.Sqrt, scale=1.0 / D,
                             bias=c("eps")[:, E_EPS:E_EPS + 1]).then_inc(*sig("norm_root").up())

    def dve(e):
        e.wait_ge(*sig("norm_root").at(1))
        link(e, "dve", nc.vector.reciprocal(core.stat[:, 4:6], core.stat[:, 2:4]))
        e.wait_ge(gain_landed.sem, 16)
        for tt in range(TT):
            nc.vector.scalar_tensor_tensor(x[:, tt, :], x[:, tt, :], core.stat[:, 4 + tt:5 + tt], gain,
                                           ALU.mult, ALU.mult)
    stage(core, sp=sp, act=act, dve=dve)

    rwkv_s5(core, w, l0, col, at_col, small)

    memT_off = 16000
    cross_attention(core, w, 0, at_col, project_to_x, memT_off)
    norm_stage(core, x, xnT, at_col("norm_ffn_2"), 0)
    swiglu(core)

    norm_stage(core, x, xnT, at_col("norm_mix_2", 8), 0)
    qkv_stage(8, None)
    qk = view(QT, 16)
    sq = a(SCR, 1024).rearrange("p (b n) -> p b n", b=2)
    root = a(SCR + 1024, 1024).rearrange("p (b n) -> p b n", b=2)
    qpe, qact, qdve = grouped_norm(core, qk[:, 0:8, :], 8, c("mean64"), 1, 64.0, E_EPS64,
                                   lambda j: col("da_q_gain_2"), sq, root)

    def pool(e):
        for h in range(8):
            nc.gpsimd.tensor_scalar(toep[:, :, :].rearrange("p h t -> p (h t)")[:, h * CAUS:(h + 1) * CAUS],
                                    c("alibi"), 2.0 ** -(h + 1), None, ALU.mult).then_inc(*sig("alibi_made").up())

    def sp(e):
        e.wait_ge(*sig("alibi_made").at(8))
    stage(core, sp=sp, pe=qpe, act=qact, dve=qdve, pool=pool)
    kpe, kact, kdve = grouped_norm(core, qk[:, 8:16, :], 8, c("mean64"), 1, 1.0, E_EPS,
                                   lambda j: col("da_k_gain_2"), sq, root)
    stage(core, pe=kpe, act=kact, dve=kdve)

    lam_sums, lam_exp = sig("lambda_sums"), sig("lambda_exp")
    lam_neg = small[:, 90:91]

    def dve(e):
        for i in range(2):
            last = nc.vector.tensor_tensor_reduce(out=a(SCR, 64) if i == 0 else a(SCR + 64, 64), in0=lam_sb[:, 2 * i, :],
                                                  in1=lam_sb[:, 2 * i + 1, :], scale=1.0, scalar=0.0, op0=ALU.mult,
                                                  op1=ALU.add, accum_out=small[:, 80 + i:81 + i])
            last.then_inc(*lam_sums.up())
        e.wait_ge(*lam_exp.at(1))
        link(e, "dve", nc.vector.tensor_tensor(small[:, 84:85], small[:, 83:84], small[:, 82:83], ALU.subtract))
        nc.vector.tensor_scalar(lam_neg, small[:, 84:85], -LAMBDA_INIT, None, ALU.add)

    def act(e):
        e.wait_ge(*lam_sums.at(2))
        nc.scalar.activation(small[:, 82:84], small[:, 80:82], ACT.Exp).then_inc(*lam_exp.up())
    stage(core, act=act, dve=dve)

    alibi = toep[:, :, :].rearrange("p h t -> p (h t)")
    oT = view(OT, 8)
    q, k = qk[:, 0:8, :], qk[:, 8:16, :]

    def bias(e, u):
        h = u // 2
        return alibi[:, h * CAUS:h * CAUS + P], alibi[:, h * CAUS + P:(h + 1) * CAUS]
    pe, act, dve = attention(core, 8, 2, lambda u, tt: [q[64 * (u % 2):64 * (u % 2) + 64, u // 2, tt * P:(tt + 1) * P]],
                             lambda u, n: [k[64 * (u % 2):64 * (u % 2) + 64, u // 2, 0:n]], lambda h: h * P, P, True,
                             bias, vN, oT, SCR, lam=lam_neg)
    stage(core, pe=pe, act=act, dve=dve)
    s2 = 1.0 / (1.0 - LAMBDA_INIT) ** 2
    ope, oact, odve = grouped_norm(core, oT, 8, c("mean128"), 1, s2, E_SUB, lambda j: col("da_sub_gain_2"), sq, root)
    stage(core, pe=ope, act=oact, dve=odve)
    project_to_x(oT)
    cross_attention(core, w, 1, at_col, project_to_x, memT_off)
    norm_stage(core, x, xnT, at_col("norm_ffn_2", 8), 0)
    mixture(core, w, l0, small)

    stored = sig("output_stored")

    def sp(e):
        e.dma_start(out[0].rearrange("(t p) d -> p t d", p=P), x[:, :, :]).then_inc(*stored.up(16))
        e.wait_ge(stored.sem, 16)
    stage(core, sp=sp)


_INS = ["x", "rel_bias", "ln_attn", "ln_mlp", "moba_w_qkv", "moba_w_o", "dsa_w_in", "dsa_g_q", "dsa_g_kv",
        "dsa_w_uq", "dsa_w_qi", "dsa_w_uk", "dsa_w_uv", "dsa_w_o", "mlp_w_up", "mlp_w_down", "final_norm",
        "mem_2", "norm_mix_2", "norm_xattn_2", "norm_mem_2", "norm_ffn_2", "xa_w_q_2", "xa_w_kv_2",
        "xa_q_gain_2", "xa_k_gain_2", "xa_w_o_2", "hy_w_in_2", "rw_mu_2", "rw_w0_2", "rw_w_up_2", "rw_a0_2",
        "rw_a_up_2", "rw_g_up_2", "rw_k_k_2", "rw_k_a_2", "rw_r_k_2", "rw_ln_w_2", "rw_ln_b_2",
        "s5_lam_re_2", "s5_lam_im_2", "s5_log_dt_2", "s5_b_re_2", "s5_b_im_2", "s5_c_re_2", "s5_c_im_2",
        "s5_d_2", "s5_w_glu_2", "s5_b_glu_2", "hy_w_out_2", "ff_w_gate_2", "ff_w_up_2", "ff_w_down_2",
        "da_w_qkv_2", "da_q_gain_2", "da_k_gain_2", "da_lam_q1_2", "da_lam_k1_2", "da_lam_q2_2",
        "da_lam_k2_2", "da_sub_gain_2", "da_w_o_2", "moe_w_router_2", "moe_b_router_2", "moe_w_gate_2",
        "moe_w_up_2", "moe_w_down_2"]


def kernel(**inputs):
    import concourse.bacc as bacc
    from concourse.bass_utils import run_bass_kernel_spmd

    nc = bacc.Bacc("TRN2", target_bir_lowering=False, num_devices=1)
    consts, const_at = constants()
    arrays = {name: np.ascontiguousarray(inputs[name]) for name in _INS}
    arrays["constants"] = consts
    aps = {name: nc.dram_tensor(name, a.shape, mybir.dt.from_np(a.dtype), kind="ExternalInput").ap()
           for name, a in arrays.items()}
    out = nc.dram_tensor("out", (1, T, D), F32, kind="ExternalOutput").ap()
    c = aps.pop("constants")
    program(nc, aps, c, const_at, out)
    r = run_bass_kernel_spmd(nc, [arrays], core_ids=[0])
    return r.results[0]["out"]
```

```python
import math

import numpy as np

import concourse.bass as bass
from concourse import mybir

F32 = mybir.dt.float32
F32R = mybir.dt.float32r
I32 = mybir.dt.int32
U32 = mybir.dt.uint32
ALU = mybir.AluOpType
ACT = mybir.ActivationFunctionType
AXX = mybir.AxisListType.X

P = 128
T = 256
TT = T // P
D = 1024
KD = D // P
H = 16
DH = 64
DFF = 4096
EPS = 1e-6
NEG = -1e30
TAKEN = -3e38
NBUCKET = 32
MAXDIST = 128
TOPK = 64
IDXH = 8
LORA = 256
CH = 64
NCH = T // CH
RW = 512
RWKV_COLS = 3 * RW + 64 + 64 + 160
SG = 16
SP_ = 64
ST = RW // SG * SP_ // P
FF2 = 2816
NE = 8
FE = 3584
GN_EPS = 1e-5 * 64
ARENA = 12544
LAMBDA_INIT = 0.8 - 0.6 * math.exp(-0.3)

RING = 6
WS_BUFS = 2
PASSES = ((0, 0), (0, 1), (1, 0))
SLOT = 2048
NW = 512
NF = 2 * P
CAUS = P + T


def _bucket(d):
    n = np.maximum(d, 0)
    exact = NBUCKET // 2
    nf = np.maximum(n, 1).astype(np.float32)
    large = exact + (np.log(nf / np.float32(exact)) / np.float32(math.log(MAXDIST / exact))
                     * np.float32(NBUCKET - exact)).astype(np.int32)
    return np.where(n < exact, n, np.minimum(large, NBUCKET - 1))


def constants():
    parts = {}
    eye = np.eye(P)
    i = np.arange(P)
    parts["ident"] = eye
    half = i // 64
    parts["mean64"] = (half[:, None] == half[None, :]) / 64.0
    parts["sum64"] = (half[:, None] == half[None, :]) * 1.0
    parts["mean128"] = np.full((P, P), 1 / 128)
    parts["mean256"] = np.full((P, P), 1 / 256)
    same = (i[:, None] // CH) == (i[None, :] // CH)
    parts["strict"] = (same & (i[:, None] < i[None, :])) * 1.0
    parts["upto"] = (same & (i[:, None] <= i[None, :])) * 1.0
    for s in (1, 2, 4, 8, 16, 32):
        parts[f"level{s}"] = ((i[:, None] // (2 * s) == i[None, :] // (2 * s))
                              & (i[:, None] % (2 * s) < s) & (i[None, :] % (2 * s) >= s)) * 1.0
    t = np.arange(T)
    parts["carry"] = np.broadcast_to((t % CH != 0) * 1.0, (P, T))
    parts["earlier"] = (i[:, None] < i[None, :]) * 1.0
    parts["ones"] = np.ones((P, P))
    parts["iota128"] = np.broadcast_to(np.arange(128.0), (P, P))
    dist = np.concatenate([i[:, None] - np.arange(P)[None, :], P + i[:, None] - np.arange(T)[None, :]], 1)
    parts["seen"] = (dist >= 0) * 1.0
    parts["unseen"] = np.where(dist >= 0, 0.0, NEG)
    q = np.concatenate([np.repeat(i[:, None], P, 1), np.repeat(P + i[:, None], T, 1)], 1)
    k = q - dist
    parts["alibi"] = np.where(k // 64 <= q // 64, -np.abs(dist), -1e33)
    j = np.arange(CAUS)
    d = T - 1 - j
    onehot = np.zeros((P, CAUS))
    onehot[_bucket(d), j] = 1.0
    parts["onehot"] = onehot
    parts["future"] = np.broadcast_to(np.where(d >= 0, 0.0, NEG), (P, CAUS))
    parts["iota8"] = np.broadcast_to(np.arange(8.0), (P, 8))
    parts["parity"] = np.stack([(i // SG) % 2 == 0, (i // SG) % 2 == 1], 1) * 1.0
    eps = [EPS, 64 * EPS, 256 * EPS, EPS / (1 - LAMBDA_INIT) ** 2, GN_EPS, math.pi / 2, 0.0, 1.0]
    parts["eps"] = np.broadcast_to(np.array(eps), (P, 8))
    at, n = {}, 0
    for name, a in parts.items():
        at[name] = (n, a.shape[1])
        n += a.shape[1]
    return np.ascontiguousarray(np.concatenate(list(parts.values()), 1).astype(np.float32)), at


E_EPS, E_EPS64, E_EPS256, E_SUB, E_GN, E_HALFPI = range(6)


class Signal:

    def __init__(self, nc, name):
        self.sem = nc.alloc_semaphore(name)
        self.base = self.total = 0

    def up(self, by=1):
        self.total += by
        return self.sem, by

    def at(self, n):
        return self.sem, self.base + n

    def close(self):
        self.base = self.total


class Core:

    def __init__(self, nc, const_at):
        self.nc = nc
        self.const_at = const_at
        self.signals = {}
        sb = lambda name, shape: nc.alloc_sbuf_tensor(name, shape, F32)
        self.ring = sb("ring", [P, RING, SLOT])
        self.x = sb("residual", [P, TT, D])
        self.XS = nc.alloc_sbuf_tensor("normed_split", [P, 2, KD, T], F32R)
        self.const = sb("const", [P, sum(n for _, n in const_at.values())])
        self.rows = sb("rows", [P, 2, P])
        self.cols = sb("cols", [P, 2, P])
        self.stat = sb("stat", [P, 8])
        self.arena = sb("arena", [P, ARENA])
        self.arena2 = None
        self.WS = None
        self.ps = nc.alloc_psum_tensor("ps", [P, 8, 512], F32)
        self.landed = [self.sig(f"weights_landed{i}") for i in range(RING)]
        self.hi_done, self.lo_done = self.sig("weights_high"), self.sig("weights_split")
        self.filled = self.sig("products")
        self.bank_full = []
        self.tile_used = []
        self.tiles = []
        self.issued = self.taken = self.hi_next = self.lo_next = 0
        self.names = 0
        self.chains = {e: self.sig(f"{e}_step") for e in ("pe", "act", "dve", "pool")}

    def sig(self, name):
        if name not in self.signals:
            self.signals[name] = Signal(self.nc, name)
        return self.signals[name]

    def c(self, name):
        at, n = self.const_at[name]
        return self.const[:, at:at + n]

    def a(self, off, n):
        if off >= ARENA:
            return self.arena2[:, off - ARENA:off - ARENA + n]
        assert off + n <= ARENA, (off, n)
        return self.arena[:, off:off + n]

    def scoped(self, name, shape, dt=F32):
        self.names += 1
        return self.nc.sbuf_tensor(f"{name}_{self.names}", shape, dt)

    def close(self):
        for s in self.signals.values():
            s.close()
        self.bank_full = []

    def fill(self, matmul, bank=False, tile=False):
        matmul.then_inc(*self.filled.up())
        if bank:
            self.bank_full.append(self.filled.total)
        if tile:
            self.tile_used.append(self.filled.total)

    def wait_bank(self, eng, unit):
        eng.wait_ge(self.filled.sem, self.bank_full[unit])

    def link(self, eng, who, ins):
        s = self.chains[who]
        ins.then_inc(*s.up())
        eng.wait_ge(s.sem, s.total)

    def shape(self, i):
        return self.tiles[i][0].shape[1], self.tiles[i][0].shape[2]

    def ring_tile(self, i):
        kt, n = self.shape(i)
        return self.ring[:, i % RING, 0:kt * n]

    def split_number(self, i):
        return sum(not raw for _, raw in self.tiles[:i])

    def wait_landed(self, eng, i):
        eng.wait_ge(self.landed[i % RING].sem, 16 * (i // RING + 1))

    def issue(self, sp, upto):
        while self.issued < min(upto, len(self.tiles)):
            i = self.issued
            if i >= RING:
                o = i - RING
                if self.tiles[o][1]:
                    if o >= len(self.tile_used):
                        return
                    sp.wait_ge(self.filled.sem, self.tile_used[o])
                else:
                    if o >= self.lo_next:
                        return
                    sp.wait_ge(self.lo_done.sem, self.split_number(o) + 1)
            src = self.tiles[i][0]
            sp.dma_start(self.ring_tile(i).rearrange("p (k n) -> p k n", n=src.shape[2]), src)\
                .then_inc(*self.landed[i % RING].up(16))
            self.issued += 1

    def half(self, i, which):
        kt, n = self.shape(i)
        return self.WS[:, self.split_number(i) % WS_BUFS, which, 0:kt * n]

    def hi(self, act, upto):
        while self.hi_next < min(upto, len(self.tiles)):
            i = self.hi_next
            if not self.tiles[i][1]:
                s = self.split_number(i)
                self.wait_landed(act, i)
                if s >= WS_BUFS:
                    before = [j for j in range(i) if not self.tiles[j][1]][s - WS_BUFS]
                    act.wait_ge(self.filled.sem, self.tile_used[before])
                self.nc.scalar.activation(self.half(i, 0), self.ring_tile(i), ACT.Copy).then_inc(*self.hi_done.up())
            self.hi_next += 1

    def lo(self, dve, upto):
        while self.lo_next < min(upto, len(self.tiles)):
            i = self.lo_next
            if not self.tiles[i][1]:
                dve.wait_ge(self.hi_done.sem, self.split_number(i) + 1)
                self.nc.vector.tensor_tensor(self.half(i, 1), self.ring_tile(i), self.half(i, 0).bitcast(F32),
                                             ALU.subtract).then_inc(*self.lo_done.up())
            self.lo_next += 1

    def weights(self, pe, i):
        kt, n = self.shape(i)
        if self.tiles[i][1]:
            self.wait_landed(pe, i)
            return self.ring_tile(i).rearrange("p (k n) -> p k n", n=n)
        pe.wait_ge(self.lo_done.sem, self.split_number(i) + 1)
        return [self.half(i, w).rearrange("p (k n) -> p k n", n=n) for w in range(2)]


def k_tiles(w):
    return w.rearrange("(k p) n -> p k n", p=P)


def feature_tiles(w, c0=0, c1=None, width=NF, raw=False):
    v = k_tiles(w)
    c1 = w.shape[1] if c1 is None else c1
    return [(v[:, :, n0:min(n0 + width, c1)], raw) for n0 in range(c0, c1, width)]


def token_tiles(w, c0=0, c1=None):
    v = k_tiles(w)
    c1 = w.shape[1] if c1 is None else c1
    return [(v[:, k0:min(k0 + 4, v.shape[1]), n0:min(n0 + NW, c1)], False)
            for n0 in range(c0, c1, NW) for k0 in range(0, v.shape[1], 4)]


def mlp_tiles(ups, down, width=NF):
    out, n = [], ups[0].shape[1] // width
    d = k_tiles(down)
    for c in range(n + 1):
        if c < n:
            for up in ups:
                out += feature_tiles(up, c * width, (c + 1) * width)
        if c:
            out.append((d[:, (c - 1) * width // P:c * width // P, :], False))
    return out


def stage(core, sp=None, pe=None, act=None, dve=None, pool=None, uses=0):
    nc = core.nc
    upto = core.taken + uses + RING + WS_BUFS
    with nc.Block(no_gpsimd_drain=True) as block:
        if pe:
            block.tensor(pe)
        if act:
            block.scalar(act)
        if dve:
            block.vector(dve)
        if pool:
            block.gpsimd(pool)

        @block.sync
        def _(e):
            if sp:
                sp(e)
            core.issue(e, upto)
    core.taken += uses
    core.close()


def product(core, out, w, w_at, x, x_at, first, last, tokens=False):
    for n, (i, j) in enumerate(PASSES):
        lhs, rhs = (x[j][x_at], w[i][w_at]) if tokens else (w[i][w_at], x[j][x_at])
        ins = core.nc.tensor.matmul(out, lhs, rhs, start=(first and n == 0), stop=(last and n == len(PASSES) - 1))
    return ins


ALL = slice(None)


def features_matmul(core, pe, unit, xs, kt, ntiles, free, bank0, nbanks, tile):
    for _ in range(ntiles):
        w = core.weights(pe, tile)
        n = core.shape(tile)[1]
        if unit >= nbanks:
            pe.wait_ge(*free.at(unit - nbanks + 1))
        for h, m0 in enumerate(range(0, n, P)):
            m = min(P, n - m0)
            for k in range(kt):
                last = product(core, core.ps[0:m, bank0 + unit % nbanks, h * T:(h + 1) * T],
                               w, (ALL, k, slice(m0, m0 + m)), xs, (ALL, k, ALL), k == 0, k == kt - 1)
        core.fill(last, bank=True, tile=True)
        unit += 1
        tile += 1
    return unit, tile


def raw_features(core, pe, unit, srcT, kt, ntiles, free, bank0, nbanks, tile):
    for _ in range(ntiles):
        w = core.weights(pe, tile)
        n = core.shape(tile)[1]
        for n0 in range(0, n, NF):
            if unit >= nbanks:
                pe.wait_ge(*free.at(unit - nbanks + 1))
            for h in range(2):
                for k in range(kt):
                    last = core.nc.tensor.matmul(core.ps[:, bank0 + unit % nbanks, h * T:(h + 1) * T],
                                                 w[:, k, n0 + h * P:n0 + (h + 1) * P], srcT[:, k, :],
                                                 start=(k == 0), stop=(k == kt - 1))
            core.fill(last, bank=True, tile=(n0 + NF >= n))
            unit += 1
        tile += 1
    return unit, tile


def tokens_matmul(core, pe, unit, xs, nchunks, free, bank0, nbanks, tile):
    for _ in range(nchunks):
        for tt in range(TT):
            if unit + tt >= nbanks:
                pe.wait_ge(*free.at(unit + tt - nbanks + 1))
        for j in range(2):
            w = core.weights(pe, tile)
            for tt in range(TT):
                for k in range(4):
                    last = product(core, core.ps[:, bank0 + (unit + tt) % nbanks, :], w, (ALL, k, ALL),
                                   xs, (ALL, 4 * j + k, slice(tt * P, (tt + 1) * P)), j + k == 0, 4 * j + k == 7,
                                   tokens=True)
                if j == 1 or tt == TT - 1:
                    core.fill(last, bank=(j == 1), tile=(tt == TT - 1))
            tile += 1
        unit += TT
    return unit, tile


def down_chunk(core, pe, hs, bank0, tile, first, final):
    w = core.weights(pe, tile)
    for tt in range(TT):
        for half in range(2):
            for k in range(2):
                last = product(core, core.ps[:, bank0 + 2 * tt + half, :], w, (ALL, k, slice(half * NW, (half + 1) * NW)),
                               hs, (ALL, k, slice(tt * P, (tt + 1) * P)), first and k == 0, final and k == 1, tokens=True)
    core.fill(last, bank=final, tile=True)


def add_to_x(core, dve, unit, bank0):
    core.wait_bank(dve, unit)
    for tt in range(TT):
        core.nc.vector.tensor_tensor(core.x[:, tt, :], core.x[:, tt, :],
                                     core.ps[:, bank0 + 2 * tt:bank0 + 2 * tt + 2, :].rearrange("p b n -> p (b n)"),
                                     ALU.add)


def halves(t):
    return [t[:, 0], t[:, 1]]


def mlp(core, n, gated):
    nc, ps = core.nc, core.ps
    tmp = core.a(8192, 2 * 512).rearrange("p (b n) -> p b n", b=2)
    h = core.a(9216, 2 * 512).rearrange("p (b n) -> p b n", b=2)
    acted, hidden, h_hi, h_lo = (core.sig(f"mlp_{x}") for x in ("activated", "hidden", "high", "split"))
    ups = 2 if gated else 1
    xs = halves(core.XS)
    t0 = core.taken
    order = []
    for c in range(n + 1):
        if c < n:
            order += [("gate", c), ("up", c)] if gated else [("up", c)]
        if c:
            order.append(("down", c - 1))

    with core.scoped("hidden_split", [P, 2, 2, 2, T], F32R) as HS:
        def pe(e):
            for i, (kind, c) in enumerate(order):
                if kind == "down":
                    e.wait_ge(*h_lo.at(c + 1))
                    down_chunk(core, e, halves(HS[:, c % 2]), 4, t0 + i, c == 0, c == n - 1)
                    continue
                w = core.weights(e, t0 + i)
                if c >= 2:
                    e.wait_ge(*hidden.at(c - 1))
                bank = (2 if gated and kind == "up" else 0) + c % 2
                for t in range(2):
                    for k in range(KD):
                        last = product(core, ps[:, bank, t * T:(t + 1) * T], w, (ALL, k, slice(t * P, (t + 1) * P)),
                                       xs, (ALL, k, ALL), k == 0, k == KD - 1)
                core.fill(last, bank=True, tile=True)

        def act(e):
            for i, (kind, c) in enumerate(order):
                core.hi(e, t0 + i + 1 + WS_BUFS)
                if kind == ("gate" if gated else "up"):
                    core.wait_bank(e, ups * c)
                    if c >= 2:
                        e.wait_ge(*hidden.at(c - 1))
                    nc.scalar.activation(tmp[:, c % 2, :], ps[:, c % 2, :], ACT.Silu if gated else ACT.Relu)\
                        .then_inc(*acted.up())
                if kind == "up":
                    e.wait_ge(*hidden.at(c + 1))
                    if c >= 2:
                        e.wait_ge(core.filled.sem, core.tile_used[t0 + order.index(("down", c - 2))])
                    nc.scalar.activation(HS[:, c % 2, 0].rearrange("p k t -> p (k t)"), h[:, c % 2, :], ACT.Copy)\
                        .then_inc(*h_hi.up())

        def dve(e):
            for i, (kind, c) in enumerate(order):
                core.lo(e, t0 + i + 1 + WS_BUFS)
                if kind == "up":
                    e.wait_ge(*acted.at(c + 1))
                    if gated:
                        core.wait_bank(e, 2 * c + 1)
                        nc.vector.tensor_tensor(h[:, c % 2, :], ps[:, 2 + c % 2, :], tmp[:, c % 2, :], ALU.mult)\
                            .then_inc(*hidden.up())
                    else:
                        nc.vector.scalar_tensor_tensor(h[:, c % 2, :], ps[:, c % 2, :], 0.0, tmp[:, c % 2, :],
                                                       ALU.max, ALU.mult).then_inc(*hidden.up())
                    e.wait_ge(*h_hi.at(c + 1))
                    nc.vector.tensor_tensor(HS[:, c % 2, 1].rearrange("p k t -> p (k t)"), h[:, c % 2, :],
                                            HS[:, c % 2, 0].rearrange("p k t -> p (k t)").bitcast(F32), ALU.subtract)\
                        .then_inc(*h_lo.up())
            add_to_x(core, e, ups * n, 4)
        stage(core, pe=pe, act=act, dve=dve, uses=len(order))


def project(core, srcT):
    nc, ps, x = core.nc, core.ps, core.x
    src_hi, src_lo = core.sig("source_high"), core.sig("source_split")
    t0 = core.taken
    pair = lambda v, u: v[:, 2 * u:2 * u + 2, :].rearrange("p a t -> p (a t)")

    def pe(e):
        e.wait_ge(*src_lo.at(4))
        tokens_matmul(core, e, 0, halves(core.XS), 2, None, 0, 4, t0)

    def act(e):
        for u in range(4):
            nc.scalar.activation(pair(core.XS[:, 0], u), pair(srcT, u), ACT.Copy).then_inc(*src_hi.up())
        for i in range(4):
            core.hi(e, t0 + i + 1 + WS_BUFS)

    def dve(e):
        for u in range(4):
            e.wait_ge(*src_hi.at(u + 1))
            nc.vector.tensor_tensor(pair(core.XS[:, 1], u), pair(srcT, u), pair(core.XS[:, 0], u).bitcast(F32),
                                    ALU.subtract).then_inc(*src_lo.up())
        for i in range(4):
            core.lo(e, t0 + i + 1 + WS_BUFS)
            if i % 2:
                for u in (i - 1, i):
                    core.wait_bank(e, u)
                    xs = x[:, u % 2, (u // 2) * NW:(u // 2 + 1) * NW]
                    nc.vector.tensor_tensor(xs, xs, ps[:, u, :], ALU.add)
    stage(core, pe=pe, act=act, dve=dve, uses=4)


def norm_stage(core, src, dst, gain_col, scratch, extra_sp=None, ahead=True):
    nc = core.nc
    sums, root, inv, scaled, turned, freed = (core.sig(f"norm_{n}") for n in
                                              ("sums", "root", "inv", "scaled", "turned", "freed"))
    sq, xs = core.a(scratch, D), core.a(scratch + D, TT * D).rearrange("p (t d) -> p t d", t=TT)
    st = core.stat

    def act(e):
        for tt in range(TT):
            nc.scalar.activation(sq, src[:, tt, :], ACT.Square, accum_out=st[:, tt:tt + 1]).then_inc(*sums.up())
            e.wait_ge(*sums.at(tt + 1))
            nc.scalar.activation(st[:, 2 + tt:3 + tt], st[:, tt:tt + 1], ACT.Sqrt, scale=1.0 / D,
                                 bias=core.c("eps")[:, E_EPS:E_EPS + 1]).then_inc(*root.up())
        if ahead:
            core.hi(e, core.taken + WS_BUFS)
        for b in range(4):
            e.wait_ge(*turned.at(b + 1))
            for j in range(2):
                k = 2 * b + j
                last = nc.scalar.activation(dst[:, 0, k, :], core.ps[:, b, j * T:(j + 1) * T], ACT.Identity, scale=g(k))
            last.then_inc(*freed.up())

    def g(k):
        return core.cols[:, gain_col[0], gain_col[1] + k:gain_col[1] + k + 1]

    def dve(e):
        for tt in range(TT):
            e.wait_ge(*root.at(tt + 1))
            nc.vector.reciprocal(st[:, 4 + tt:5 + tt], st[:, 2 + tt:3 + tt]).then_inc(*inv.up())
            e.wait_ge(*inv.at(tt + 1))
            nc.vector.tensor_scalar(xs[:, tt, :], src[:, tt, :], st[:, 4 + tt:5 + tt], None, ALU.mult)\
                .then_inc(*scaled.up())
        if ahead:
            core.lo(e, core.taken + WS_BUFS)
        for b in range(4):
            e.wait_ge(*freed.at(b + 1))
            for j in range(2):
                k = 2 * b + j
                nc.vector.scalar_tensor_tensor(dst[:, 1, k, :], core.ps[:, b, j * T:(j + 1) * T], g(k),
                                               dst[:, 0, k, :].bitcast(F32), ALU.mult, ALU.subtract)

    def pe(e):
        e.wait_ge(*scaled.at(TT))
        for b in range(4):
            for j in range(2):
                for tt in range(TT):
                    k = 2 * b + j
                    last = nc.tensor.transpose(core.ps[:, b, j * T + tt * P:j * T + (tt + 1) * P],
                                               xs[:, tt, k * P:(k + 1) * P], core.c("ident"))
            last.then_inc(*turned.up())

    stage(core, sp=extra_sp, pe=pe, act=act, dve=dve)


def grouped_norm(core, buf, ntiles, mean, span, scale2, eps_col, gain, sq, root, bank0=0, subtract=False):
    nc = core.nc
    squares, means, roots, done = (core.sig(f"group_{n}") for n in ("squares", "means", "roots", "inv"))
    units = ntiles // 2

    def act(e):
        for u in range(units):
            nc.scalar.activation(sq[:, u % 2, :], buf[:, 2 * u:2 * u + 2, :].rearrange("p a t -> p (a t)"),
                                 ACT.Square).then_inc(*squares.up())
            if u:
                take_root(e, u - 1)
        take_root(e, units - 1)

    def take_root(e, u):
        e.wait_ge(*means.at(u + 1))
        if u >= 2:
            e.wait_ge(*done.at(u - 1))
        nc.scalar.activation(root[:, u % 2, :], core.ps[:, bank0 + u % 4, :], ACT.Sqrt, scale=scale2,
                             bias=core.c("eps")[:, eps_col:eps_col + 1]).then_inc(*roots.up())

    def pe(e):
        for u in range(units):
            e.wait_ge(*squares.at(u + 1))
            if u >= 4:
                e.wait_ge(*roots.at(u - 3))
            for j in range(2):
                for s in range(span):
                    src = sq[:, u % 2, (s if span == 2 else j) * T:((s if span == 2 else j) + 1) * T]
                    last = nc.tensor.matmul(core.ps[:, bank0 + u % 4, j * T:(j + 1) * T], mean, src,
                                            start=(s == 0), stop=(s == span - 1))
            last.then_inc(*means.up())

    def dve(e):
        for u in range(units):
            e.wait_ge(*roots.at(u + 1))
            core.link(e, "dve", nc.vector.reciprocal(root[:, u % 2, :], root[:, u % 2, :]))
            for j in range(2):
                last = nc.vector.scalar_tensor_tensor(buf[:, 2 * u + j, :], buf[:, 2 * u + j, :], gain(2 * u + j),
                                                      root[:, u % 2, j * T:(j + 1) * T], ALU.mult, ALU.mult)
            last.then_inc(*done.up())

    return pe, act, dve


def attention(core, heads, comps, q_rows, k_rows, v_cols, dv, causal, bias, vN, oT, scratch, lam=None):
    nc = core.nc
    units = heads * comps
    W = CAUS if causal else 2 * T
    q1 = P if causal else T
    spans = [(0, q1), (q1, T)]
    nd = max(1, dv // P)
    pair = dv == DH
    scores, negmax, expd, probs, flipped, copied, outs, kept = (
        core.sig(f"attn_{n}") for n in
        ("scores", "negmax", "expd", "probs", "flipped", "copied", "outs", "kept"))
    s_sb = core.a(scratch, 2 * 512).rearrange("p (b n) -> p b n", b=2)
    p_sb = core.a(scratch + 1024, 4 * 512).rearrange("p (b n) -> p b n", b=4)
    pT = core.a(scratch + 3072, 2 * 512).rearrange("p (b n) -> p b n", b=2)
    nmx = core.a(scratch + 4096, 2 * units)
    sums = core.a(scratch + 4096 + 2 * units, 2 * units)
    rs = core.a(scratch + 4096 + 4 * units, 2 * units)

    def pe(e):
        for s in range(heads + 2):
            if s < heads:
                for c in range(comps):
                    u = s * comps + c
                    if u >= 2:
                        e.wait_ge(*probs.at(u - 1))
                    for tt in range(TT):
                        lo, n = spans[tt]
                        ql, kl = q_rows(u, tt), k_rows(u, n)
                        for i, (q, k) in enumerate(zip(ql, kl)):
                            last = nc.tensor.matmul(core.ps[:, u % 2, lo:lo + n], q, k,
                                                    start=(i == 0), stop=(i == len(ql) - 1))
                    last.then_inc(*scores.up())
            if 1 <= s <= heads:
                h = s - 1
                u = (h + 1) * comps - 1
                e.wait_ge(*probs.at(u + 1))
                if h >= 2:
                    e.wait_ge(*copied.at(h - 1))
                for tt in range(TT):
                    lo, n = spans[tt]
                    for kt in range(n // P):
                        at = (kt * T + tt * P) if (kt == 0 or not causal) else T
                        last = nc.tensor.transpose(core.ps[:, 2 + h % 2, at:at + P],
                                                   p_sb[:, u % 4, lo + kt * P:lo + (kt + 1) * P], core.c("ident"))
                last.then_inc(*flipped.up())
            if s >= 2:
                h = s - 2
                e.wait_ge(*copied.at(h + 1))
                o = h // 2 if pair else h
                if o >= 4 and (not pair or h % 2 == 0):
                    e.wait_ge(*kept.at(o - 3))
                for d in range(nd):
                    m = min(dv, P)
                    m0 = DH * (h % 2) if pair else 0
                    for kt in range(2):
                        if kt == 0 or not causal:
                            cols, src = (d * T, T), pT[:, h % 2, kt * T:(kt + 1) * T]
                        else:
                            cols, src = (d * T + P, P), pT[:, h % 2, T:T + P]
                        last = nc.tensor.matmul(core.ps[m0:m0 + m, 4 + o % 4, cols[0]:cols[0] + cols[1]],
                                                vN[:, kt, v_cols(h) + d * P:v_cols(h) + d * P + m], src,
                                                start=(kt == 0), stop=(kt == 1))
                last.then_inc(*outs.up())

    def act(e):
        for s in range(heads + 2):
            if s < heads:
                for c in range(comps):
                    u = s * comps + c
                    e.wait_ge(*negmax.at(u + 1))
                    if u >= 4:
                        e.wait_ge(*flipped.at((u - 4) // comps + 1))
                    for tt in range(TT):
                        lo, n = spans[tt]
                        src = s_sb[:, u % 2, lo:lo + n] if bias else core.ps[:, u % 2, lo:lo + n]
                        last = nc.scalar.activation(p_sb[:, u % 4, lo:lo + n], src, ACT.Exp,
                                                    bias=nmx[:, 2 * u + tt:2 * u + tt + 1],
                                                    accum_out=sums[:, 2 * u + tt:2 * u + tt + 1])
                    last.then_inc(*expd.up())
            if 1 <= s <= heads:
                h = s - 1
                e.wait_ge(*flipped.at(h + 1))
                if h >= 2:
                    e.wait_ge(*outs.at(h - 1))
                nc.scalar.activation(pT[:, h % 2, 0:W], core.ps[:, 2 + h % 2, 0:W], ACT.Copy).then_inc(*copied.up())
            if s >= 2:
                h = s - 2
                if not pair or h % 2 == 1:
                    o = h // 2 if pair else h
                    e.wait_ge(*outs.at(h + 1))
                    nc.scalar.activation(oT[:, o * nd:(o + 1) * nd, :].rearrange("p a t -> p (a t)"),
                                         core.ps[:, 4 + o % 4, 0:nd * T], ACT.Copy).then_inc(*kept.up())

    def dve(e):
        for u in range(units + 1):
            if u < units:
                e.wait_ge(*scores.at(u + 1))
                if bias:
                    b = bias(e, u)
                    if u >= 2:
                        e.wait_ge(*expd.at(u - 1))
                    for tt in range(TT):
                        lo, n = spans[tt]
                        last = nc.vector.tensor_tensor_reduce(
                            out=s_sb[:, u % 2, lo:lo + n], in0=core.ps[:, u % 2, lo:lo + n], in1=b[tt], scale=1.0,
                            scalar=-3e38, op0=ALU.add, op1=ALU.max, accum_out=rs[:, 2 * u + tt:2 * u + tt + 1])
                    core.link(e, "dve", last)
                    nc.vector.tensor_scalar(nmx[:, 2 * u:2 * u + 2], rs[:, 2 * u:2 * u + 2], -1.0, None, ALU.mult)\
                        .then_inc(*negmax.up())
                else:
                    nc.vector.tensor_reduce(nmx[:, 2 * u:2 * u + 2],
                                            core.ps[:, u % 2, :].rearrange("p (t n) -> p t n", t=TT),
                                            AXX, ALU.max, negate=True).then_inc(*negmax.up())
            if u >= 1:
                w = u - 1
                e.wait_ge(*expd.at(w + 1))
                core.link(e, "dve", nc.vector.reciprocal(rs[:, 2 * w:2 * w + 2], sums[:, 2 * w:2 * w + 2]))
                second = comps == 2 and w % 2 == 1
                if second:
                    e.wait_ge(*probs.at(w))
                    core.link(e, "dve", nc.vector.tensor_scalar(rs[:, 2 * w:2 * w + 2], rs[:, 2 * w:2 * w + 2],
                                                                lam, None, ALU.mult))
                for tt in range(TT):
                    lo, n = spans[tt]
                    p = p_sb[:, w % 4, lo:lo + n]
                    r = rs[:, 2 * w + tt:2 * w + tt + 1]
                    if second:
                        last = nc.vector.scalar_tensor_tensor(p, p, r, p_sb[:, (w - 1) % 4, lo:lo + n],
                                                              ALU.mult, ALU.add)
                    else:
                        last = nc.vector.tensor_scalar(p, p, r, None, ALU.mult)
                last.then_inc(*probs.up())

    return pe, act, dve


def bc(ap, axis, n):
    ap = ap.unsqueeze(axis)
    shape = list(ap.shape)
    shape[axis] = n
    return ap.broadcast_to(shape)


def cross_attention(core, w, layer, at_col, mem_off):
    nc, a, ps, c = core.nc, core.a, core.ps, core.c
    freed = core.sig("bank_copied")
    MH, MD = 4, 256
    mem = a(mem_off, TT * D).rearrange("p (t d) -> p t d", t=TT)
    mem_landed = core.sig("memory_landed")

    def sp(e):
        e.dma_start(mem, w["mem_2"][0].rearrange("(t p) d -> p t d", p=P)).then_inc(*mem_landed.up(16))
    norm_stage(core, core.x, core.XS, at_col("norm_xattn_2", 8 * layer), 0, extra_sp=sp)

    def sp(e):
        e.wait_ge(*mem_landed.at(0))
    stage(core, sp=sp)
    qk = a(0, 16 * T).rearrange("p (n t) -> p n t", t=T)
    vN = a(4096, TT * D).rearrange("p (t d) -> p t d", t=TT)
    oT = a(6144, 8 * T).rearrange("p (n t) -> p n t", t=T)
    SCR = 8192
    with core.scoped("memory_split", [P, 2, KD, T], F32R) as MS:
        norm_stage(core, mem, MS, at_col("norm_mem_2", 8 * layer), 0)
        qkv_products(core, halves(core.XS), halves(MS), qk, vN, None)

    sq = a(SCR, 1024).rearrange("p (b n) -> p b n", b=2)
    root = a(SCR + 1024, 1024).rearrange("p (b n) -> p b n", b=2)

    def gain(name):
        which, r = at_col(name, 2 * layer)
        return lambda j: core.cols[:, which, r + j % 2:r + j % 2 + 1]
    for part, scale2, eps, name in ((0, 256.0, E_EPS256, "xa_q_gain_2"), (8, 1.0, E_EPS, "xa_k_gain_2")):
        gpe, gact, gdve = grouped_norm(core, qk[:, part:part + 8, :], 8, c("mean256"), 2, scale2, eps, gain(name), sq, root)
        stage(core, pe=gpe, act=gact, dve=gdve)
    q, k = qk[:, 0:8, :], qk[:, 8:16, :]
    pe, act, dve = attention(core, MH, 1, lambda u, tt: [q[:, 2 * u + i, tt * P:(tt + 1) * P] for i in range(2)],
                             lambda u, n: [k[:, 2 * u + i, 0:n] for i in range(2)], lambda h: h * MD, MD, False,
                             None, vN, oT, SCR)
    stage(core, pe=pe, act=act, dve=dve)
    project(core, oT)


def qkv_products(core, xs_q, xs_kv, qk, vN, q_scale):
    nc, ps = core.nc, core.ps
    freed = core.sig("bank_copied")
    t0 = core.taken

    def pe(e):
        u, tile = features_matmul(core, e, 0, xs_q, KD, 4, freed, 0, 4, t0)
        u, tile = features_matmul(core, e, u, xs_kv, KD, 4, freed, 0, 4, tile)
        tokens_matmul(core, e, 0, xs_kv, 2, freed, 4, 4, tile)

    def act(e):
        for i in range(12):
            core.hi(e, t0 + i + 1 + WS_BUFS)
            if i < 8:
                core.wait_bank(e, i)
                nc.scalar.activation(qk[:, 2 * i:2 * i + 2, :].rearrange("p a t -> p (a t)"), ps[:, i % 4, :], ACT.Copy,
                                     scale=q_scale if i < 4 and q_scale else 1.0).then_inc(*freed.up())
            elif i % 2:
                for u in (i - 9, i - 8):
                    core.wait_bank(e, 8 + u)
                    nc.scalar.activation(vN[:, u % 2, (u // 2) * NW:(u // 2 + 1) * NW], ps[:, 4 + u, :], ACT.Copy)

    def dve(e):
        for i in range(12):
            core.lo(e, t0 + i + 1 + WS_BUFS)
    stage(core, pe=pe, act=act, dve=dve, uses=12)


EXPERT_CHUNKS = FE // NW
EXPERT_TILES = [(part, c, half) for s in range(EXPERT_CHUNKS + 1)
                for part, c in (("gate", s), ("up", s), ("down", s - 1)) if 0 <= c < EXPERT_CHUNKS
                for half in range(2)]
CAP = P
PIECE = SLOT // 2
AHEAD = 4


def expert_tile(l0, ex, j):
    part, c, half = EXPERT_TILES[j]
    rows, cols = (c, half) if part == "down" else (half, c)
    return l0[f"moe_w_{part}_2"][bass.ds(ex, 1), rows * NW:(rows + 1) * NW, cols * NW:(cols + 1) * NW]\
        .rearrange("e (k p) n -> p (e k) n", p=P)


def mixture(core, w, l0, small):
    nc, a, ps, c, x = core.nc, core.a, core.ps, core.c, core.x
    link = core.link
    gain, hn = a(0, D), a(D, TT * D).rearrange("p (t d) -> p t d", t=TT)
    wr = a(3072, KD * NE).rearrange("p (k e) -> p k e", k=KD)
    br = a(3136, NE)
    lg = a(3152, 16).rearrange("p (t e) -> p t e", t=2)
    top = a(3168, 16).rearrange("p (t e) -> p t e", t=2)
    idx = a(3184, 16).bitcast(U32).rearrange("p (t e) -> p t e", t=2)
    idf = a(3200, 16).rearrange("p (t e) -> p t e", t=2)
    diff, ex_, w1, w2 = (a(3216 + 2 * i, 2) for i in range(4))
    onehot = a(3232, 32).rearrange("p (t i e) -> p t i e", t=2, i=2)
    mask = a(3264, 16).rearrange("p (t e) -> p t e", t=2)
    place = a(3280, 18).rearrange("p (t e) -> p t e", t=2)
    count = a(3300, NE).bitcast(I32)
    sel = a(3328, 2 * CAP).rearrange("p (t s) -> p t s", t=2)
    selT = a(3584, TT * P)
    tmp = a(3840, 2 * NW).rearrange("p (b n) -> p b n", b=2)
    h = a(4864, 2 * NW).rearrange("p (b n) -> p b n", b=2)
    y = a(5888, D)
    gates = small[:, 0:16].rearrange("p (t e) -> p t e", t=2)
    landed, logits, shifted = core.sig("router_landed"), core.sig("router_logits"), core.sig("router_gap")
    expd, masked, placed, hn_done = (core.sig(f"router_{n}") for n in ("exp", "mask", "places", "rows"))
    used, high, split, turns = (core.sig(f"moe_{n}") for n in ("used", "high", "split", "turns"))
    selected, gathered, sel_turned, sel_kept, xg_high, xg_split = (
        core.sig(f"moe_{n}") for n in ("selected", "gathered", "sel_turned", "sel_kept", "xg_high", "xg_split"))
    silud, gated, turned, ht_high, ht_split, y_kept, scattered, summed = (
        core.sig(f"moe_{n}") for n in ("silu", "gated", "turned", "ht_high", "ht_split", "y_kept", "scattered", "summed"))
    FAR = 1000.0

    def select(e):
        for tt in range(TT):
            last = nc.vector.tensor_scalar(sel[:, tt, :], c("iota128"), place[:, tt, bass.ds(e, 1)], None, ALU.is_equal)
        last.then_inc(selected.sem, 1)

    def sp(e):
        e.dma_start(wr, k_tiles(l0["moe_w_router_2"])).then_inc(*landed.up(16))
        e.dma_start(br, w["moe_b_router_2"][0].partition_broadcast(P)).then_inc(*landed.up(16))
        e.dma_start(gain, w["norm_ffn_2"][1].partition_broadcast(P)).then_inc(*landed.up(16))
        e.sem_inc(used.sem, AHEAD)
        e.sem_inc(summed.sem, TT)

    def pe(e):
        e.wait_ge(*landed.at(48))
        hs = [v.bitcast(F32) for v in halves(core.XS)]
        for tt in range(TT):
            for i in range(2):
                for k in range(KD):
                    last = nc.tensor.matmul(ps[:, 0, tt * NE:(tt + 1) * NE], hs[i][:, k, tt * P:(tt + 1) * P],
                                            wr[:, k, :], start=(i + k == 0), stop=(i * KD + k == 2 * KD - 1))
        last.then_inc(*logits.up())
        e.wait_ge(*masked.at(1))
        nc.tensor.matmul(ps[:, 1, 0:NE], c("earlier"), mask[:, 0, :], start=True, stop=True)
        for i, (tt, m) in enumerate(((0, "ones"), (1, "earlier"))):
            nc.tensor.matmul(ps[:, 1, NE:2 * NE], c(m), mask[:, tt, :], start=(i == 0), stop=(i == 1))
        for tt in range(TT):
            last = nc.tensor.matmul(ps[:, 1, 2 * NE:3 * NE], c("ones"), mask[:, tt, :], start=(tt == 0), stop=(tt == 1))
        last.then_inc(*placed.up())

    def dve(e):
        e.wait_ge(*landed.at(48))
        for tt in range(TT):
            nc.vector.tensor_tensor(hn[:, tt, :], hn[:, tt, :], gain, ALU.mult)
        link(e, "dve", nc.vector.tensor_scalar(a(3280, 18), c("ones")[:, 0:18], FAR, None, ALU.mult))
        e.wait_ge(*logits.at(1))
        link(e, "dve", nc.vector.tensor_tensor(lg, ps[:, 0, 0:16].rearrange("p (t e) -> p t e", t=2), bc(br, 1, 2), ALU.add))
        for tt in range(TT):
            link(e, "dve", nc.vector.max(top[:, tt, :], lg[:, tt, :]))
            link(e, "dve", nc.vector.max_index(idx[:, tt, :], top[:, tt, :], lg[:, tt, :]))
        nc.vector.tensor_tensor(diff, top[:, :, 1], top[:, :, 0], ALU.subtract).then_inc(*shifted.up())
        link(e, "dve", nc.vector.tensor_copy(idf, idx))
        for tt in range(TT):
            for i in range(2):
                link(e, "dve", nc.vector.tensor_scalar(onehot[:, tt, i, :], c("iota8"), idf[:, tt, i:i + 1], None, ALU.is_equal))
        nc.vector.tensor_tensor(mask, onehot[:, :, 0, :], onehot[:, :, 1, :], ALU.max).then_inc(*masked.up())
        e.wait_ge(*expd.at(1))
        link(e, "dve", nc.vector.tensor_scalar(w1, ex_, 1.0, None, ALU.add))
        link(e, "dve", nc.vector.reciprocal(w1, w1))
        link(e, "dve", nc.vector.tensor_tensor(w2, ex_, w1, ALU.mult))
        for tt in range(TT):
            link(e, "dve", nc.vector.tensor_scalar(gates[:, tt, :], onehot[:, tt, 0, :], w1[:, tt:tt + 1], None, ALU.mult))
            link(e, "dve", nc.vector.scalar_tensor_tensor(gates[:, tt, :], onehot[:, tt, 1, :], w2[:, tt:tt + 1],
                                                          gates[:, tt, :], ALU.mult, ALU.add))
        e.wait_ge(*placed.at(1))
        e.wait_ge(*masked.at(1))
        link(e, "dve", nc.vector.scalar_tensor_tensor(place[:, :, 0:NE], mask, -FAR,
                                                      ps[:, 1, 0:2 * NE].rearrange("p (t e) -> p t e", t=2),
                                                      ALU.mult, ALU.add))
        link(e, "dve", nc.vector.tensor_scalar(place[:, :, 0:NE], place[:, :, 0:NE], FAR, None, ALU.add))
        nc.vector.tensor_copy(count, ps[:, 1, 2 * NE:3 * NE])
        select(0)

    def act(e):
        e.wait_ge(*shifted.at(1))
        nc.scalar.activation(ex_, diff, ACT.Exp).then_inc(*expd.up())
    stage(core, sp=sp, pe=pe, act=act, dve=dve)

    assert core.issued == len(core.tiles) == core.taken + RING
    first = core.taken
    per = len(EXPERT_TILES)
    pieces = 2 * per
    N = EXPERT_CHUNKS
    assert per % RING == 0 and per % WS_BUFS == 0
    last_of = {(part, chunk): 2 * j + 1 for j, (part, chunk, _) in enumerate(EXPERT_TILES)}
    guard = core.scoped("expert_split", [P, 2, 2, D], F32R)
    split_room = guard.__enter__()
    XG, HT = split_room[:, 0], split_room[:, 1]

    def slot(j):
        return (first + j) % RING

    def ring_piece(p):
        return core.ring[:, slot(p // 2), p % 2 * PIECE:(p % 2 + 1) * PIECE]

    def split_piece(p, half):
        return core.WS[:, p // 2 % WS_BUFS, half, p % 2 * PIECE:(p % 2 + 1) * PIECE]

    def used_value(e, p):
        return e * pieces + (p + 1 + AHEAD)

    def high_half(act, e, p):
        if p % 2 == 0:
            act.wait_ge(core.landed[slot(p // 2)].sem, e * (16 * per // RING) + 16 * ((first + p // 2) // RING + 1))
        act.wait_ge(used.sem, used_value(e, p - AHEAD))
        nc.scalar.activation(split_piece(p, 0), ring_piece(p), ACT.Copy).then_inc(high.sem, 1)

    def low_half(dve, e, p):
        dve.wait_ge(high.sem, e * pieces + (p + 1))
        nc.vector.tensor_tensor(split_piece(p, 1), ring_piece(p), split_piece(p, 0).bitcast(F32), ALU.subtract)\
            .then_inc(split.sem, 1)

    def gather(pe, e):
        pe.wait_ge(selected.sem, e + 1)
        for k in range(KD):
            for tt in range(TT):
                last = nc.tensor.matmul(ps[:, 6 + k // 4, k % 4 * CAP:(k % 4 + 1) * CAP], hn[:, tt, k * P:(k + 1) * P],
                                        sel[:, tt, :], start=(tt == 0), stop=(tt == TT - 1))
            if k % 4 == 3:
                last.then_inc(gathered.sem, 1)

    def turn_selection(pe):
        for tt in range(TT):
            last = nc.tensor.transpose(ps[:, 5, tt * P:(tt + 1) * P], sel[:, tt, :], c("ident"))
        last.then_inc(sel_turned.sem, 1)

    def keep_high(act, e):
        for b in range(2):
            act.wait_ge(gathered.sem, e * 2 + (b + 1))
            nc.scalar.activation(XG[:, 0, b * NW:(b + 1) * NW], ps[:, 6 + b, :], ACT.Copy).then_inc(xg_high.sem, 1)

    def keep_low(dve, e):
        for b in range(2):
            dve.wait_ge(xg_high.sem, e * 2 + (b + 1))
            nc.vector.tensor_tensor(XG[:, 1, b * NW:(b + 1) * NW], ps[:, 6 + b, :],
                                    XG[:, 0, b * NW:(b + 1) * NW].bitcast(F32), ALU.subtract).then_inc(xg_split.sem, 1)

    def products(pe, e, part, chunk, banks, stationary, opens=True, closes=True):
        tts = len(banks[0])
        for half in range(2):
            j = EXPERT_TILES.index((part, chunk, half))
            for q in range(2):
                p = 2 * j + q
                pe.wait_ge(split.sem, e * pieces + (p + 1))
                for tt in range(tts):
                    for kk in range(2):
                        k = 2 * q + kk + (4 * half if part != "down" else 0)
                        for n, (i, s) in enumerate(PASSES):
                            last = nc.tensor.matmul(
                                ps[:, banks[half][tt], :], stationary(s, k, tt),
                                split_piece(p, i)[:, kk * NW:(kk + 1) * NW],
                                start=(opens and n == 0 and k == 0),
                                stop=(closes and n == len(PASSES) - 1 and k == (3 if part == "down" else KD - 1)))
                last.then_inc(used.sem, 1)

    def add_tile(dve, ex, tt, bank):
        dve.wait_ge(summed.sem, ex * TT + (tt + 1))
        nc.vector.scalar_tensor_tensor(
            x[:, tt, :], ps[:, bank:bank + 2, :].rearrange("p b n -> p (b n)"),
            gates[:, tt, bass.ds(ex, 1)], x[:, tt, :], ALU.mult, ALU.add).then_inc(summed.sem, 1)

    def slots_pe(pe, ex):
        rows = lambda i, k, tt: XG[:, i, k * CAP:(k + 1) * CAP]
        for s in range(N + 1):
            if s < N:
                if s == 0:
                    pe.wait_ge(xg_split.sem, ex * 2 + 2)
                    pe.wait_ge(summed.sem, ex * TT + 1)
                elif s >= 2:
                    pe.wait_ge(silud.sem, ex * N + (s - 1))
                products(pe, ex, "gate", s, [[s % 2]] * 2, rows)
            if s >= 1:
                pe.wait_ge(gated.sem, ex * N + s)
                for k in range(4):
                    last = nc.tensor.transpose(ps[:, 6 + (s - 1) % 2, k * CAP:(k + 1) * CAP],
                                               h[:, (s - 1) % 2, k * P:(k + 1) * P], c("ident"))
                last.then_inc(turned.sem, 1)
            if s < N:
                if s == 0:
                    pe.wait_ge(summed.sem, ex * TT + 2)
                elif s >= 2:
                    pe.wait_ge(gated.sem, ex * N + (s - 1))
                products(pe, ex, "up", s, [[2 + s % 2]] * 2, rows)
            if s >= 1:
                if s == 1:
                    pe.wait_ge(sel_kept.sem, ex + 1)
                pe.wait_ge(ht_split.sem, ex * N + s)
                hidden = lambda i, k, tt: HT[:, i, (s - 1) % 2 * NW + k * CAP:(s - 1) % 2 * NW + (k + 1) * CAP]
                products(pe, ex, "down", s - 1, [[4], [5]], hidden, s == 1, s == N)
        gather(pe, ex + 1)
        pe.wait_ge(y_kept.sem, ex + 1)
        for tt in range(TT):
            for half in range(2):
                last = nc.tensor.matmul(ps[:, 2 * tt + half, :], selT[:, tt * P:(tt + 1) * P],
                                        y[:, half * NW:(half + 1) * NW], start=True, stop=True)
            last.then_inc(scattered.sem, 1)
        turn_selection(pe)

    def slots_act(act, ex):
        for p in range(pieces):
            high_half(act, ex, p + AHEAD)
            for chunk in range(N):
                turned_after = last_of["gate", chunk + 1] if chunk < N - 1 else last_of["down", N - 2]
                if p == turned_after:
                    act.wait_ge(turned.sem, ex * N + (chunk + 1))
                    nc.scalar.activation(HT[:, 0, chunk % 2 * NW:(chunk % 2 + 1) * NW], ps[:, 6 + chunk % 2, :],
                                         ACT.Copy).then_inc(ht_high.sem, 1)
            for chunk in range(N):
                if p == last_of["gate", chunk]:
                    act.wait_ge(used.sem, used_value(ex, p))
                    if chunk >= 2:
                        act.wait_ge(gated.sem, ex * N + (chunk - 1))
                    nc.scalar.activation(tmp[:, chunk % 2, :], ps[:, chunk % 2, :], ACT.Silu).then_inc(silud.sem, 1)
        act.wait_ge(used.sem, used_value(ex, pieces - 1))
        nc.scalar.activation(y, ps[:, 4:6, :].rearrange("p b n -> p (b n)"), ACT.Copy).then_inc(y_kept.sem, 1)
        keep_high(act, ex + 1)

    def slots_dve(dve, ex):
        for p in range(pieces):
            low_half(dve, ex, p + AHEAD)
            for chunk in range(N):
                turned_after = last_of["gate", chunk + 1] if chunk < N - 1 else last_of["down", N - 2]
                if p == turned_after:
                    dve.wait_ge(ht_high.sem, ex * N + (chunk + 1))
                    at = slice(chunk % 2 * NW, (chunk % 2 + 1) * NW)
                    nc.vector.tensor_tensor(HT[:, 1, at], ps[:, 6 + chunk % 2, :], HT[:, 0, at].bitcast(F32),
                                            ALU.subtract).then_inc(ht_split.sem, 1)
                if p == last_of["up", chunk]:
                    dve.wait_ge(used.sem, used_value(ex, p))
                    dve.wait_ge(silud.sem, ex * N + (chunk + 1))
                    if chunk >= 2:
                        dve.wait_ge(turned.sem, ex * N + (chunk - 1))
                    nc.vector.tensor_tensor(h[:, chunk % 2, :], ps[:, 2 + chunk % 2, :], tmp[:, chunk % 2, :], ALU.mult)\
                        .then_inc(gated.sem, 1)
        dve.wait_ge(sel_turned.sem, ex + 1)
        select(ex + 1)
        keep_low(dve, ex + 1)
        for tt in range(TT):
            dve.wait_ge(scattered.sem, ex * TT + (tt + 1))
            add_tile(dve, ex, tt, 2 * tt)

    def dense_pe(pe, ex):
        rows = lambda i, k, tt: core.XS[:, i, k, tt * P:(tt + 1) * P]
        hidden = lambda i, k, tt: HT[:, i, k * T + tt * P:k * T + (tt + 1) * P]
        for s in range(N + 1):
            if s < N:
                if s == 0:
                    pe.wait_ge(summed.sem, ex * TT + 2)
                    pe.wait_ge(sel_kept.sem, ex + 1)
                    pe.wait_ge(xg_split.sem, ex * 2 + 2)
                else:
                    pe.wait_ge(ht_split.sem, ex * N + s)
                products(pe, ex, "gate", s, [[0, 1]] * 2, rows)
                products(pe, ex, "up", s, [[2, 3]] * 2, rows)
            if s >= 1:
                pe.wait_ge(ht_split.sem, ex * N + s)
                products(pe, ex, "down", s - 1, [[4, 6], [5, 7]], hidden, s == 1, s == N)
            if s < N:
                pe.wait_ge(gated.sem, ex * N + (s + 1))
                for k in range(4):
                    for tt in range(TT):
                        last = nc.tensor.transpose(ps[:, k // 2, k % 2 * T + tt * P:k % 2 * T + (tt + 1) * P],
                                                   h[:, tt, k * P:(k + 1) * P], c("ident"))
                last.then_inc(turned.sem, 1)
        pe.wait_ge(summed.sem, ex * TT + 4)
        pe.sem_inc(scattered.sem, TT)
        gather(pe, ex + 1)
        turn_selection(pe)

    def dense_act(act, ex):
        for p in range(pieces):
            high_half(act, ex, p + AHEAD)
            for chunk in range(N):
                if p == last_of["gate", chunk]:
                    act.wait_ge(used.sem, used_value(ex, p))
                    for tt in range(TT):
                        last = nc.scalar.activation(tmp[:, tt, :], ps[:, tt, :], ACT.Silu)
                    last.then_inc(silud.sem, 1)
                if p == (last_of["down", chunk - 1] if chunk else last_of["up", 0]):
                    act.wait_ge(turned.sem, ex * N + (chunk + 1))
                    nc.scalar.activation(HT[:, 0, :], ps[:, 0:2, :].rearrange("p b n -> p (b n)"), ACT.Copy)\
                        .then_inc(ht_high.sem, 1)
        act.sem_inc(y_kept.sem, 1)
        keep_high(act, ex + 1)

    def dense_dve(dve, ex):
        for p in range(pieces):
            low_half(dve, ex, p + AHEAD)
            for chunk in range(N):
                if p == last_of["up", chunk]:
                    dve.wait_ge(used.sem, used_value(ex, p))
                    dve.wait_ge(silud.sem, ex * N + (chunk + 1))
                    for tt in range(TT):
                        last = nc.vector.tensor_tensor(h[:, tt, :], ps[:, 2 + tt, :], tmp[:, tt, :], ALU.mult)
                    last.then_inc(gated.sem, 1)
                if p == (last_of["down", chunk - 1] if chunk else last_of["up", 0]):
                    dve.wait_ge(ht_high.sem, ex * N + (chunk + 1))
                    nc.vector.tensor_tensor(HT[:, 1, :], ps[:, 0:2, :].rearrange("p b n -> p (b n)"),
                                            HT[:, 0, :].bitcast(F32), ALU.subtract).then_inc(ht_split.sem, 1)
        dve.wait_ge(used.sem, used_value(ex, pieces - 1))
        for tt in range(TT):
            add_tile(dve, ex, tt, 4 + 2 * tt)
        dve.wait_ge(sel_turned.sem, ex + 1)
        select(ex + 1)
        keep_low(dve, ex + 1)

    with nc.Block(no_gpsimd_drain=True) as block:
        @block.sync
        def _(sp):
            def load(e, j):
                sp.wait_ge(split.sem, e * pieces + 2 * (j - RING + 1))
                sp.sem_inc(turns.sem, 1)
                sp.dma_start(core.ring[:, slot(j), :].rearrange("p (k n) -> p k n", n=NW),
                             expert_tile(l0, e + j // per, j % per)).then_inc(core.landed[slot(j)].sem, 16)
            with sp.Fori(0, NE - 1) as ex:
                for j in range(RING, per + RING):
                    load(ex, j)
            for j in range(RING, per):
                load(NE - 1, j)
            for j in range(per, per + AHEAD // 2):
                sp.wait_ge(split.sem, (NE - 1) * pieces + 2 * (j - RING + 1))
                sp.sem_inc(core.landed[slot(j)].sem, 16)

        @block.tensor
        def _(pe):
            gather(pe, 0)
            turn_selection(pe)
            with pe.Fori(0, NE) as ex:
                n = pe.value_load(count[0:1, bass.ds(ex, 1)])
                with pe.If(n > CAP):
                    dense_pe(pe, ex)
                with pe.Else():
                    slots_pe(pe, ex)

        @block.scalar
        def _(act):
            for p in range(AHEAD):
                high_half(act, 0, p)
            keep_high(act, 0)
            with act.Fori(0, NE) as ex:
                n = act.value_load(count[0:1, bass.ds(ex, 1)])
                act.wait_ge(sel_turned.sem, ex + 1)
                nc.scalar.activation(selT, ps[:, 5, 0:TT * P], ACT.Copy).then_inc(sel_kept.sem, 1)
                with act.If(n > CAP):
                    dense_act(act, ex)
                with act.Else():
                    slots_act(act, ex)

        @block.vector
        def _(dve):
            for p in range(AHEAD):
                low_half(dve, 0, p)
            keep_low(dve, 0)
            with dve.Fori(0, NE) as ex:
                n = dve.value_load(count[0:1, bass.ds(ex, 1)])
                with dve.If(n > CAP):
                    dense_dve(dve, ex)
                with dve.Else():
                    slots_dve(dve, ex)
    guard.__exit__(None, None, None)


def rwkv_s5(core, w, l0, col, at_col, small, ws_guard):
    nc, a, ps, c, x, link = core.nc, core.a, core.ps, core.c, core.x, core.link
    freed = core.sig("bank_copied")
    NT = 15
    J = RW // P
    v3 = lambda off, n: a(off, n * T).rearrange("p (n t) -> p n t", t=T)
    flat = lambda b: b.rearrange("p a t -> p (a t)")
    YT = v3(0, 8)
    UT = v3(2048, J)
    LORA_W = a(3072, RW)
    GUP = a(3584, 2 * RW).rearrange("p (k n) -> p k n", k=2)
    Z = a(4608, NT * (T + 1)).rearrange("p (n t) -> p n t", t=T + 1)
    DIF = v3(8704, NT)
    lora_landed = core.sig("lora_landed")

    def sp(e):
        e.dma_start(LORA_W[0:64, :], l0["rw_w_up_2"]).then_inc(*lora_landed.up(16))
        e.dma_start(LORA_W[64:128, :], l0["rw_a_up_2"]).then_inc(*lora_landed.up(16))
        e.dma_start(GUP[:, 0, :], l0["rw_g_up_2"][0:P, :]).then_inc(*lora_landed.up(16))
        e.dma_start(GUP[0:32, 1, :], l0["rw_g_up_2"][P:160, :]).then_inc(*lora_landed.up(16))
    norm_stage(core, x, core.XS, at_col("norm_mix_2"), 8704, extra_sp=sp)

    unit_tiles = [(0, 2), (2, 2), (4, 2), (6, 2), (8, 2), (10, 2), (12, 2), (14, 1)]

    t0 = core.taken

    def pe(e):
        features_matmul(core, e, 0, halves(core.XS), KD, 10, freed, 0, 8, core.taken)

    def act(e):
        for i in range(10):
            core.hi(e, min(t0 + i + 1 + WS_BUFS, t0 + 10))

    def dve(e):
        zero = core.sig("z_cleared")
        nc.vector.memset(Z[:, :, 0:1], 0.0)
        nc.vector.memset(Z[:, 14, 1:T + 1], 0.0).then_inc(*zero.up())
        e.wait_ge(*zero.at(1))
        for u, (z0, n) in enumerate(unit_tiles):
            core.lo(e, min(t0 + u + 1 + WS_BUFS, t0 + 10))
            core.wait_bank(e, u)
            m = 32 if u == 7 else P
            nc.vector.tensor_copy(Z[0:m, z0:z0 + n, 1:T + 1], ps[0:m, u, 0:n * T].rearrange("p (n t) -> p n t", t=T))\
                .then_inc(*freed.up())
        for u in (8, 9):
            core.wait_bank(e, u)
            last = nc.vector.tensor_copy(flat(UT[:, 2 * (u - 8):2 * (u - 8) + 2, :]), ps[:, u - 8, :])
            last.then_inc(*freed.up())
        e.wait_ge(*freed.at(8))
        link(e, "dve", nc.vector.tensor_tensor(DIF, Z[:, :, 0:T], Z[:, :, 1:T + 1], ALU.subtract))
        for t in range(NT):
            nc.vector.scalar_tensor_tensor(DIF[:, t, :], DIF[:, t, :], col("mu", t), Z[:, t, 1:T + 1], ALU.mult, ALU.add)
    stage(core, pe=pe, act=act, dve=dve, uses=10)
    ws_guard.__exit__(None, None, None)
    room = core.scoped("mixers", [P, 24576 - ARENA])
    core.arena2 = room.__enter__()

    R, K, V = DIF[:, 0:4, :], DIF[:, 4:8, :], DIF[:, 8:12, :]
    WA, GD = DIF[:, 12, :], DIF[:, 13:15, :]
    G = v3(4608, J)
    A = v3(5632, J)
    LD = v3(6656, J)
    LC = v3(7680, J)
    KK = v3(12544, J)
    PINC, PINV, PEXC = v3(13568, J), v3(14592, J), v3(15616, J)
    BT, KT = v3(16640, J), v3(17664, J)
    AR = a(18688, 2 * J * T).rearrange("p (j t q n) -> p j t q n", j=J, t=TT, q=2)
    BON = v3(20736, J)
    VN = a(21760, TT * RW).rearrange("p (t n) -> p t n", t=TT)

    act_in, lora, act_out = core.sig("lora_inputs"), core.sig("lora_products"), core.sig("lora_applied")
    scan_done, kk_in, kk_sum, kk_root = (core.sig(f"kk_{n}") for n in ("scan", "squares", "sums", "roots"))

    def pe(e):
        e.wait_ge(*lora_landed.at(0))
        e.wait_ge(*act_in.at(1))
        for j in range(J):
            last = nc.tensor.matmul(ps[:, j // 2, (j % 2) * T:(j % 2 + 1) * T], LORA_W[0:64, j * P:(j + 1) * P],
                                    WA[0:64, :], start=True, stop=True)
        last.then_inc(*lora.up())
        for j in range(J):
            last = nc.tensor.matmul(ps[:, 2 + j // 2, (j % 2) * T:(j % 2 + 1) * T], LORA_W[64:128, j * P:(j + 1) * P],
                                    WA[64:128, :], start=True, stop=True)
        last.then_inc(*lora.up())
        e.wait_ge(*act_in.at(2))
        for j in range(J):
            nc.tensor.matmul(ps[:, 4 + j // 2, (j % 2) * T:(j % 2 + 1) * T], GUP[:, 0, j * P:(j + 1) * P],
                             GD[:, 0, :], start=True, stop=False)
            last = nc.tensor.matmul(ps[:, 4 + j // 2, (j % 2) * T:(j % 2 + 1) * T], GUP[0:32, 1, j * P:(j + 1) * P],
                                    GD[0:32, 1, :], start=False, stop=True)
        last.then_inc(*lora.up())
        e.wait_ge(*kk_in.at(1))
        for j in range(J):
            last = nc.tensor.matmul(ps[:, 6 + j // 2, (j % 2) * T:(j % 2 + 1) * T], c("sum64"), PEXC[:, j, :],
                                    start=True, stop=True)
        last.then_inc(*kk_sum.up())

    def act(e):
        nc.scalar.activation(WA[0:64, :], WA[0:64, :], ACT.Tanh).then_inc(*act_in.up())
        nc.scalar.activation(flat(GD), flat(GD), ACT.Sigmoid).then_inc(*act_in.up())
        e.wait_ge(*lora.at(1))
        for j in range(J):
            last = nc.scalar.activation(LD[:, j, :], ps[:, j // 2, (j % 2) * T:(j % 2 + 1) * T], ACT.Sigmoid,
                                        bias=col("rw_w0_2", j))
        last.then_inc(*act_out.up())
        e.wait_ge(*lora.at(2))
        for j in range(J):
            last = nc.scalar.activation(A[:, j, :], ps[:, 2 + j // 2, (j % 2) * T:(j % 2 + 1) * T], ACT.Sigmoid,
                                        bias=col("rw_a0_2", j))
        last.then_inc(*act_out.up())
        e.wait_ge(*lora.at(3))
        nc.scalar.activation(flat(G), ps[:, 4:6, :].rearrange("p b n -> p (b n)"), ACT.Copy)
        e.wait_ge(*kk_root.at(1))
        nc.scalar.activation(flat(PEXC), flat(PEXC), ACT.Sqrt).then_inc(*kk_root.up())

    def dve(e):
        for j in range(J):
            last = nc.vector.tensor_scalar(KK[:, j, :], K[:, j, :], col("rw_k_k_2", j), None, ALU.mult)
        link(e, "dve", last)
        nc.vector.tensor_tensor(flat(PEXC), flat(KK), flat(KK), ALU.mult).then_inc(*kk_in.up())
        e.wait_ge(*act_out.at(1))
        link(e, "dve", nc.vector.tensor_scalar(flat(LD), flat(LD), -math.exp(-0.5), None, ALU.mult))
        for j in range(J):
            last = nc.vector.tensor_tensor_scan(LC[:, j, :], c("carry"), LD[:, j, :], 0.0, ALU.mult, ALU.add)
        link(e, "dve", last)
        e.wait_ge(*kk_sum.at(1))
        nc.vector.tensor_scalar(flat(PEXC), ps[:, 6:8, :].rearrange("p b n -> p (b n)"), 1e-24, None, ALU.max)\
            .then_inc(*kk_root.up())
        e.wait_ge(*kk_root.at(2))
        link(e, "dve", nc.vector.reciprocal(flat(PEXC), flat(PEXC)))
        link(e, "dve", nc.vector.tensor_tensor(flat(KK), flat(KK), flat(PEXC), ALU.mult))
        e.wait_ge(*act_out.at(2))
        for j in range(J):
            link(e, "dve", nc.vector.tensor_scalar(small[:, 20 + j:21 + j], col("rw_k_a_2", j), -1.0, 1.0, ALU.mult, ALU.add))
        for j in range(J):
            last = nc.vector.tensor_scalar(PINC[:, j, :], A[:, j, :], col("rw_k_a_2", j), small[:, 20 + j:21 + j],
                                           ALU.mult, ALU.add)
        link(e, "dve", last)
        link(e, "dve", nc.vector.tensor_tensor(flat(K), flat(K), flat(PINC), ALU.mult))
        for j in range(J):
            last = nc.vector.scalar_tensor_tensor(BON[:, j, :], R[:, j, :], col("rw_r_k_2", j), K[:, j, :], ALU.mult, ALU.mult)
        nc.vector.tensor_tensor(flat(PEXC), flat(LC), flat(LD), ALU.subtract)
        nc.vector.tensor_tensor(flat(A), flat(A), flat(KK), ALU.mult)
    stage(core, pe=pe, act=act, dve=dve)

    exps, applied, turned, bsum = (core.sig(f"decay_{n}") for n in ("exps", "applied", "turned", "bonus"))
    PC = small[:, 24:24 + J * NCH].rearrange("p (j c) -> p j c", c=NCH)
    BN = a(4608 + 1024, TT * RW).rearrange("p (t n) -> p t n", t=TT)
    KN = a(6656, TT * RW).rearrange("p (t n) -> p t n", t=TT)

    def act(e):
        nc.scalar.activation(flat(PINV), flat(LC), ACT.Exp, scale=-1.0).then_inc(*exps.up())
        nc.scalar.activation(flat(PINC), flat(LC), ACT.Exp).then_inc(*exps.up())
        nc.scalar.activation(flat(PEXC), flat(PEXC), ACT.Exp).then_inc(*exps.up())
        for i, dst in enumerate((VN, BN, KN)):
            e.wait_ge(*turned.at(i + 1))
            for tt in range(TT):
                nc.scalar.activation(dst[:, tt, :], ps[:, 2 * i + tt, :], ACT.Copy)

    def dve(e):
        e.wait_ge(*exps.at(1))
        nc.vector.tensor_tensor(flat(BT), flat(A), flat(PINV), ALU.mult).then_inc(*applied.up())
        nc.vector.tensor_tensor(flat(KT), flat(K), flat(PINV), ALU.mult).then_inc(*applied.up())
        e.wait_ge(*exps.at(3))
        shape = lambda b: b.rearrange("p j (t n) -> p j t n", t=TT)
        for j in range(J):
            nc.vector.tensor_tensor(AR[:, j, :, 0, :], shape(KK)[:, j], shape(PEXC)[:, j], ALU.mult)
            nc.vector.tensor_tensor(AR[:, j, :, 1, :], shape(R)[:, j], shape(PINC)[:, j], ALU.mult)
        nc.vector.tensor_copy(PC, PINC.rearrange("p j (c n) -> p j c n", n=CH)[:, :, :, CH - 1])
        e.wait_ge(*bsum.at(1))
        nc.vector.tensor_tensor(flat(BON), ps[:, 6:8, :].rearrange("p b n -> p (b n)"), flat(V), ALU.mult)

    def pe(e):
        for i, src in enumerate((V, BT, KT)):
            if i:
                e.wait_ge(*applied.at(i))
            for tt in range(TT):
                for j in range(J):
                    last = nc.tensor.transpose(ps[:, 2 * i + tt, j * P:(j + 1) * P], src[:, j, tt * P:(tt + 1) * P], c("ident"))
            last.then_inc(*turned.up())
        for j in range(J):
            last = nc.tensor.matmul(ps[:, 6 + j // 2, (j % 2) * T:(j % 2 + 1) * T], c("sum64"), BON[:, j, :],
                                    start=True, stop=True)
        last.then_inc(*bsum.up())
    stage(core, pe=pe, act=act, dve=dve)

    NU = 16
    PB, PK = (a(off, NU * 256).rearrange("p (u n) -> p u n", u=NU) for off in (7680, 12544))
    pairs, masked = core.sig("pairs"), core.sig("pairs_masked")
    at, _ = core.const_at["strict"]
    masks = core.const[:, at:at + 2 * P]

    def pe(e):
        for u in range(NU):
            j, tt, hp = u // 4, (u // 2) % 2, u % 2
            if u >= 4:
                e.wait_ge(*masked.at(u - 3))
            rows = slice(64 * hp, 64 * hp + 64)
            for i, src in enumerate((BT, KT)):
                last = nc.tensor.matmul(ps[:, u % 4, i * 256:(i + 1) * 256], src[rows, j, tt * P:(tt + 1) * P],
                                        AR[rows, j, tt, :, :].rearrange("p q n -> p (q n)"), start=True, stop=True)
            last.then_inc(*pairs.up())

    def dve(e):
        for u in range(NU):
            e.wait_ge(*pairs.at(u + 1))
            nc.vector.tensor_tensor(PB[:, u, :], ps[:, u % 4, 0:256], masks, ALU.mult)
            nc.vector.tensor_tensor(PK[:, u, :], ps[:, u % 4, 256:512], masks, ALU.mult).then_inc(*masked.up())
    stage(core, pe=pe, dve=dve)

    XT = a(16640, NU * P).rearrange("p (b n) -> p b n", b=4)
    inverse(core, PB, a(0, NU * P).rearrange("p (b n) -> p b n", b=4), XT,
            a(22784, 1024).rearrange("p (b n) -> p b n", b=2), a(3072, 1024).rearrange("p (b n) -> p b n", b=2))
    O = YT[:, 0:4, :]
    recurrence(core, PB, PK, XT, AR, BN, KN, VN, PC, O, a(3072, RW), a(22784, RW),
               a(4096, 512).rearrange("p (j n) -> p j n", j=J))
    head_norm(core, O, BON, G, col, v3(7680, J))
    s5(core, l0, col, UT, YT[:, 4:8, :])

    room.__exit__(None, None, None)
    core.arena2 = None
    ws_guard = core.scoped("weights_split", [P, WS_BUFS, 2, SLOT], F32R)
    core.WS = ws_guard.__enter__()
    project(core, YT)
    return ws_guard


def inverse(core, PB, X, XT, LM, W1):
    nc, ps, c = core.nc, core.ps, core.c
    started, turned, xready, masked, w1, w1_copied, prods, updated = (core.sig(f"inverse_{n}") for n in
        ("started", "turned", "x_ready", "masked", "w1", "w1_copied", "products", "updated"))
    LT = lambda b: PB[:, 4 * b:4 * b + 4, 0:P]
    q = lambda v: v.rearrange("p (u n) -> p u n", u=4)
    levels = (2, 4, 8, 16, 32)
    steps = [(s, b) for s in levels for b in range(4)]

    def dve(e):
        for b in range(4):
            core.link(e, "dve", nc.vector.tensor_tensor(q(XT[:, b, :]), LT(b), bc(c("level1"), 1, 4), ALU.mult))
            nc.vector.tensor_tensor(q(XT[:, b, :]), bc(c("ident"), 1, 4), q(XT[:, b, :]), ALU.subtract)\
                .then_inc(*started.up())
        for n, (s, b) in enumerate(steps):
            e.wait_ge(*prods.at(n + 1))
            if s != levels[-1]:
                nc.vector.tensor_tensor(X[:, b, :], X[:, b, :], ps[:, 2 + n % 2, :], ALU.subtract)
            nc.vector.tensor_tensor(XT[:, b, :], XT[:, b, :], ps[:, 4 + n % 2, :], ALU.subtract).then_inc(*updated.up())

    def act(e):
        for b in range(4):
            e.wait_ge(*turned.at(b + 1))
            nc.scalar.activation(X[:, b, :], ps[:, 6 + b % 2, :], ACT.Copy).then_inc(*xready.up())
        for n in range(len(steps)):
            e.wait_ge(*w1.at(n + 1))
            if n >= 2:
                e.wait_ge(*prods.at(n - 1))
            nc.scalar.activation(W1[:, n % 2, :], ps[:, n % 2, :], ACT.Copy).then_inc(*w1_copied.up())

    def pool(e):
        for n, (s, b) in enumerate(steps):
            if n >= 2:
                e.wait_ge(*w1.at(n - 1))
            nc.gpsimd.tensor_tensor(q(LM[:, n % 2, :]), LT(b), bc(c(f"level{s}"), 1, 4), ALU.mult).then_inc(*masked.up())

    def pe(e):
        for b in range(4):
            e.wait_ge(*started.at(b + 1))
            if b >= 2:
                e.wait_ge(*xready.at(b - 1))
            for u in range(4):
                last = nc.tensor.transpose(ps[:, 6 + b % 2, u * P:(u + 1) * P], XT[:, b, u * P:(u + 1) * P], c("ident"))
            last.then_inc(*turned.up())
        for n in range(len(steps) + 1):
            if n < len(steps):
                s, b = steps[n]
                e.wait_ge(*masked.at(n + 1))
                if n < 4:
                    e.wait_ge(*xready.at(n + 1))
                else:
                    e.wait_ge(*updated.at(n - 3))
                if n >= 2:
                    e.wait_ge(*w1_copied.at(n - 1))
                for u in range(4):
                    cols = slice(u * P, (u + 1) * P)
                    last = nc.tensor.matmul(ps[:, n % 2, cols], LM[:, n % 2, cols], X[:, b, cols], start=True, stop=True)
                last.then_inc(*w1.up())
            if n >= 1:
                m = n - 1
                s, b = steps[m]
                e.wait_ge(*w1_copied.at(m + 1))
                if m >= 2:
                    e.wait_ge(*updated.at(m - 1))
                for u in range(4):
                    cols = slice(u * P, (u + 1) * P)
                    if s != levels[-1]:
                        nc.tensor.matmul(ps[:, 2 + m % 2, cols], XT[:, b, cols], W1[:, m % 2, cols], start=True, stop=True)
                for u in range(4):
                    cols = slice(u * P, (u + 1) * P)
                    last = nc.tensor.matmul(ps[:, 4 + m % 2, cols], W1[:, m % 2, cols], XT[:, b, cols], start=True, stop=True)
                last.then_inc(*prods.up())
    stage(core, pe=pe, act=act, dve=dve, pool=pool)


def recurrence(core, PB, PK, XT, AR, BN, KN, VN, PC, O, GS, US, S):
    nc, ps = core.nc, core.ps
    J = RW // P
    cleared, g_done, g_neg, u_done, u_copied, o_done, o_copied, s_done, s_new = (core.sig(f"state_{n}") for n in
        ("cleared", "g", "g_negated", "u", "u_copied", "o", "o_copied", "products", "new"))

    def split(c):
        return c // 2, CH * (c % 2)

    def pe(e):
        e.wait_ge(*cleared.at(3))
        for c in range(NCH):
            tt, pb = split(c)
            tok = slice(pb, pb + CH)
            if c:
                e.wait_ge(*s_new.at(c))
            for j in range(J):
                nc.tensor.matmul(ps[tok, 0, j * P:(j + 1) * P], AR[:, j, tt, 0, tok], S[:, j, :], start=True, stop=False)
                for hp in range(2):
                    u = 4 * j + 2 * tt + hp
                    h0 = j * P + 64 * hp
                    last = nc.tensor.matmul(ps[tok, 0, h0:h0 + 64], PK[:, u, pb:pb + CH], VN[:, tt, h0:h0 + 64],
                                            start=False, stop=(hp == 1))
            last.then_inc(*g_done.up())
            e.wait_ge(*g_neg.at(c + 1))
            for j in range(J):
                for hp in range(2):
                    u = 4 * j + 2 * tt + hp
                    h0 = j * P + 64 * hp
                    xt = XT[:, u // 4, (u % 4) * P + pb:(u % 4) * P + pb + CH]
                    last = nc.tensor.matmul(ps[tok, 1, h0:h0 + 64], xt, GS[:, h0:h0 + 64], start=True, stop=True)
            last.then_inc(*u_done.up())
            e.wait_ge(*u_copied.at(c + 1))
            if c >= 2:
                e.wait_ge(*o_copied.at(c - 1))
            ob, db = 2 + c % 2, 4 + c % 2
            for j in range(J):
                nc.tensor.matmul(ps[:, ob, j * CH:(j + 1) * CH], S[:, j, :], AR[:, j, tt, 1, tok], start=True, stop=False)
                for hp in range(2):
                    u = 4 * j + 2 * tt + hp
                    h0 = j * P + 64 * hp
                    out = ps[64 * hp:64 * hp + 64, ob, j * CH:(j + 1) * CH]
                    nc.tensor.matmul(out, US[:, h0:h0 + 64], PB[:, u, P + pb:P + pb + CH], start=False, stop=False)
                    last = nc.tensor.matmul(out, VN[:, tt, h0:h0 + 64], PK[:, u, P + pb:P + pb + CH],
                                            start=False, stop=True)
            last.then_inc(*o_done.up())
            if c < NCH - 1:
                for j in range(J):
                    cols = slice(j * P, (j + 1) * P)
                    nc.tensor.matmul(ps[:, db, cols], BN[tok, tt, cols], US[tok, cols], start=True, stop=False)
                    last = nc.tensor.matmul(ps[:, db, cols], KN[tok, tt, cols], VN[tok, tt, cols], start=False, stop=True)
                last.then_inc(*s_done.up())

    def act(e):
        e.wait_ge(*cleared.at(3))
        for c in range(NCH):
            tt, pb = split(c)
            tok = slice(pb, pb + CH)
            e.wait_ge(*g_done.at(c + 1))
            nc.scalar.activation(GS[tok, :], ps[tok, 0, :], ACT.Copy, scale=-1.0).then_inc(*g_neg.up())
            e.wait_ge(*u_done.at(c + 1))
            nc.scalar.activation(US[tok, :], ps[tok, 1, :], ACT.Copy).then_inc(*u_copied.up())
            e.wait_ge(*o_done.at(c + 1))
            nc.scalar.activation(O[:, :, tt * P + pb:tt * P + pb + CH],
                                 ps[:, 2 + c % 2, 0:J * CH].rearrange("p (j n) -> p j n", j=J), ACT.Copy)\
                .then_inc(*o_copied.up())

    def dve(e):
        nc.vector.memset(S, 0.0).then_inc(*cleared.up())
        nc.vector.memset(GS, 0.0).then_inc(*cleared.up())
        nc.vector.memset(US, 0.0).then_inc(*cleared.up())
        for c in range(NCH - 1):
            e.wait_ge(*s_done.at(c + 1))
            for hp in range(2):
                r = slice(64 * hp, 64 * hp + 64)
                own = S[r, :, 64 * hp:64 * hp + 64]
                new = ps[r, 4 + c % 2, :].rearrange("p (j n) -> p j n", j=J)[:, :, 64 * hp:64 * hp + 64]
                core.link(e, "dve", nc.vector.tensor_tensor(own, own, new, ALU.add))
                last = nc.vector.tensor_tensor(own, own, bc(PC[r, :, c], 2, 64), ALU.mult)
                if hp == 0:
                    core.link(e, "dve", last)
            last.then_inc(*s_new.up())
    stage(core, pe=pe, act=act, dve=dve)


def head_norm(core, O, BON, G, col, sq):
    nc, ps, c = core.nc, core.ps, core.c
    J = RW // P
    flat = lambda b: b.rearrange("p a t -> p (a t)")
    mean, squares, var, root = (core.sig(f"head_{n}") for n in ("mean", "squares", "variance", "root"))
    two = lambda b: ps[:, b:b + 2, :].rearrange("p b n -> p (b n)")

    def pe(e):
        for src, bank, s in ((O, 0, mean), (sq, 2, var)):
            if bank:
                e.wait_ge(*squares.at(1))
            for j in range(J):
                last = nc.tensor.matmul(ps[:, bank + j // 2, (j % 2) * T:(j % 2 + 1) * T], c("mean64"), src[:, j, :],
                                        start=True, stop=True)
            last.then_inc(*s.up())

    def act(e):
        e.wait_ge(*var.at(1))
        nc.scalar.activation(flat(sq), two(2), ACT.Sqrt, bias=c("eps")[:, E_GN:E_GN + 1]).then_inc(*root.up())

    def dve(e):
        e.wait_ge(*mean.at(1))
        core.link(e, "dve", nc.vector.tensor_tensor(flat(O), flat(O), two(0), ALU.subtract))
        nc.vector.tensor_tensor(flat(sq), flat(O), flat(O), ALU.mult).then_inc(*squares.up())
        e.wait_ge(*root.at(1))
        core.link(e, "dve", nc.vector.reciprocal(flat(sq), flat(sq)))
        core.link(e, "dve", nc.vector.tensor_tensor(flat(O), flat(O), flat(sq), ALU.mult))
        for j in range(J):
            last = nc.vector.tensor_scalar(O[:, j, :], O[:, j, :], col("rw_ln_w_2", j), col("rw_ln_b_2", j), ALU.mult, ALU.add)
        core.link(e, "dve", last)
        core.link(e, "dve", nc.vector.tensor_tensor(flat(O), flat(O), flat(BON), ALU.add))
        nc.vector.tensor_tensor(flat(O), flat(O), flat(G), ALU.mult)
    stage(core, pe=pe, act=act, dve=dve)


def s5(core, l0, col, UT, Y):
    nc, a, ps, c = core.nc, core.a, core.ps, core.c
    link = core.link
    f16 = lambda off: a(off, ST)
    COS, SIN = (a(off, ST * T).rearrange("p (s t) -> p s t", t=T) for off in (3072, 7168))
    b_re, b_im = (a(off, ST * SG).rearrange("p (s i) -> p s i", i=SG) for off in (11264, 11520))
    bd = [a(off, ST * 32).rearrange("p (s n) -> p s n", n=32) for off in (11776, 12544)]
    bdT = [a(off, 4 * P).rearrange("p (c n) -> p c n", c=4) for off in (13056, 13568)]
    cn = [a(off, 4 * 64).rearrange("p (c n) -> p c n", c=4) for off in (14080, 14336)]
    cpad = [a(off, 4 * P).rearrange("p (c g n) -> p c g n", c=4, g=2) for off in (14592, 15104)]
    cT = [a(off, 4 * P).rearrange("p (c n) -> p c n", c=4) for off in (15616, 16128, 16640)]
    W = 17152
    (dt, re, im, rho, n_, r_, h_, ah, sh, ch, co, si, t1, t2, nr, ni, den, cr, ci, qc, qs, qc2, qs2) = (
        f16(23552 + ST * i) for i in range(23))
    landed = core.sig("s5_landed")
    ex, ang, trig, made, turned = (core.sig(f"s5_{n}") for n in ("exps", "angles", "trig", "made", "turned"))

    def sp(e):
        for dst, name in ((b_re, "s5_b_re_2"), (b_im, "s5_b_im_2")):
            e.dma_start(dst, l0[name].rearrange("(s g) p i -> (g p) s i", g=2)).then_inc(*landed.up(16))
        for dst, name in ((cn[0], "s5_c_re_2"), (cn[1], "s5_c_im_2")):
            e.dma_start(dst, l0[name].rearrange("(c g) i p -> (g i) c p", g=8)).then_inc(*landed.up(16))

    def span(name):
        first = col(name, 0)
        return bass.AP(first.tensor, first.offset, [list(first.ap[0]), [1, ST]])
    lam_re, lam_im, log_dt = span("s5_lam_re_2"), span("s5_lam_im_2"), span("s5_log_dt_2")
    MAGIC = 1.5 * 2 ** 23
    PI_HI = float(np.float32(6.28125))
    PI_LO = 2 * math.pi - PI_HI

    def act(e):
        nc.scalar.activation(dt, log_dt, ACT.Exp).then_inc(*ex.up())
        e.wait_ge(*ang.at(1))
        nc.scalar.activation(rho, re, ACT.Exp).then_inc(*ex.up())
        e.wait_ge(*ang.at(2))
        nc.scalar.activation(sh, h_, ACT.Sin).then_inc(*trig.up())
        e.wait_ge(*ang.at(3))
        nc.scalar.activation(ch, ah, ACT.Sin, scale=-1.0, bias=c("eps")[:, E_HALFPI:E_HALFPI + 1]).then_inc(*trig.up())
        for i in range(2):
            e.wait_ge(*turned.at(i + 1))
            nc.scalar.activation(bdT[i].rearrange("p c n -> p (c n)"), ps[:, i, :], ACT.Copy)
        e.wait_ge(*turned.at(3))
        nc.scalar.activation(cT[0].rearrange("p c n -> p (c n)"), ps[:, 2, :], ACT.Copy)
        nc.scalar.activation(cT[2].rearrange("p c n -> p (c n)"), ps[:, 2, :], ACT.Copy, scale=-1.0)
        e.wait_ge(*turned.at(4))
        nc.scalar.activation(cT[1].rearrange("p c n -> p (c n)"), ps[:, 3, :], ACT.Copy, scale=-1.0)

    def pe(e):
        for i in range(2):
            e.wait_ge(*made.at(i + 1))
            for ct in range(4):
                last = nc.tensor.transpose(ps[:, i, ct * P:(ct + 1) * P],
                                           bd[i][:, 4 * ct:4 * ct + 4, :].rearrange("p s n -> p (s n)"), c("ident"))
            last.then_inc(*turned.up())
        for i in range(2):
            e.wait_ge(*made.at(i + 3))
            for ct in range(4):
                last = nc.tensor.transpose(ps[:, 2 + i, ct * P:(ct + 1) * P],
                                           cpad[i][:, ct, :, :].rearrange("p g n -> p (g n)"), c("ident"))
            last.then_inc(*turned.up())

    V = nc.vector
    tt_ = lambda e, o, x0, x1, op: link(e, "dve", V.tensor_tensor(o, x0, x1, op))
    ts_ = lambda e, o, x0, s1, s2, o0, o1=ALU.bypass: link(e, "dve", V.tensor_scalar(o, x0, s1, s2, o0, o1))

    def dve(e):
        e.wait_ge(*ex.at(1))
        V.tensor_tensor(re, lam_re, dt, ALU.mult).then_inc(*ang.up())
        tt_(e, im, lam_im, dt, ALU.mult)
        ts_(e, n_, im, 1 / (2 * math.pi), MAGIC, ALU.mult, ALU.add)
        ts_(e, n_, n_, MAGIC, None, ALU.subtract)
        link(e, "dve", V.scalar_tensor_tensor(r_, n_, -PI_HI, im, ALU.mult, ALU.add))
        link(e, "dve", V.scalar_tensor_tensor(r_, n_, -PI_LO, r_, ALU.mult, ALU.add))
        V.tensor_scalar(h_, r_, 0.5, None, ALU.mult).then_inc(*ang.up())
        e.wait_ge(*ang.at(2))
        link(e, "dve", V.tensor_scalar(ah, h_, -1.0, None, ALU.mult))
        V.tensor_tensor(ah, ah, h_, ALU.max).then_inc(*ang.up())
        e.wait_ge(*trig.at(2))
        tt_(e, si, sh, ch, ALU.mult)
        ts_(e, si, si, 2.0, None, ALU.mult)
        tt_(e, co, sh, sh, ALU.mult)
        ts_(e, co, co, -2.0, 1.0, ALU.mult, ALU.add)
        e.wait_ge(*ex.at(2))
        tt_(e, nr, rho, co, ALU.mult)
        ts_(e, nr, nr, -1.0, None, ALU.add)
        tt_(e, ni, rho, si, ALU.mult)
        tt_(e, t1, lam_re, lam_re, ALU.mult)
        tt_(e, t2, lam_im, lam_im, ALU.mult)
        tt_(e, den, t1, t2, ALU.add)
        link(e, "dve", V.reciprocal(den, den))
        tt_(e, t1, nr, lam_re, ALU.mult)
        tt_(e, t2, ni, lam_im, ALU.mult)
        tt_(e, cr, t1, t2, ALU.add)
        tt_(e, cr, cr, den, ALU.mult)
        tt_(e, t1, ni, lam_re, ALU.mult)
        tt_(e, t2, nr, lam_im, ALU.mult)
        tt_(e, ci, t1, t2, ALU.subtract)
        tt_(e, ci, ci, den, ALU.mult)
        e.wait_ge(*landed.at(64))
        w1, w2 = (a(W + i * 256, 256).rearrange("p (s i) -> p s i", i=SG) for i in range(2))
        wide = lambda v: bc(v, 2, SG)
        for i, (x1, x2, op) in enumerate(((b_re, b_im, ALU.subtract), (b_im, b_re, ALU.add))):
            link(e, "dve", V.memset(bd[i], 0.0))
            tt_(e, w1, x1, wide(cr), ALU.mult)
            tt_(e, w2, x2, wide(ci), ALU.mult)
            for g in range(2):
                r = slice(64 * g, 64 * g + 64)
                last = V.tensor_tensor(bd[i][r, :, SG * g:SG * g + SG], w1[r], w2[r], op)
                if g == 0:
                    link(e, "dve", last)
            last.then_inc(*made.up())
            e.wait_ge(*made.at(i + 1))
        for i in range(2):
            for g in range(2):
                last = V.tensor_scalar(cpad[i][:, :, g, :], cn[i], c("parity")[:, g:g + 1], None, ALU.mult)
                if g == 0:
                    link(e, "dve", last)
            last.then_inc(*made.up())
        tmp = [a(W + i * 2048, ST * 128) for i in range(2)]
        link(e, "dve", V.memset(COS[:, :, 0:1], 1.0))
        link(e, "dve", V.memset(SIN[:, :, 0:1], 0.0))
        q, q2 = (co, si), (qc, qs)
        n = 1
        while n < T:
            x1, x2 = (t[:, 0:ST * n].rearrange("p (s n) -> p s n", n=n) for t in tmp)
            qc_, qs_ = bc(q[0], 2, n), bc(q[1], 2, n)
            tt_(e, x1, COS[:, :, 0:n], qc_, ALU.mult)
            tt_(e, x2, SIN[:, :, 0:n], qs_, ALU.mult)
            tt_(e, COS[:, :, n:2 * n], x1, x2, ALU.subtract)
            tt_(e, x1, COS[:, :, 0:n], qs_, ALU.mult)
            tt_(e, x2, SIN[:, :, 0:n], qc_, ALU.mult)
            tt_(e, SIN[:, :, n:2 * n], x1, x2, ALU.add)
            tt_(e, t1, q[0], q[0], ALU.mult)
            tt_(e, t2, q[1], q[1], ALU.mult)
            tt_(e, q2[0], t1, t2, ALU.subtract)
            tt_(e, t1, q[0], q[1], ALU.mult)
            ts_(e, q2[1], t1, 2.0, None, ALU.mult)
            q, q2 = q2, ((qc2, qs2) if q2[0] is qc else (qc, qs))
            n *= 2
    stage(core, sp=sp, pe=pe, act=act, dve=dve)

    M1, M2, VV, ZZ = (a(W + i * 1024, 1024).rearrange("p (b n) -> p b n", b=2) for i in range(4))
    N1, N2 = (a(W + 4096 + i * 1024, 1024).rearrange("p (b n) -> p b n", b=2) for i in range(2))
    proj, rot, added, back, ysum, ypre = (core.sig(f"s5_{n}") for n in
                                          ("projected", "rotated", "summed", "back", "outputs", "with_skip"))

    def pe(e):
        for s in range(ST + 1):
            if s < ST:
                ct, j = s // 4, s % 4
                if s >= 4:
                    e.wait_ge(*rot.at(s - 3))
                rows = slice(32 * j, 32 * j + 32)
                for i in range(2):
                    last = nc.tensor.matmul(ps[:, j, i * T:(i + 1) * T], bdT[i][rows, ct, :], UT[rows, ct, :],
                                            start=True, stop=True)
                last.then_inc(*proj.up())
            if s >= 1:
                m = s - 1
                ct, j = m // 4, m % 4
                e.wait_ge(*back.at(m + 1))
                out = ps[32 * j:32 * j + 32, 4 + ct, 0:T]
                cols = slice(32 * j, 32 * j + 32)
                terms = ((cT[0], N1, 0), (cT[2], N2, 1), (cT[1], N1, 1), (cT[1], N2, 0))
                for k, (w_, src, part) in enumerate(terms):
                    last = nc.tensor.matmul(out, w_[:, ct, cols], src[:, m % 2, part * T:(part + 1) * T],
                                            start=(k == 0), stop=(k == 3))
                last.then_inc(*ysum.up())

    def pool(e):
        for s in range(ST):
            e.wait_ge(*rot.at(s + 1))
            if s >= 2:
                e.wait_ge(*back.at(s - 1))
            b = s % 2
            nc.gpsimd.tensor_tensor(VV[:, b, 0:T], M1[:, b, 0:T], M2[:, b, T:2 * T], ALU.add)
            nc.gpsimd.tensor_tensor(VV[:, b, T:2 * T], M1[:, b, T:2 * T], M2[:, b, 0:T], ALU.subtract).then_inc(*added.up())

    def dve(e):
        two = lambda v, s: bc(v[:, s, :], 1, 2)
        half = lambda v, b: v[:, b, :].rearrange("p (i t) -> p i t", i=2)
        for s in range(ST + 1):
            if s < ST:
                e.wait_ge(*proj.at(s + 1))
                if s >= 2:
                    e.wait_ge(*added.at(s - 1))
                pb = ps[:, s % 4, :].rearrange("p (i t) -> p i t", i=2)
                V.tensor_tensor(half(M1, s % 2), two(COS, s), pb, ALU.mult)
                V.tensor_tensor(half(M2, s % 2), two(SIN, s), pb, ALU.mult).then_inc(*rot.up())
            if s >= 1:
                m = s - 1
                b = m % 2
                e.wait_ge(*added.at(m + 1))
                decay = rho[:, m:m + 1].broadcast_to([P, T])
                V.tensor_tensor_scan(ZZ[:, b, 0:T], decay, VV[:, b, 0:T], 0.0, ALU.mult, ALU.add)
                link(e, "dve", V.tensor_tensor_scan(ZZ[:, b, T:2 * T], decay, VV[:, b, T:2 * T], 0.0, ALU.mult, ALU.add))
                if m >= 2:
                    e.wait_ge(*ysum.at(m - 1))
                V.tensor_tensor(half(N1, b), two(COS, m), half(ZZ, b), ALU.mult)
                V.tensor_tensor(half(N2, b), two(SIN, m), half(ZZ, b), ALU.mult).then_inc(*back.up())
        for ct in range(4):
            e.wait_ge(*ysum.at(4 * ct + 4))
            V.scalar_tensor_tensor(Y[:, ct, :], UT[:, ct, :], col("s5_d_2", ct), ps[:, 4 + ct, 0:T], ALU.mult, ALU.add)\
                .then_inc(*ypre.up())

    def act(e):
        for ct in range(4):
            e.wait_ge(*ypre.at(ct + 1))
            nc.scalar.activation(Y[:, ct, :], Y[:, ct, :], ACT.Gelu_apprx_tanh)
    stage(core, pe=pe, act=act, dve=dve, pool=pool)

    freed = core.sig("bank_copied")
    gate = a(W, 4 * T).rearrange("p (n t) -> p n t", t=T)

    def pe(e):
        raw_features(core, e, 0, Y, 4, 1, freed, 0, 4, core.taken)

    def act(e):
        for u in range(2):
            core.wait_bank(e, u)
            for h in range(2):
                j = 2 * u + h
                nc.scalar.activation(gate[:, j, :], ps[:, u, h * T:(h + 1) * T], ACT.Sigmoid, bias=col("s5_b_glu_2", j))\
                    .then_inc(*freed.up())

    def dve(e):
        core.wait_bank(e, 1)
        e.wait_ge(*freed.at(4))
        V.tensor_tensor(Y.rearrange("p a t -> p (a t)"), Y.rearrange("p a t -> p (a t)"),
                        gate.rearrange("p a t -> p (a t)"), ALU.mult)
    stage(core, pe=pe, act=act, dve=dve, uses=1)


def program(nc, w, consts, const_at, out):
    core = Core(nc, const_at)
    c, a, ps, x = core.c, core.a, core.ps, core.x
    sig, link = core.sig, core.link
    l0 = {k: (v[0] if v.shape[0] == 1 else v) for k, v in w.items() if len(v.shape) > 1}

    tiles = core.tiles
    def qkv_tiles(wq, wkv, k0):
        return feature_tiles(wq, 0, D) + feature_tiles(wkv, k0, k0 + D) + token_tiles(wkv, k0 + D, k0 + 2 * D)

    def xattn_tiles(l):
        return qkv_tiles(w["xa_w_q_2"][l], w["xa_w_kv_2"][l], 0) + token_tiles(w["xa_w_o_2"][l])

    tiles += qkv_tiles(l0["moba_w_qkv"], l0["moba_w_qkv"], D) + token_tiles(l0["moba_w_o"])
    tiles += mlp_tiles([w["mlp_w_up"][0]], w["mlp_w_down"][0])
    tiles += feature_tiles(l0["dsa_w_in"], 0, 512) + feature_tiles(l0["dsa_w_in"], 512, 584)
    tiles += feature_tiles(l0["dsa_w_uq"], width=512, raw=True) + feature_tiles(l0["dsa_w_qi"], width=512, raw=True)
    tiles += token_tiles(l0["dsa_w_o"])
    tiles += mlp_tiles([w["mlp_w_up"][1]], w["mlp_w_down"][1])
    tiles += feature_tiles(l0["hy_w_in_2"], 0, RWKV_COLS) + feature_tiles(l0["hy_w_in_2"], RWKV_COLS, RWKV_COLS + RW)
    tiles += feature_tiles(l0["s5_w_glu_2"], width=512, raw=True) + token_tiles(l0["hy_w_out_2"])
    tiles += xattn_tiles(0)
    tiles += mlp_tiles([l0["ff_w_gate_2"], l0["ff_w_up_2"]], l0["ff_w_down_2"])
    tiles += qkv_tiles(l0["da_w_qkv_2"], l0["da_w_qkv_2"], D) + token_tiles(l0["da_w_o_2"])
    tiles += xattn_tiles(1)
    tiles += [(expert_tile(l0, 0, j), True) for j in range(RING)]

    col_at, loads = {}, []
    place = [0, 0]

    def vector(name, ap, which):
        n = ap.shape[0]
        full = n // P
        r = place[which]
        col_at[name] = (which, r)
        if full:
            loads.append((core.rows[r:r + full, which, :], ap[0:full * P].rearrange("(r p) -> r p", p=P)))
        if n % P:
            loads.append((core.rows[r + full:r + full + 1, which, 0:n % P], ap[full * P:n].rearrange("(r p) -> r p", r=1)))
        place[which] += full + (n % P > 0)

    for name in ("ln_attn", "ln_mlp", "norm_mix_2", "norm_xattn_2", "norm_mem_2", "norm_ffn_2"):
        vector(name, w[name].rearrange("l d -> (l d)"), 0)
    vector("dsa_g_q", l0["dsa_g_q"], 0)
    vector("dsa_g_kv", l0["dsa_g_kv"], 0)
    vector("xa_q_gain_2", w["xa_q_gain_2"].rearrange("l d -> (l d)"), 0)
    vector("xa_k_gain_2", w["xa_k_gain_2"].rearrange("l d -> (l d)"), 0)
    vector("da_sub_gain_2", l0["da_sub_gain_2"], 0)
    for name in ("rw_w0_2", "rw_a0_2", "rw_k_k_2", "rw_k_a_2"):
        vector(name, l0[name], 0)
    mu = l0["rw_mu_2"]
    vector("mu", mu[0:3 * RW + 128], 1)
    vector("mu_g", mu[3 * RW + 128:RWKV_COLS], 1)
    vector("rw_r_k_2", l0["rw_r_k_2"].rearrange("h d -> (h d)"), 1)
    for name in ("rw_ln_w_2", "rw_ln_b_2", "s5_d_2", "s5_b_glu_2"):
        vector(name, l0[name], 1)
    vector("s5_lam_re_2", l0["s5_lam_re_2"].rearrange("g p -> (g p)"), 1)
    vector("s5_lam_im_2", l0["s5_lam_im_2"].rearrange("g p -> (g p)"), 1)
    for name in ("da_q_gain_2", "da_k_gain_2"):
        r = place[1]
        col_at[name] = (1, r)
        for half in range(2):
            loads.append((core.rows[r:r + 1, 1, half * 64:(half + 1) * 64], w[name]))
        place[1] += 1
    col_at["s5_log_dt_2"] = (1, 96)
    assert place[0] <= P and place[1] <= 96

    def col(name, k=0):
        which, r = col_at[name]
        return core.cols[:, which, r + k:r + k + 1]

    def at_col(name, k=0):
        which, r = col_at[name]
        return (which, r + k)

    lam_sb = nc.alloc_sbuf_tensor("lam", [P, 4, 64], F32)
    dt_rows = nc.alloc_sbuf_tensor("dt_rows", [P, 2], F32)
    relb = nc.alloc_sbuf_tensor("relb", [NBUCKET, H], F32)
    small = nc.alloc_sbuf_tensor("small", [P, 96], F32)
    toep = nc.alloc_sbuf_tensor("toep", [P, H, T], F32)
    ext_dram = nc.dram_tensor("bias_rows", [H, P, CAUS], F32, kind="Internal").ap()
    BIAS_SB = 8192
    ext_sb = a(BIAS_SB, CAUS)

    def dve(e):
        nc.vector.memset(core.rows[:, :, :], 0.0)
    stage(core, dve=dve)

    ready = sig("inputs_landed")

    def sp(e):
        e.dma_start(core.const[:, :], consts).then_inc(*ready.up(16))
        e.dma_start(x[:, :, :], w["x"][0].rearrange("(t p) d -> p t d", p=P)).then_inc(*ready.up(16))
        e.dma_start(relb[:, :], w["rel_bias"]).then_inc(*ready.up(16))
        for i, name in enumerate(("da_lam_q1_2", "da_lam_k1_2", "da_lam_q2_2", "da_lam_k2_2")):
            e.dma_start(lam_sb[:, i, :], w[name][0].partition_broadcast(P)).then_inc(*ready.up(16))
        e.dma_start(dt_rows[0:16, :], l0["s5_log_dt_2"].rearrange("(r g) -> r g", g=2)).then_inc(*ready.up(16))
        for dst, src in loads:
            e.dma_start(dst, src).then_inc(*ready.up(16))
        core.issue(e, RING)
        e.wait_ge(ready.sem, ready.total)
    stage(core, sp=sp)

    turned, extd, dt_ok = sig("params_turned"), sig("bias_rows_ready"), sig("dt_spread")
    bias_written, bias_read = sig("bias_rows_written"), sig("bias_landed")
    dt_wide = a(BIAS_SB + 1024, P).rearrange("p (g s) -> p g s", g=2)

    def pe(e):
        nc.tensor.matmul(ps[0:H, 0, 0:CAUS], relb[:, :], c("onehot")[0:NBUCKET, :], start=True, stop=True)\
            .then_inc(*turned.up())
        nc.tensor.transpose(ps[:, 1, 0:P], core.rows[:, 0, :], c("ident")).then_inc(*turned.up())
        nc.tensor.transpose(ps[:, 2, 0:P], core.rows[:, 1, :], c("ident")).then_inc(*turned.up())
        e.wait_ge(*dt_ok.at(1))
        nc.tensor.transpose(ps[:, 3, 0:16], dt_wide[0:16, :, :].rearrange("p g s -> p (g s)"),
                            c("ident")[0:16, 0:16]).then_inc(*turned.up())

    def dve(e):
        nc.vector.tensor_copy(dt_wide[0:16, :, :], bc(dt_rows[0:16, :], 2, 64)).then_inc(*dt_ok.up())
        e.wait_ge(*turned.at(1))
        nc.vector.tensor_tensor(ext_sb[0:H, :], ps[0:H, 0, 0:CAUS], c("future")[0:H, :], ALU.add)\
            .then_inc(*extd.up())
        e.wait_ge(*turned.at(2))
        nc.vector.tensor_copy(core.cols[:, 0, :], ps[:, 1, 0:P])
        e.wait_ge(*turned.at(3))
        nc.vector.tensor_copy(core.cols[:, 1, 0:96], ps[:, 2, 0:96])
        e.wait_ge(*turned.at(4))
        nc.vector.tensor_copy(core.cols[:, 1, 96:112], ps[:, 3, 0:16])

    def sp(e):
        e.wait_ge(*extd.at(1))
        e.dma_start(ext_dram.rearrange("h r n -> h r n"), bc(ext_sb[0:H, :], 1, P)).then_inc(*bias_written.up(16))
    stage(core, sp=sp, pe=pe, dve=dve)

    ws_guard = core.scoped("weights_split", [P, WS_BUFS, 2, SLOT], F32R)
    core.WS = ws_guard.__enter__()

    def read_bias(e):
        e.wait_ge(*bias_written.at(0))
        skew = bass.AP(ext_dram.tensor, ext_dram.offset + P - 1, [[CAUS - 1, P], [P * CAUS, H], [1, T]])
        e.dma_start(toep[:, :, :], skew).then_inc(*bias_read.up(16))

    freed = sig("bank_copied")

    QT, KT_, VN, OT, SCR = 0, 2048, 4096, 6144, 8192

    def view(off, n):
        return a(off, n * T).rearrange("p (n t) -> p n t", t=T)

    def copy_bank(e, eng, dst, bank, scale=None):
        src = ps[:, bank, :]
        if eng == "act":
            return nc.scalar.activation(dst, src, ACT.Copy, scale=1.0 if scale is None else scale)
        return nc.vector.tensor_scalar(dst, src, 1.0 if scale is None else scale, None, ALU.mult)

    def pairs(buf, u):
        return buf[:, 2 * u:2 * u + 2, :].rearrange("p a t -> p (a t)")

    def rows64(buf):
        return lambda u: buf[64 * (u % 2):64 * (u % 2) + 64, u // 2, :]

    def first_attention(before_dve_bias, sel=None):
        qT, kT, oT = view(QT, 8), view(KT_, 8), view(OT, 8)
        vN = a(VN, 2 * D).rearrange("p (t d) -> p t d", t=TT)
        q, k = rows64(qT), rows64(kT)
        masked = sig("bias_masked")
        tmp = None if sel is None else dsa[:, 0:2 * CAUS].rearrange("p (b n) -> p b n", b=2)

        def bias(e, u):
            if u == 0 and before_dve_bias:
                e.wait_ge(*bias_read.at(0))
            if sel is None:
                return toep[:, u, P:T], toep[:, u, :]
            e.wait_ge(*masked.at(u + 1))
            return tmp[:, u % 2, 0:P], tmp[:, u % 2, P:CAUS]

        pe, act, dve = attention(core, H, 1, lambda u, tt: [q(u)[:, tt * P:(tt + 1) * P]],
                                 lambda u, n: [k(u)[:, 0:n]], lambda h: h * DH, DH, True, bias, vN, oT, SCR)

        def pool(e):
            for u in range(H):
                if u >= 2:
                    e.wait_ge(*sig("attn_negmax").at(u - 1))
                nc.gpsimd.tensor_tensor(tmp[:, u % 2, 0:P], toep[:, u, P:T], sel[:, 0:P], ALU.add)
                nc.gpsimd.tensor_tensor(tmp[:, u % 2, P:CAUS], toep[:, u, :], sel[:, P:CAUS], ALU.add)\
                    .then_inc(*masked.up())
        stage(core, pe=pe, act=act, dve=dve, pool=pool if sel is not None else None)

    norm_stage(core, x, core.XS, at_col("ln_attn"), 0, extra_sp=read_bias)

    qk = view(QT, 16)
    vN = a(VN, 2 * D).rearrange("p (t d) -> p t d", t=TT)
    xs = halves(core.XS)
    qkv_products(core, xs, xs, qk, vN, DH ** -0.5)
    first_attention(True)
    project(core, view(OT, 8))
    norm_stage(core, x, core.XS, at_col("ln_mlp"), 0)
    mlp(core, DFF // NF, False)

    dsa_guard = core.scoped("dsa", [P, 4096])
    dsa = dsa_guard.__enter__()
    uk_n = a(8192, 8 * 256).rearrange("p (r c) -> p r c", r=8)
    uv = a(10240, 2 * D).rearrange("p (k h d) -> p k h d", k=2, h=H)
    lat_landed = sig("latent_weights_landed")

    def sp(e):
        e.dma_start(uk_n, l0["dsa_w_uk"].rearrange("(r a) d c -> (a d) r c", a=2)).then_inc(*lat_landed.up(16))
        for k in range(2):
            e.dma_start(uv[:, k, :, :], l0["dsa_w_uv"][:, k * P:(k + 1) * P, :].rearrange("h c d -> c h d"))\
                .then_inc(*lat_landed.up(16))
    norm_stage(core, x, core.XS, at_col("ln_attn", 8), 0, extra_sp=sp)

    sview = lambda off, n: dsa[:, off:off + n * T].rearrange("p (n t) -> p n t", t=T)
    cqkv = sview(2048, 4)
    kiT = a(12288, T)
    wi = small[:, 0:2 * IDXH].rearrange("p (t h) -> p t h", t=TT)

    def pe(e):
        t0 = core.taken
        u, tile = features_matmul(core, e, 0, xs, KD, 2, freed, 0, 4, t0)
        wt = core.weights(e, tile)
        for k in range(KD):
            last = product(core, ps[0:64, 2, 0:T], wt, (ALL, k, slice(0, 64)), xs, (ALL, k, ALL), k == 0, k == KD - 1)
        core.fill(last, bank=True)
        for tt in range(TT):
            for k in range(KD):
                last = product(core, ps[:, 3, tt * 8:tt * 8 + 8], wt, (ALL, k, slice(64, 72)),
                               xs, (ALL, k, slice(tt * P, (tt + 1) * P)), k == 0, k == KD - 1, tokens=True)
        core.fill(last, bank=True, tile=True)

    def act(e):
        t0 = core.taken
        for i in range(3):
            core.hi(e, t0 + i + 1 + WS_BUFS)
            core.wait_bank(e, i)
            if i < 2:
                copy_bank(e, "act", pairs(cqkv, i), i)
            else:
                for half in range(2):
                    nc.scalar.activation(kiT[half * 64:(half + 1) * 64, :], ps[0:64, 2, 0:T], ACT.Copy)
        core.wait_bank(e, 3)
        nc.scalar.activation(wi.rearrange("p t h -> p (t h)"), ps[:, 3, 0:16], ACT.Copy,
                             scale=IDXH ** -0.5 * 64 ** -0.5)

    def dve(e):
        for i in range(3):
            core.lo(e, core.taken + i + 1 + WS_BUFS)
    stage(core, pe=pe, act=act, dve=dve, uses=3)

    sq = a(0, 1024).rearrange("p (b n) -> p b n", b=2)
    root = a(1024, 1024).rearrange("p (b n) -> p b n", b=2)
    gpe, gact, gdve = grouped_norm(core, cqkv, 4, c("mean256"), 2, 1.0, E_EPS,
                                   lambda j: col("dsa_g_q", j) if j < 2 else col("dsa_g_kv", j - 2), sq, root)
    ukT = dsa[:, 0:2 * D].rearrange("p (k n) -> p k n", k=2)
    uk_turned = sig("uk_turned")

    def pe(e):
        gpe(e)
        e.wait_ge(*lat_landed.at(0))
        for k in range(2):
            for b in range(2):
                for j in range(4):
                    r = 4 * b + j
                    last = nc.tensor.transpose(ps[:, 4 + 2 * k + b, j * P:(j + 1) * P], uk_n[:, r, k * P:(k + 1) * P],
                                               c("ident"))
                last.then_inc(*uk_turned.up())

    def act(e):
        gact(e)
        for k in range(2):
            for b in range(2):
                e.wait_ge(*uk_turned.at(2 * k + b + 1))
                nc.scalar.activation(ukT[:, k, b * 512:(b + 1) * 512], ps[:, 4 + 2 * k + b, :], ACT.Copy)
    stage(core, pe=pe, act=act, dve=gdve)

    qT, kT = view(QT, 8), view(KT_, 8)
    vN = a(VN, 2 * D).rearrange("p (t d) -> p t d", t=TT)
    qiT = sview(3072, 4)

    def pe(e):
        cq, ckv = cqkv[:, 0:2, :], cqkv[:, 2:4, :]
        u, tile = raw_features(core, e, 0, cq, 2, 3, freed, 0, 8, core.taken)
        for b in range(4):
            if u >= 8:
                e.wait_ge(*freed.at(u - 7))
            for j in range(2):
                for k in range(2):
                    last = nc.tensor.matmul(ps[:, u % 8, j * T:(j + 1) * T], ukT[:, k, (2 * b + j) * P:(2 * b + j + 1) * P],
                                            ckv[:, k, :], start=(k == 0), stop=(k == 1))
            core.fill(last, bank=True)
            u += 1
        for half in range(2):
            for tt in range(TT):
                e.wait_ge(*freed.at(u - 7))
                for k in range(2):
                    last = nc.tensor.matmul(ps[:, u % 8, :], ckv[:, k, tt * P:(tt + 1) * P],
                                            uv[:, k, half * 8:half * 8 + 8, :].rearrange("p h d -> p (h d)"),
                                            start=(k == 0), stop=(k == 1))
                core.fill(last, bank=True)
                u += 1

    def act(e):
        for u in range(14):
            core.wait_bank(e, u)
            if u < 4:
                dst, s = pairs(qT, u), DH ** -0.5
            elif u < 6:
                dst, s = pairs(qiT, u - 4), None
            elif u < 10:
                dst, s = pairs(kT, u - 6), None
            else:
                dst, s = vN[:, u % 2, ((u - 10) // 2) * NW:((u - 10) // 2 + 1) * NW], None
            copy_bank(e, "act", dst, u % 8, s).then_inc(*freed.up())
    stage(core, pe=pe, act=act, uses=3)

    score = a(8192, CAUS)
    work = a(8192 + CAUS, CAUS)
    relu = a(9216, 4 * T).rearrange("p (b n) -> p b n", b=4)
    best = a(10300, 16).rearrange("p (t n) -> p t n", t=2)
    sel = dsa[:, 1024:1024 + CAUS]
    spans = [(0, P), (P, T)]

    def pe(e):
        qi = rows64(qiT)
        for u in range(2 * IDXH):
            tt, h = u // IDXH, u % IDXH
            b0 = 64 * (h % 2)
            if u >= 4:
                e.wait_ge(*sig("relu_done").at(u - 3))
            nc.tensor.matmul(ps[:, u % 4, 0:spans[tt][1]], qi(h)[:, tt * P:(tt + 1) * P], kiT[b0:b0 + 64, 0:spans[tt][1]],
                             start=True, stop=True).then_inc(*sig("index_scores").up())

    def act(e):
        for u in range(2 * IDXH):
            e.wait_ge(*sig("index_scores").at(u + 1))
            if u >= 4:
                e.wait_ge(*sig("index_added").at(u - 3))
            n = spans[u // IDXH][1]
            nc.scalar.activation(relu[:, u % 4, 0:n], ps[:, u % 4, 0:n], ACT.Relu).then_inc(*sig("relu_done").up())

    def dve(e):
        added = sig("index_added")
        for u in range(2 * IDXH):
            tt, h = u // IDXH, u % IDXH
            lo, n = spans[tt]
            e.wait_ge(*sig("relu_done").at(u + 1))
            if h == 0:
                nc.vector.tensor_scalar(score[:, lo:lo + n], relu[:, u % 4, 0:n], wi[:, tt, h:h + 1], None, ALU.mult)\
                    .then_inc(*added.up())
            else:
                e.wait_ge(*added.at(u))
                nc.vector.scalar_tensor_tensor(score[:, lo:lo + n], relu[:, u % 4, 0:n], wi[:, tt, h:h + 1],
                                               score[:, lo:lo + n], ALU.mult, ALU.add).then_inc(*added.up())
        e.wait_ge(*added.at(2 * IDXH))
        link(e, "dve", nc.vector.tensor_tensor(score, score, c("seen"), ALU.mult))
        link(e, "dve", nc.vector.tensor_tensor(score, score, c("unseen"), ALU.add))
        src, dst = score, work
        for r in range(TOPK // 8):
            for tt in range(TT):
                lo, n = spans[tt]
                last = nc.vector.max(best[:, tt, :], src[:, lo:lo + n])
            link(e, "dve", last)
            for tt in range(TT):
                lo, n = spans[tt]
                last = nc.vector.match_replace(dst[:, lo:lo + n], best[:, tt, :], src[:, lo:lo + n], TAKEN)
            link(e, "dve", last)
            src, dst = dst, src
        nc.vector.tensor_scalar(sel, src, TAKEN, NEG, ALU.not_equal, ALU.mult)
    stage(core, pe=pe, act=act, dve=dve)

    first_attention(False, sel=sel)
    dsa_guard.__exit__(None, None, None)
    project(core, view(OT, 8))
    norm_stage(core, x, core.XS, at_col("ln_mlp", 8), 0)
    mlp(core, DFF // NF, False)

    gain_landed = sig("final_gain_landed")
    gain = a(0, D)

    def sp(e):
        e.dma_start(gain, w["final_norm"].partition_broadcast(P)).then_inc(*gain_landed.up(16))

    def act(e):
        for tt in range(TT):
            nc.scalar.activation(a(1024 * (1 + tt), D), x[:, tt, :], ACT.Square, accum_out=core.stat[:, tt:tt + 1])\
                .then_inc(*sig("norm_sums").up())
        e.wait_ge(*sig("norm_sums").at(2))
        nc.scalar.activation(core.stat[:, 2:4], core.stat[:, 0:2], ACT.Sqrt, scale=1.0 / D,
                             bias=c("eps")[:, E_EPS:E_EPS + 1]).then_inc(*sig("norm_root").up())

    def dve(e):
        e.wait_ge(*sig("norm_root").at(1))
        link(e, "dve", nc.vector.reciprocal(core.stat[:, 4:6], core.stat[:, 2:4]))
        e.wait_ge(gain_landed.sem, 16)
        for tt in range(TT):
            nc.vector.scalar_tensor_tensor(x[:, tt, :], x[:, tt, :], core.stat[:, 4 + tt:5 + tt], gain,
                                           ALU.mult, ALU.mult)
    stage(core, sp=sp, act=act, dve=dve)

    ws_guard = rwkv_s5(core, w, l0, col, at_col, small, ws_guard)

    cross_attention(core, w, 0, at_col, 8192)
    norm_stage(core, x, core.XS, at_col("norm_ffn_2"), 0)
    mlp(core, FF2 // NF, True)

    norm_stage(core, x, core.XS, at_col("norm_mix_2", 8), 0)
    qkv_products(core, xs, xs, qk, vN, None)
    sq = a(SCR, 1024).rearrange("p (b n) -> p b n", b=2)
    root = a(SCR + 1024, 1024).rearrange("p (b n) -> p b n", b=2)
    qpe, qact, qdve = grouped_norm(core, qk[:, 0:8, :], 8, c("mean64"), 1, 64.0, E_EPS64,
                                   lambda j: col("da_q_gain_2"), sq, root)

    def pool(e):
        for h in range(8):
            nc.gpsimd.tensor_scalar(toep[:, :, :].rearrange("p h t -> p (h t)")[:, h * CAUS:(h + 1) * CAUS],
                                    c("alibi"), 2.0 ** -(h + 1), None, ALU.mult).then_inc(*sig("alibi_made").up())

    def sp(e):
        e.wait_ge(*sig("alibi_made").at(8))
    stage(core, sp=sp, pe=qpe, act=qact, dve=qdve, pool=pool)
    kpe, kact, kdve = grouped_norm(core, qk[:, 8:16, :], 8, c("mean64"), 1, 1.0, E_EPS,
                                   lambda j: col("da_k_gain_2"), sq, root)
    stage(core, pe=kpe, act=kact, dve=kdve)

    lam_sums, lam_exp = sig("lambda_sums"), sig("lambda_exp")
    lam_neg = small[:, 90:91]

    def dve(e):
        for i in range(2):
            last = nc.vector.tensor_tensor_reduce(out=a(SCR, 64) if i == 0 else a(SCR + 64, 64), in0=lam_sb[:, 2 * i, :],
                                                  in1=lam_sb[:, 2 * i + 1, :], scale=1.0, scalar=0.0, op0=ALU.mult,
                                                  op1=ALU.add, accum_out=small[:, 80 + i:81 + i])
            last.then_inc(*lam_sums.up())
        e.wait_ge(*lam_exp.at(1))
        link(e, "dve", nc.vector.tensor_tensor(small[:, 84:85], small[:, 83:84], small[:, 82:83], ALU.subtract))
        nc.vector.tensor_scalar(lam_neg, small[:, 84:85], -LAMBDA_INIT, None, ALU.add)

    def act(e):
        e.wait_ge(*lam_sums.at(2))
        nc.scalar.activation(small[:, 82:84], small[:, 80:82], ACT.Exp).then_inc(*lam_exp.up())
    stage(core, act=act, dve=dve)

    alibi = toep[:, :, :].rearrange("p h t -> p (h t)")
    oT = view(OT, 8)
    q, k = qk[:, 0:8, :], qk[:, 8:16, :]

    def bias(e, u):
        h = u // 2
        return alibi[:, h * CAUS:h * CAUS + P], alibi[:, h * CAUS + P:(h + 1) * CAUS]
    pe, act, dve = attention(core, 8, 2, lambda u, tt: [q[64 * (u % 2):64 * (u % 2) + 64, u // 2, tt * P:(tt + 1) * P]],
                             lambda u, n: [k[64 * (u % 2):64 * (u % 2) + 64, u // 2, 0:n]], lambda h: h * P, P, True,
                             bias, vN, oT, SCR, lam=lam_neg)
    stage(core, pe=pe, act=act, dve=dve)
    s2 = 1.0 / (1.0 - LAMBDA_INIT) ** 2
    ope, oact, odve = grouped_norm(core, oT, 8, c("mean128"), 1, s2, E_SUB, lambda j: col("da_sub_gain_2"), sq, root)
    stage(core, pe=ope, act=oact, dve=odve)
    project(core, oT)
    cross_attention(core, w, 1, at_col, 8192)
    norm_stage(core, x, core.XS, at_col("norm_ffn_2", 8), 0)
    mixture(core, w, l0, small)

    stored = sig("output_stored")

    def sp(e):
        e.dma_start(out[0].rearrange("(t p) d -> p t d", p=P), x[:, :, :]).then_inc(*stored.up(16))
        e.wait_ge(stored.sem, 16)
    stage(core, sp=sp)


_INS = ["x", "rel_bias", "ln_attn", "ln_mlp", "moba_w_qkv", "moba_w_o", "dsa_w_in", "dsa_g_q", "dsa_g_kv",
        "dsa_w_uq", "dsa_w_qi", "dsa_w_uk", "dsa_w_uv", "dsa_w_o", "mlp_w_up", "mlp_w_down", "final_norm",
        "mem_2", "norm_mix_2", "norm_xattn_2", "norm_mem_2", "norm_ffn_2", "xa_w_q_2", "xa_w_kv_2",
        "xa_q_gain_2", "xa_k_gain_2", "xa_w_o_2", "hy_w_in_2", "rw_mu_2", "rw_w0_2", "rw_w_up_2", "rw_a0_2",
        "rw_a_up_2", "rw_g_up_2", "rw_k_k_2", "rw_k_a_2", "rw_r_k_2", "rw_ln_w_2", "rw_ln_b_2",
        "s5_lam_re_2", "s5_lam_im_2", "s5_log_dt_2", "s5_b_re_2", "s5_b_im_2", "s5_c_re_2", "s5_c_im_2",
        "s5_d_2", "s5_w_glu_2", "s5_b_glu_2", "hy_w_out_2", "ff_w_gate_2", "ff_w_up_2", "ff_w_down_2",
        "da_w_qkv_2", "da_q_gain_2", "da_k_gain_2", "da_lam_q1_2", "da_lam_k1_2", "da_lam_q2_2",
        "da_lam_k2_2", "da_sub_gain_2", "da_w_o_2", "moe_w_router_2", "moe_b_router_2", "moe_w_gate_2",
        "moe_w_up_2", "moe_w_down_2"]


def kernel(**inputs):
    import concourse.bacc as bacc
    from concourse.bass_utils import run_bass_kernel_spmd

    nc = bacc.Bacc("TRN2", target_bir_lowering=False, num_devices=1)
    consts, const_at = constants()
    arrays = {name: np.ascontiguousarray(inputs[name]) for name in _INS}
    arrays["constants"] = consts
    aps = {name: nc.dram_tensor(name, a.shape, mybir.dt.from_np(a.dtype), kind="ExternalInput").ap()
           for name, a in arrays.items()}
    out = nc.dram_tensor("out", (1, T, D), F32, kind="ExternalOutput").ap()
    c = aps.pop("constants")
    program(nc, aps, c, const_at, out)
    r = run_bass_kernel_spmd(nc, [arrays], core_ids=[0])
    return r.results[0]["out"]
```
